# Optimizing a Trainium2 kernel written in Bass

```python
import jax, jax.numpy as jnp
from jax import lax
import numpy as np

D_MODEL = 1024
BATCH = 1
SEQ = 1024
DEPTH = 1

CTX_LEN = 256
GRID_W = 64

GLA_HEADS = 4
GLA_DK = 128
GLA_DV = 256
GLA_KW = GLA_HEADS * GLA_DK
GLA_VW = GLA_HEADS * GLA_DV
GATE_RANK = 16
GATE_NORM = 16.0
CHUNK = 64
ROPE_BASE = 10000.0

POOL_WINDOWS = (2, 4, 8, 16)
POOL_GROUPS = 4
POOL_W = D_MODEL
POOL_GW = POOL_W // POOL_GROUPS

EPS = 1e-6

IN_SPLITS = (GLA_KW, GLA_KW, GLA_VW, GLA_VW, GATE_RANK, GATE_RANK, POOL_W, POOL_W, D_MODEL, D_MODEL)
D_IN = 2 * GLA_KW + 2 * GLA_VW + 2 * GATE_RANK + 2 * POOL_W + 2 * D_MODEL


def rmsnorm(x, g):
    xf = x.astype(jnp.float32)
    y = xf * lax.rsqrt(jnp.mean(xf * xf, axis=-1, keepdims=True) + EPS)
    return (y * g.astype(jnp.float32)).astype(x.dtype)

def rope_2d(t, row, col):
    half = GLA_DK // 2
    nf = half // 2
    freqs = ROPE_BASE ** (-jnp.arange(nf, dtype=jnp.float32) / nf)

    def rot(xp, pos):
        ang = pos[:, None] * freqs
        cos = jnp.cos(ang)[None, :, None, :]
        sin = jnp.sin(ang)[None, :, None, :]
        xa, xb = xp[..., :nf], xp[..., nf:]
        return jnp.concatenate([xa * cos - xb * sin, xa * sin + xb * cos], axis=-1)

    return jnp.concatenate([rot(t[..., :half], row), rot(t[..., half:], col)], axis=-1)

def gla_chunked(q, k, v, log_a, s0, with_output):
    B, L, H, DK = q.shape
    n = L // CHUNK

    def to_chunks(t):
        return t.astype(jnp.float32).reshape(B, n, CHUNK, H, t.shape[-1]).transpose(1, 0, 3, 2, 4)

    tri = jnp.tril(jnp.ones((CHUNK, CHUNK), dtype=bool))

    def step(S, inp):
        qc, kc, vc, ac = inp
        b = jnp.cumsum(ac, axis=2)
        bC = b[:, :, -1:, :]
        S_new = jnp.exp(bC[:, :, 0, :, None]) * S + jnp.einsum(
            'bhjd,bhjv->bhdv', kc * jnp.exp(bC - b), vc)
        if not with_output:
            return S_new, None
        diff = b[:, :, :, None, :] - b[:, :, None, :, :]
        decay = jnp.exp(jnp.where(tri[:, :, None], diff, -jnp.inf))
        scores = jnp.einsum('bhid,bhjd,bhijd->bhij', qc, kc, decay)
        o = jnp.einsum('bhij,bhjv->bhiv', scores, vc) + jnp.einsum(
            'bhid,bhdv->bhiv', qc * jnp.exp(b), S)
        return S_new, o

    S, o = lax.scan(step, s0, (to_chunks(q), to_chunks(k), to_chunks(v), to_chunks(log_a)))
    if not with_output:
        return None, S
    o = o.transpose(1, 0, 3, 2, 4).reshape(B, L, H, v.shape[-1])
    return o, S

def gla_bidir(q, k, v, la_f, la_b, s0_f, s0_b, with_output):
    flip = lambda t: t[:, ::-1]
    o_f, s_f = gla_chunked(q, k, v, la_f, s0_f, with_output)
    o_b, s_b = gla_chunked(flip(q), flip(k), flip(v), flip(la_b), s0_b, with_output)
    o = o_f + flip(o_b) if with_output else None
    return o, s_f, s_b

def gla_log_decay(lowrank, w_up, b):
    B, L, _ = lowrank.shape
    gk = (lowrank @ w_up + b).astype(jnp.float32)
    return (jax.nn.log_sigmoid(gk) / GATE_NORM).reshape(B, L, GLA_HEADS, GLA_DK)

def mixer_inputs(h, w_in, w_up_f, b_f, w_up_b, b_b, row, col):
    B, L, _ = h.shape
    p = h @ w_in
    idx = np.cumsum(IN_SPLITS)[:-1].tolist()
    pq, pk, pv, zA, lr_f, lr_b, uB, zB, gA, gB = jnp.split(p, idx, axis=-1)
    q = pq.reshape(B, L, GLA_HEADS, GLA_DK) * (GLA_DK ** -0.5)
    k = pk.reshape(B, L, GLA_HEADS, GLA_DK)
    if row is not None:
        q = rope_2d(q, row, col)
        k = rope_2d(k, row, col)
    v = pv.reshape(B, L, GLA_HEADS, GLA_DV)
    la_f = gla_log_decay(lr_f, w_up_f, b_f)
    la_b = gla_log_decay(lr_b, w_up_b, b_b)
    return q, k, v, la_f, la_b, zA, uB, zB, gA, gB

def multiscale_pool(u, w_pool, pool_scale):
    B, L, _ = u.shape
    uf = u.astype(jnp.float32)
    cs = jnp.concatenate([jnp.zeros_like(uf[:, :1]), jnp.cumsum(uf, axis=1)], axis=1)
    t = jnp.arange(L)
    parts = []
    for g, w in enumerate(POOL_WINDOWS):
        lo = jnp.clip(t - w // 2, 0, L - 1)
        hi = jnp.clip(t + (w - 1 - w // 2), 0, L - 1)
        sl = slice(g * POOL_GW, (g + 1) * POOL_GW)
        csg = cs[..., sl]
        cnt = (hi - lo + 1).astype(jnp.float32)[:, None]
        parts.append((csg[:, hi + 1] - csg[:, lo]) / cnt - uf[..., sl])
    d = jnp.stack(parts, axis=2)
    y = jnp.einsum('blgc,gcd->blgd', d, w_pool.astype(jnp.float32)).reshape(B, L, POOL_W)
    return (y * pool_scale.astype(jnp.float32)).astype(u.dtype)

def branch_out(o, zA, uB, zB, gA, gB, gla_norm_g, w_pool, pool_scale, w_branch_a, w_branch_b, w_out):
    B, L, _ = zA.shape
    o_n = rmsnorm(o, gla_norm_g).astype(zA.dtype).reshape(B, L, GLA_VW)
    yA = (o_n * jax.nn.silu(zA)) @ w_branch_a
    yB = (multiscale_pool(uB, w_pool, pool_scale) * jax.nn.silu(zB)) @ w_branch_b
    merged = jax.nn.sigmoid(gA) * yA + jax.nn.sigmoid(gB) * yB
    return merged @ w_out

def first_inputs(seed: int = 0) -> dict:
    key = jax.random.key(seed)
    ks = jax.random.split(key, 24)
    f32 = jnp.float32
    nrm = lambda k, s, sc: jax.random.normal(k, s, f32) * sc
    return {
        "x": nrm(ks[0], (BATCH, SEQ, D_MODEL), 1.0),
        "c": nrm(ks[1], (BATCH, D_MODEL), 1.0),
        "ctx": nrm(ks[2], (BATCH, CTX_LEN, D_MODEL), 1.0),
        "c_ctx": nrm(ks[3], (D_MODEL,), 1.0),
        "w_mod": nrm(ks[4], (DEPTH, D_MODEL, 3 * D_MODEL), D_MODEL ** -0.5),
        "b_mod": nrm(ks[5], (DEPTH, 3 * D_MODEL), 0.01),
        "norm_g": 1.0 + nrm(ks[6], (DEPTH, D_MODEL), 0.1),
        "w_in": nrm(ks[7], (DEPTH, D_MODEL, D_IN), D_MODEL ** -0.5),
        "w_gate_up_f": nrm(ks[8], (DEPTH, GATE_RANK, GLA_KW), GATE_RANK ** -0.5),
        "b_gate_f": jax.random.uniform(ks[9], (DEPTH, GLA_KW), f32, 1.0, 5.0),
        "w_gate_up_b": nrm(ks[10], (DEPTH, GATE_RANK, GLA_KW), GATE_RANK ** -0.5),
        "b_gate_b": jax.random.uniform(ks[11], (DEPTH, GLA_KW), f32, 1.0, 5.0),
        "gla_norm_g": 1.0 + nrm(ks[12], (DEPTH, GLA_DV), 0.1),
        "w_pool": nrm(ks[13], (DEPTH, POOL_GROUPS, POOL_GW, POOL_GW), POOL_GW ** -0.5),
        "pool_scale": 1.0 + nrm(ks[14], (DEPTH, POOL_W), 0.1),
        "w_branch_a": nrm(ks[15], (DEPTH, GLA_VW, D_MODEL), GLA_VW ** -0.5),
        "w_branch_b": nrm(ks[16], (DEPTH, POOL_W, D_MODEL), POOL_W ** -0.5),
        "w_out": nrm(ks[17], (DEPTH, D_MODEL, D_MODEL), D_MODEL ** -0.5),
        "final_norm_g": 1.0 + nrm(ks[18], (D_MODEL,), 0.1),
    }

def first_block(x, c, ctx, c_ctx, w_mod, b_mod, norm_g, w_in, w_gate_up_f, b_gate_f,
              w_gate_up_b, b_gate_b, gla_norm_g, w_pool, pool_scale, w_branch_a,
              w_branch_b, w_out, final_norm_g):
    B, L, _ = x.shape
    ROWS = L // GRID_W
    t = jnp.arange(ROWS * GRID_W)
    row = (t // GRID_W).astype(jnp.float32)
    col = (t % GRID_W).astype(jnp.float32)

    for l in range(DEPTH):
        last = l == DEPTH - 1
        shift_x, scale_x, gate_x = jnp.split(jax.nn.silu(c) @ w_mod[l] + b_mod[l], 3, axis=-1)
        shift_x, scale_x, gate_x = shift_x[:, None], scale_x[:, None], gate_x[:, None]
        shift_c, scale_c, gate_c = jnp.split(jax.nn.silu(c_ctx) @ w_mod[l] + b_mod[l], 3, axis=-1)

        hc = rmsnorm(ctx, norm_g[l]) * (1.0 + scale_c) + shift_c
        qc, kc, vc, laf_c, lab_c, zAc, uBc, zBc, gAc, gBc = mixer_inputs(
            hc, w_in[l], w_gate_up_f[l], b_gate_f[l], w_gate_up_b[l], b_gate_b[l], None, None)
        s_zero = jnp.zeros((B, GLA_HEADS, GLA_DK, GLA_DV), jnp.float32)
        oc, s_f, s_b = gla_bidir(qc, kc, vc, laf_c, lab_c, s_zero, s_zero, not last)

        hx = rmsnorm(x, norm_g[l]) * (1.0 + scale_x) + shift_x
        q, k, v, la_f, la_b, zA, uB, zB, gA, gB = mixer_inputs(
            hx, w_in[l], w_gate_up_f[l], b_gate_f[l], w_gate_up_b[l], b_gate_b[l], row, col)
        ox, _, _ = gla_bidir(q, k, v, la_f, la_b, s_f, s_b, True)
        y = branch_out(ox.astype(x.dtype), zA, uB, zB, gA, gB, gla_norm_g[l], w_pool[l],
                       pool_scale[l], w_branch_a[l], w_branch_b[l], w_out[l])
        x_new = x + gate_x * y

        if not last:
            yc = branch_out(oc.astype(ctx.dtype), zAc, uBc, zBc, gAc, gBc, gla_norm_g[l], w_pool[l],
                            pool_scale[l], w_branch_a[l], w_branch_b[l], w_out[l])
            ctx = ctx + gate_c * yc
        x = x_new

    return rmsnorm(x, final_norm_g)


HEAD_DIM = 64
N_HEADS = D_MODEL // HEAD_DIM
N_FOX_HEADS = N_HEADS // 2
N_SB_HEADS = N_HEADS - N_FOX_HEADS
FOX_WIDTH = N_FOX_HEADS * HEAD_DIM
SB_WIDTH = N_SB_HEADS * HEAD_DIM
MIX_WIDTH = FOX_WIDTH + SB_WIDTH
IN_COLS = 3 * FOX_WIDTH + N_FOX_HEADS + 3 * SB_WIDTH
D_FF = ((8 * D_MODEL // 3 + 127) // 128) * 128
CONV_WIDTH = 3
BLOCK_Q = 128


def rmsnorm_2(x, g):
    xf = x.astype(jnp.float32)
    y = xf * lax.rsqrt(jnp.mean(xf * xf, axis=-1, keepdims=True) + EPS)
    return (y * g.astype(jnp.float32)).astype(x.dtype)

def split_heads(t, n_heads):
    b, s, _ = t.shape
    return t.reshape(b, s, n_heads, HEAD_DIM).transpose(0, 2, 1, 3)

def merge_heads(t):
    b, h, s, d = t.shape
    return t.transpose(0, 2, 1, 3).reshape(b, s, h * d)

def to_blocks(t):
    b, h, s = t.shape[:3]
    t = t.reshape(b, h, s // BLOCK_Q, BLOCK_Q, *t.shape[3:])
    return jnp.moveaxis(t, 2, 0)

def from_blocks(t):
    nb, b, h, bq, d = t.shape
    return jnp.moveaxis(t, 0, 2).reshape(b, h, nb * bq, d)

def fox_attention(q, k, v, log_f):
    s_len = q.shape[2]
    scale = HEAD_DIM ** -0.5
    kf = k.astype(jnp.float32)
    vf = v.astype(jnp.float32)
    F = jnp.cumsum(log_f, axis=-1)
    kpos = jnp.arange(s_len)

    def block(args):
        i, qi, Fi = args
        qpos = i * BLOCK_Q + jnp.arange(BLOCK_Q)
        logits = (jnp.einsum('bhqd,bhkd->bhqk', qi.astype(jnp.float32), kf) * scale
                  + Fi[..., :, None] - F[:, :, None, :])
        logits = jnp.where(kpos[None, :] <= qpos[:, None], logits, -jnp.inf)
        p = jax.nn.softmax(logits, axis=-1)
        return jnp.einsum('bhqk,bhkd->bhqd', p, vf)

    out = lax.map(block, (jnp.arange(s_len // BLOCK_Q), to_blocks(q), to_blocks(F)))
    return from_blocks(out).astype(v.dtype)

def stick_breaking_attention(q, k, v):
    s_len = q.shape[2]
    scale = HEAD_DIM ** -0.5
    kf = k.astype(jnp.float32)
    vf = v.astype(jnp.float32)
    kpos = jnp.arange(s_len)

    def block(args):
        i, qi = args
        qpos = i * BLOCK_Q + jnp.arange(BLOCK_Q)
        mask = kpos[None, :] < qpos[:, None]
        z = jnp.einsum('bhqd,bhkd->bhqk', qi.astype(jnp.float32), kf) * scale
        log_beta = jax.nn.log_sigmoid(z)
        log_one_minus = jnp.where(mask, jax.nn.log_sigmoid(-z), 0.0)
        after = lax.cumsum(log_one_minus, axis=3, reverse=True) - log_one_minus
        weights = jnp.where(mask, jnp.exp(log_beta + after), 0.0)
        return jnp.einsum('bhqk,bhkd->bhqd', weights, vf)

    out = lax.map(block, (jnp.arange(s_len // BLOCK_Q), to_blocks(q)))
    return from_blocks(out).astype(v.dtype)

def causal_dwconv(u, w, b):
    s_len = u.shape[1]
    up = jnp.pad(u, ((0, 0), (CONV_WIDTH - 1, 0), (0, 0)))
    out = b + w[0] * up[:, 0:s_len]
    for kk in range(1, CONV_WIDTH):
        out = out + w[kk] * up[:, kk:kk + s_len]
    return out

def second_inputs(seed: int = 0) -> dict:
    key = jax.random.key(seed)
    ks = jax.random.split(key, 13)
    f32 = jnp.float32
    x = jax.random.normal(ks[0], (BATCH, SEQ, D_MODEL), f32)
    attn_norm_g = 1.0 + 0.05 * jax.random.normal(ks[1], (DEPTH, D_MODEL), f32)
    w_in = jax.random.normal(ks[2], (DEPTH, D_MODEL, IN_COLS), f32) * D_MODEL ** -0.5
    forget_bias = (jnp.linspace(1.0, 6.0, N_FOX_HEADS, dtype=f32)[None, :]
                   + 0.1 * jax.random.normal(ks[3], (DEPTH, N_FOX_HEADS), f32))
    fox_out_g = 1.0 + 0.05 * jax.random.normal(ks[4], (DEPTH, FOX_WIDTH), f32)
    sb_out_g = 1.0 + 0.05 * jax.random.normal(ks[5], (DEPTH, SB_WIDTH), f32)
    w_out = jax.random.normal(ks[6], (DEPTH, MIX_WIDTH, D_MODEL), f32) * MIX_WIDTH ** -0.5
    ffn_norm_g = 1.0 + 0.05 * jax.random.normal(ks[7], (DEPTH, D_MODEL), f32)
    w_up = jax.random.normal(ks[8], (DEPTH, D_MODEL, 2 * D_FF), f32) * D_MODEL ** -0.5
    conv_w = jax.random.normal(ks[9], (DEPTH, CONV_WIDTH, 2 * D_FF), f32) * CONV_WIDTH ** -0.5
    conv_b = 0.02 * jax.random.normal(ks[10], (DEPTH, 2 * D_FF), f32)
    w_down = jax.random.normal(ks[11], (DEPTH, D_FF, D_MODEL), f32) * D_FF ** -0.5
    final_norm_g = 1.0 + 0.05 * jax.random.normal(ks[12], (D_MODEL,), f32)
    return {"x": x, "attn_norm_g": attn_norm_g, "w_in": w_in, "forget_bias": forget_bias,
            "fox_out_g": fox_out_g, "sb_out_g": sb_out_g, "w_out": w_out,
            "ffn_norm_g": ffn_norm_g, "w_up": w_up, "conv_w": conv_w, "conv_b": conv_b,
            "w_down": w_down, "final_norm_g": final_norm_g}

def second_block(x, attn_norm_g, w_in, forget_bias, fox_out_g, sb_out_g, w_out,
              ffn_norm_g, w_up, conv_w, conv_b, w_down, final_norm_g):
    b, s_len, _ = x.shape
    splits = [FOX_WIDTH, 2 * FOX_WIDTH, 3 * FOX_WIDTH, 3 * FOX_WIDTH + N_FOX_HEADS,
              3 * FOX_WIDTH + N_FOX_HEADS + SB_WIDTH,
              3 * FOX_WIDTH + N_FOX_HEADS + 2 * SB_WIDTH]
    for l in range(DEPTH):
        h = rmsnorm_2(x, attn_norm_g[l])
        proj = h @ w_in[l]
        fq, fk, fv, f_logit, sq, sk, sv = jnp.split(proj, splits, axis=-1)
        log_f = jax.nn.log_sigmoid(
            (f_logit + forget_bias[l]).astype(jnp.float32)).transpose(0, 2, 1)
        o_fox = fox_attention(split_heads(fq, N_FOX_HEADS), split_heads(fk, N_FOX_HEADS),
                              split_heads(fv, N_FOX_HEADS), log_f)
        o_sb = stick_breaking_attention(split_heads(sq, N_SB_HEADS), split_heads(sk, N_SB_HEADS),
                                        split_heads(sv, N_SB_HEADS))
        o = jnp.concatenate([rmsnorm_2(merge_heads(o_fox), fox_out_g[l]),
                             rmsnorm_2(merge_heads(o_sb), sb_out_g[l])], axis=-1)
        x = x + o @ w_out[l]
        h = rmsnorm_2(x, ffn_norm_g[l])
        u = causal_dwconv(h @ w_up[l], conv_w[l], conv_b[l])
        gate, val = jnp.split(u, 2, axis=-1)
        x = x + (jax.nn.silu(gate) * val) @ w_down[l]
    return rmsnorm_2(x, final_norm_g)


def setup_inputs(seed=0):
    out = dict(first_inputs(seed))
    for name, value in second_inputs(seed + 1).items():
        if name != "x":
            out[name + "_2"] = value
    return out


def reference(
    x, c, ctx, c_ctx, w_mod, b_mod, norm_g, w_in, w_gate_up_f, b_gate_f, w_gate_up_b, b_gate_b,
    gla_norm_g, w_pool, pool_scale, w_branch_a, w_branch_b, w_out, final_norm_g, attn_norm_g_2,
    w_in_2, forget_bias_2, fox_out_g_2, sb_out_g_2, w_out_2, ffn_norm_g_2, w_up_2, conv_w_2,
    conv_b_2, w_down_2, final_norm_g_2,
):
    x = first_block(
        x, c, ctx, c_ctx, w_mod, b_mod, norm_g, w_in, w_gate_up_f, b_gate_f, w_gate_up_b,
        b_gate_b, gla_norm_g, w_pool, pool_scale, w_branch_a, w_branch_b, w_out, final_norm_g,
    )
    return second_block(
        x, attn_norm_g_2, w_in_2, forget_bias_2, fox_out_g_2, sb_out_g_2, w_out_2, ffn_norm_g_2,
        w_up_2, conv_w_2, conv_b_2, w_down_2, final_norm_g_2,
    )


_drawn_inputs = setup_inputs


def setup_inputs(seed=0):
    import zlib

    import numpy as np

    out = dict(_drawn_inputs(seed))
    spreads = {}
    factors = {'b_mod': 3.776, 'conv_b_2': 5.013}
    for name, (base, spread) in spreads.items():
        noise = np.random.default_rng([zlib.crc32(name.encode()), seed]).standard_normal(out[name].shape)
        drawn = base * np.exp(spread * noise) if base else spread * noise
        out[name] = __import__('jax').numpy.asarray(drawn.astype(out[name].dtype))
    for name, factor in factors.items():
        out[name] = (out[name] * factor).astype(out[name].dtype)
    return out
```

```python
import numpy as np
import concourse.bass as bass
from concourse import mybir

F32 = mybir.dt.float32
F32R = mybir.dt.float32r
BF16 = mybir.dt.bfloat16
U8 = mybir.dt.uint8
ALU = mybir.AluOpType
ACT = mybir.ActivationFunctionType
AX = mybir.AxisListType

P = 128
D = 1024
KT = D // P
T = 1024
TT = T // P
TC = 256
NB = 512
EPS = 1e-6
HEADS, DK, DV = 4, 128, 256
RANK = 16
GATE_NORM = 16.0
GRID_W = 64
CH = 128
POOL_WINDOWS = (2, 4, 8, 16)
LEVELS = (64, 32, 16, 8, 4, 2, 1)
C_Q, C_K, C_V, C_ZA = 0, 512, 1024, 2048
C_LR, C_UB, C_ZB, C_GA, C_GB = 3072, 3104, 4128, 5152, 6176
HD = 64
S_HEADS = 8
S_FQ, S_FK, S_FV, S_FL, S_SQ, S_SK, S_SV = 0, 512, 1024, 1536, 1544, 2056, 2568
DFF = 2816
FT = DFF // P

R0 = dict(c=0, cc=8, ng=16, bm=24, bgf=48, bgb=52, gg=56, ps=58, ag=66, fg=74, sg=78, fn=82, fin=90, f1=98)
R0_ROWS = 106
R1_ROWS = 88
R2_ROWS = 88

J_CTX = 0
J_LR = 13
J_GLA = 14
GLA_JOBS = 10
J_POOL = J_GLA + HEADS * GLA_JOBS
POOL_JOBS = 6
J_BRA = J_POOL + 4 * POOL_JOBS
J_BRB = J_BRA + KT
J_OUT = J_BRB + KT
J_FL = J_OUT + KT
J_ATT = J_FL + 1
ATT_JOBS = 6
J_OUT2 = J_ATT + 4 * ATT_JOBS
J_FFN = J_OUT2 + KT
FFN_GROUPS = ((0, 8), (8, 8), (16, 6))



class Steps:

    def __init__(self, known):
        self.known, self.at, self.n, self.loop, self.sems = known, {}, {}, {}, {}

    def start(self, nc, names):
        self.sems = {n: nc.alloc_semaphore(f"{n}_steps") for n in names}
        self.n = dict.fromkeys(names, 0) | {(n, "settled"): 0 for n in names}
        self.settled = {n: nc.alloc_semaphore(f"{n}_waits_taken") for n in ("act", "dve")}

    def mark(self, engine, name, ins):
        ins.then_inc(self.sems[engine], 1)
        self.n[engine] += 1
        key = (engine, name)
        assert key not in self.at, key
        self.at[key] = (self.n[engine], self.loop.get(engine))
        return ins

    def value(self, engine, name, turn=None):
        table = self.at if (engine, name) in self.at else self.known
        if (engine, name) not in table:
            assert not self.known, (engine, name)
            return 1
        n, loop = table[engine, name]
        if loop is None:
            return n
        before, per = self.known.get(loop, (0, 1))
        return before + (n - before) + turn * per

    def wait(self, eng, engine, name, turn=None):
        eng.wait_ge(self.sems[engine], self.value(engine, name, turn))

    def wait_last(self, eng, engine, names, turn=None):
        self.wait(eng, engine, max(names, key=lambda name: self.value(engine, name, 0)), turn)

    def settle(self, engine, eng):
        eng.sem_inc(self.settled[engine], 1)
        self.n[engine, "settled"] += 1

    def enter(self, engine, name):
        self.loop[engine] = ("loop", engine, name)
        self.before = self.n[engine]
        self.before_settled = self.n[engine, "settled"]

    def leave(self, engine, turns):
        per = self.n[engine] - self.before
        self.at[self.loop[engine]] = (self.before, per)
        self.n[engine] += (turns - 1) * per
        self.n[engine, "settled"] += (turns - 1) * (self.n[engine, "settled"] - self.before_settled)
        self.loop[engine] = None


def program(nc, a, out, known):
    base = (nc.sbuf_base + 31) // 32 * 32
    KB = 1024
    END = 229344 - base

    def sb(name, off, shape, dt=F32):
        return nc.alloc_sbuf_tensor_at(name, shape, dt, offset=base + off)[tuple(slice(None) for _ in shape)]

    H = [sb("H_hi", 0, [P, KT, T], F32R), sb("H_lo", 32 * KB, [P, KT, T], F32R)]
    w_raw = sb("w_raw", 64 * KB, [P, 2, KT, P])
    w_hi = sb("w_hi", 72 * KB, [P, 2, KT, P], F32R)
    w_lo = sb("w_lo", 80 * KB, [P, 2, KT, P], F32R)
    C0 = 88 * KB
    par = sb("par", C0, [P, R0_ROWS + R1_ROWS + R2_ROWS])
    ident = sb("ident", C0 + 1152, [P, P])
    ones = sb("ones", C0 + 1664, [P, P])
    lvl = sb("lvl", C0 + 2176, [P, len(LEVELS), P], U8)
    mod = sb("mod", C0 + 3072, [P, 24, 2])
    gsc = sb("gsc", C0 + 3264, [P, KT, 2])
    identb = sb("identb", C0 + 3328, [P, P], BF16)
    maskb = sb("maskb", C0 + 3584, [P, 2, P], BF16)
    fbias = sb("fbias", C0 + 4096, [P, 1])
    epsc = sb("epsc", C0 + 4128, [P, 1])
    W0 = C0 + 4160

    def col(name, i=0):
        return par[:, R0[name] + i:R0[name] + i + 1]

    def conv_col(which, i):
        o = R0_ROWS + which * (2 * FT) + i
        return par[:, bass.ds(o, 1)]

    G = [nc.alloc_psum_tensor(f"G{s}", [P, 2 * NB], F32)[:, :] for s in range(2)]
    S2 = nc.alloc_psum_tensor("S2", [P, 2 * NB], F32)[:, :]
    U = [nc.alloc_psum_tensor(f"U{s}", [P, NB], F32)[:, :] for s in range(2)]

    def scratch(name, shape):
        return nc.dram_tensor(name, shape, F32, kind="Internal").ap()

    xT_d, s0_d = scratch("xT_d", (KT, P, T)), scratch("s0_d", (HEADS, 2, P, DV))
    a_d, b_d = scratch("a_d", (KT, P, T)), scratch("b_d", (KT, P, T))
    sga_d, sgb_d = scratch("sga_d", (KT, P, T)), scratch("sgb_d", (KT, P, T))
    o_d = scratch("o_d", (T, D))

    sem = nc.alloc_semaphore
    w_landed = [sem("w_landed0"), sem("w_landed1")]
    w_hi_made, w_ready, gemm_done = sem("w_hi_made"), sem("w_ready"), sem("gemm_done")
    S = Steps(known)
    S.start(nc, ("pe", "act", "dve", "pool"))
    engines = {"pe": nc.tensor, "act": nc.scalar, "dve": nc.vector, "pool": nc.gpsimd}

    def gemm(j, slot, mov, freed=None, n_cols=T, kt=KT, pair=None):
        pe, (hi, lo) = nc.tensor, mov
        dst = G[slot if pair is None else pair]
        pe.wait_ge(w_ready, j + 1)
        if freed:
            S.wait(pe, *freed)
        halves = [(n, min(NB, n_cols - n * NB)) for n in range((n_cols + NB - 1) // NB)]
        for k in range(kt):
            for w, m, first, last in ((w_hi, hi, k == 0, False), (w_hi, lo, False, False),
                                      (w_lo, hi, False, k == kt - 1)):
                for n, c in halves:
                    mm = pe.matmul(dst[:, n * NB:n * NB + c], w[:, slot, k, :], m[:, k, n * NB:n * NB + c],
                                   start=first, stop=last)
        mm.then_inc(gemm_done, 1)

    def load_w(j, slot, src, kt=KT, first=False):
        if not first:
            nc.sync.wait_ge(w_ready, j - 1)
        nc.sync.dma_start(w_raw[:, slot, 0:kt, :], src).then_inc(w_landed[slot], 16)

    def split_hi(eng, j, slot, landed, kt=KT, first=False):
        eng.wait_ge(w_landed[slot], 16 * landed)
        if not first:
            eng.wait_ge(gemm_done, j - 1)
        dst, src = w_hi[:, slot, 0:kt, :], w_raw[:, slot, 0:kt, :]
        i = eng.activation(dst, src, ACT.Copy) if eng is nc.scalar else \
            eng.tensor_tensor(dst, src, ones.unsqueeze(1).to_broadcast([P, kt, P]), ALU.mult)
        i.then_inc(w_hi_made, 1)

    def split_lo(j, slot, kt=KT):
        nc.gpsimd.wait_ge(w_hi_made, j + 1)
        nc.gpsimd.tensor_tensor(w_lo[:, slot, 0:kt, :], w_raw[:, slot, 0:kt, :],
                                w_hi[:, slot, 0:kt, :].bitcast(F32), ALU.subtract).then_inc(w_ready, 1)

    def split(j, slot, landed, kt=KT):
        split_hi(nc.gpsimd, j, slot, landed, kt)
        split_lo(j, slot, kt)

    def slab(w, c0, kt=KT, r0=0):
        return w[r0:r0 + kt * P, c0:c0 + P].rearrange("(k p) c -> p k c", p=P)

    def settle(eng, turn=None):
        S.settle({nc.scalar: "act", nc.vector: "dve"}[eng], eng)

    def barrier(engine, n):
        eng = engines[engine]
        S.mark(engine, f"phase {n} ended", eng.drain())
        for other in ("pe", "act", "dve"):
            S.wait(eng, other, f"phase {n} ended")

    def after_phase(eng, n):
        for other in ("pe", "act", "dve"):
            S.wait(eng, other, f"phase {n} ended")

    w_in, w_mod = a["w_in"][0], a["w_mod"][0]

    o = W0
    def take(name, shape, dt=F32, size=None):
        nonlocal o
        at = o
        n = int(np.prod(shape[1:])) * {F32: 4, F32R: 4, BF16: 2, U8: 1}[dt]
        o = (o + n + 31) // 32 * 32
        assert o <= END, (name, o, END)
        return sb(name, at, shape, dt)

    xT = take("xT", [P, KT, T])
    wm = take("wm", [P, 2, KT, NB])
    cT = take("cT", [P, KT, TC])
    hc = [take("hc_hi", [P, KT, TC], F32R), take("hc_lo", [P, KT, TC], F32R)]
    x_in = take("x_in", [P, 2, D])
    sq = take("sq", [P, 2, T])
    rb = take("rb", [P, T + TC])
    prow = take("prow", [P, 3, P])
    silc = take("silc", [P, 16])
    lvl_in = take("levels_in", [P, len(LEVELS), P])
    mask_in = take("masks_in", [P, 2, P])
    o = W0
    lrc = take("lrc", [2 * RANK, TC])
    wup = take("wup", [2 * RANK, 2, HEADS * DK])
    smask = take("smask", [P, T], BF16)
    kc = take("kc", [P, T])
    vcT = take("vcT", [P, 2, 2, TC])
    vc = take("vc", [P, 2, HEADS * DV])
    c_g = [take("c_gf", [P, T + 8]), take("c_gb", [P, T + 8])]
    c_l = [take("c_lf", [P, T]), take("c_lb", [P, T])]
    c_F = [take("c_F", [P, T]), take("c_X", [P, T])]
    c_k = [take("c_kf", [P, T]), take("c_kb", [P, T])]
    c_kn = [take("c_kfT", [P, 8, P]), take("c_kbT", [P, 8, P])]
    c_t = take("c_t", [P, 2, 8])
    assert o <= W0 + 72 * KB, o
    o = W0 + 88 * KB
    c_S = take("c_S", [P, HEADS, 2, DV])

    par_landed, const_landed = sem("params_landed"), sem("constants_landed")
    x_landed, wm_landed = [sem("x_landed0"), sem("x_landed1")], [sem("wm_landed0"), sem("wm_landed1")]
    xT_stored, s0_stored, cpar_landed = sem("xT_stored"), sem("s0_stored"), sem("ctx_params_landed")

    def ctx_col(j):
        return C_LR if j == 0 else C_K + (j - 1) * P if j < 5 else C_V + (j - 5) * P

    def rows(v):
        return v.rearrange("(r c) -> r c", c=P)

    def broadcast(ap, n):
        return ap.to_broadcast([ap.shape[0], ap.shape[1], n])

    def chunks(v, n=8):
        return v.rearrange("p (c t) -> p c t", c=n)

    def chunk_mask(dst, name):
        g = nc.gpsimd
        S.mark("pool", f"{name} ones", g.memset(dst, 1.0))
        S.wait(g, "pool", f"{name} ones")
        S.mark("pool", name, g.memset(chunks(dst)[:, :, 0:1], 0.0))

    block = nc.Block()
    with block:
        @block.sync
        def _(sp):
            vectors = (("c", a["c"][0]), ("cc", a["c_ctx"]), ("ng", a["norm_g"][0]), ("bm", a["b_mod"][0]),
                       ("bgf", a["b_gate_f"][0]), ("bgb", a["b_gate_b"][0]), ("gg", a["gla_norm_g"][0]),
                       ("ps", a["pool_scale"][0]), ("ag", a["attn_norm_g_2"][0]), ("fg", a["fox_out_g_2"][0]),
                       ("sg", a["sb_out_g_2"][0]), ("fn", a["ffn_norm_g_2"][0]), ("fin", a["final_norm_g_2"]), ("f1", a["final_norm_g"]))
            for name, src in vectors:
                sp.dma_start(prow[R0[name]:R0[name] + src.shape[0] // P, 0, :], rows(src)).then_inc(par_landed, 16)
            cw = a["conv_w_2"][0]
            for row, g, src in ((0, 1, a["conv_b_2"][0]), (44, 1, cw[0]), (0, 2, cw[1]), (44, 2, cw[2])):
                sp.dma_start(prow[row:row + 44, g, :], rows(src)).then_inc(par_landed, 16)
            sp.dma_start(ident, a["identity"]).then_inc(par_landed, 16)
            tiles = [a["ctx"][0, t * P:(t + 1) * P, :] for t in range(2)] + \
                    [a["x"][0, t * P:(t + 1) * P, :] for t in range(TT)]

            def load_tile(t):
                if t >= 2:
                    S.wait(sp, "pe", ("turned", t - 2, 1))
                sp.dma_start(x_in[:, t % 2, :], tiles[t]).then_inc(x_landed[t % 2], 16)

            def load_mod(q):
                if q >= 2:
                    S.wait(sp, "pe", ("modulation", q - 2))
                sp.dma_start(wm[:, q % 2, :, :], w_mod[:, q * NB:(q + 1) * NB].rearrange("(k p) c -> p k c", p=P))\
                    .then_inc(wm_landed[q % 2], 16)
            load_tile(0)
            load_tile(1)
            load_mod(0)
            for t in range(2, 6):
                load_tile(t)
            load_mod(1)
            for t in range(6, 10):
                load_tile(t)
            load_mod(2)
            load_mod(3)
            for j in range(2):
                load_w(J_CTX + j, j, slab(w_in, ctx_col(j)), first=True)
            load_mod(4)
            load_mod(5)
            sp.dma_start(lvl_in, a["levels"]).then_inc(const_landed, 16)
            sp.dma_start(mask_in, a["causal"]).then_inc(const_landed, 16)
            sp.dma_start(fbias[0:S_HEADS, :], a["forget_bias_2"].rearrange("a h -> h a")).then_inc(const_landed, 16)
            after_phase(sp, 1)
            sp.wait_ge(const_landed, 48)
            S.wait(sp, "pool", "gate weights cleared")
            sp.dma_start(wup[0:RANK, 0, :], a["w_gate_up_f"][0]).then_inc(cpar_landed, 16)
            sp.dma_start(wup[RANK:2 * RANK, 1, :], a["w_gate_up_b"][0]).then_inc(cpar_landed, 16)
            for j in range(2, J_LR):
                load_w(j, j % 2, slab(w_in, ctx_col(j)))

        @block.gpsimd
        def _(g):
            S.mark("pool", "ones made", g.memset(ones, 1.0))
            S.mark("pool", "eps made", g.memset(epsc, EPS))
            split_lo(0, 0)
            split_lo(1, 1)
            after_phase(g, 1)
            S.mark("pool", "gate weights cleared", g.memset(wup, 0.0))
            chunk_mask(smask, "chunk mask")
            for j in range(2, J_LR):
                split_lo(j, j % 2)

        @block.tensor
        def _(pe):
            pe.wait_ge(par_landed, 16 * 19)
            for g, (n, at) in enumerate(((R0_ROWS, 0), (R1_ROWS, R0_ROWS), (R2_ROWS, R0_ROWS + R1_ROWS))):
                mm = pe.transpose(G[1][:, at:at + n], prow[0:n, g, :], ident[0:n, 0:n])
            S.mark("pe", "parameters turned", mm)

            def turn(t):
                pe.wait_ge(x_landed[t % 2], 16 * (t // 2 + 1))
                for h in range(2):
                    if t >= 1:
                        S.wait(pe, "act" if h == 0 else "dve", ("turned copied", t - 1))
                    for i in range(4):
                        mm = pe.transpose(U[h][:, i * P:(i + 1) * P], x_in[:, t % 2, (4 * h + i) * P:(4 * h + i + 1) * P], ident)
                    S.mark("pe", ("turned", t, h), mm)

            def modulation(q):
                pe.wait_ge(wm_landed[q % 2], 16 * (q // 2 + 1))
                if q == 0:
                    S.wait(pe, "act", "silu made")
                for m in range(4):
                    c = NB + (4 * q + m) * 2
                    for k in range(KT):
                        mm = pe.matmul(G[1][:, c:c + 2], wm[:, q % 2, k, m * P:(m + 1) * P], silc[:, k:16:8],
                                       start=k == 0, stop=k == KT - 1)
                S.mark("pe", ("modulation", q), mm)
            turn(0)
            turn(1)
            modulation(0)
            for t in range(2, 6):
                turn(t)
            modulation(1)
            for t in range(6, 10):
                turn(t)
            S.wait(pe, "pool", "ones made")
            S.wait(pe, "act", ("turned copied", 9))
            for k in range(KT):
                S.wait(pe, "act", ("ctx squares", k // 4))
                mm = pe.matmul(U[0][:, 0:TC], ones, sq[:, k // 4, (k % 4) * TC:(k % 4 + 1) * TC], start=k == 0, stop=k == KT - 1)
                if k % 4 == 3:
                    S.mark("pe", ("ctx squares summed", k // 4), mm)
            for k in range(KT):
                S.wait(pe, "act", ("squares", k))
                for n in range(2):
                    mm = pe.matmul(S2[:, n * NB:(n + 1) * NB], ones, sq[:, k % 2, n * NB:(n + 1) * NB], start=k == 0, stop=k == KT - 1)
                S.mark("pe", ("squares summed", k), mm)
            modulation(2)
            modulation(3)
            for j in range(2):
                if j == 0:
                    S.wait(pe, "dve", ("scaled", "c", KT - 1))
                    gemm(0, 0, hc, n_cols=TC)
            modulation(4)
            modulation(5)
            barrier("pe", 1)
            gemm(1, 1, hc, n_cols=TC)
            S.wait(pe, "act", ("ctx job", 0))
            pe.wait_ge(cpar_landed, 32)
            for d in range(2):
                for hh in range(2):
                    if d:
                        S.wait(pe, "act", ("ctx gates", 0, hh))
                    for h in range(2):
                        w = wup[:, d, (2 * hh + h) * DK:(2 * hh + h + 1) * DK]
                        mm = pe.matmul(U[hh][:, h * TC:(h + 1) * TC], w, lrc, start=True, stop=True)
                    S.mark("pe", ("ctx gates", d, hh), mm)

            def turn_values(i):
                S.wait(pe, "act", ("ctx job", 6 + 2 * i))
                S.wait(pe, *(("act", ("ctx gates", 1, i)) if i < 2 else ("dve", ("vc", i - 2))))
                for c in range(2):
                    for m in range(2):
                        mm = pe.transpose(U[i % 2][:, (2 * c + m) * P:(2 * c + m + 1) * P], vcT[:, i % 2, m, c * P:(c + 1) * P], ident)
                S.mark("pe", ("vc turned", i), mm)
            for j in range(2, J_LR):
                gemm(j, j % 2, hc, ("act", ("ctx job", j - 2)), n_cols=TC)
                if j in (8, 10, 12):
                    turn_values((j - 8) // 2)
            turn_values(3)
            for d in range(2):
                S.wait(pe, "dve", ("ctx keys", d))
                for h in range(2):
                    S.wait(pe, *(("dve", ("vc", 2 + h)) if d == 0 else ("act", ("ctx keys turned", 0, h))))
                    for i in range(4):
                        mm = pe.transpose(U[h][:, i * P:(i + 1) * P], c_k[d][:, (4 * h + i) * P:(4 * h + i + 1) * P], ident)
                    S.mark("pe", ("ctx keys turned", d, h), mm)
            for d in range(2):
                for h in range(HEADS):
                    S.wait(pe, "act", ("ctx keys turned", d, h // 2))
                    if d == 0 and h < 2:
                        S.wait(pe, "act", ("ctx keys turned", 1, h))
                    else:
                        S.wait(pe, "dve", ("ctx state", d - (h < 2), (h - 2) % 4))
                    for c in range(2):
                        mm = pe.matmul(U[h % 2][:, c * DV:(c + 1) * DV], c_kn[d][:, 2 * h + c, :], vc[:, c, h * DV:(h + 1) * DV], start=True, stop=True)
                    S.mark("pe", ("ctx updates", d, h), mm)
            barrier("pe", 2)

        @block.scalar
        def _(act):
            S.wait(act, "pe", "parameters turned")
            S.mark("act", "parameters", act.activation(par, G[1][:, 0:R0_ROWS + R1_ROWS + R2_ROWS], ACT.Copy))
            S.wait(act, "act", "parameters")
            S.mark("act", "silu made", act.activation(silc, par[:, 0:16], ACT.Silu))
            for t in range(10):
                S.wait(act, "pe", ("turned", t, 0))
                dst = cT[:, 0:4, t * P:(t + 1) * P] if t < 2 else xT[:, 0:4, (t - 2) * P:(t - 1) * P]
                S.mark("act", ("turned copied", t), act.activation(dst, U[0].rearrange("p (i t) -> p i t", i=4), ACT.Copy))
            S.wait(act, "act", ("turned copied", 9))
            S.wait(act, "dve", ("turned copied", 9))
            for i in range(2):
                S.mark("act", ("ctx squares", i), act.activation(sq[:, i, :].rearrange("p (k t) -> p k t", k=4), cT[:, 4 * i:4 * i + 4, :], ACT.Square))
            for k in range(KT):
                S.wait(act, "pe", ("ctx squares summed", k) if k < 2 else ("squares summed", k - 2))
                S.mark("act", ("squares", k), act.activation(sq[:, k % 2, :], xT[:, k, :], ACT.Square))
            S.wait(act, "pe", ("ctx squares summed", 1))
            S.wait(act, "pool", "eps made")
            S.mark("act", "ctx root", act.activation(rb[:, T:T + TC], U[0][:, 0:TC], ACT.Sqrt, scale=1.0 / D, bias=epsc))
            S.wait(act, "pe", ("squares summed", KT - 1))
            S.mark("act", "root", act.activation(rb[:, 0:T], S2, ACT.Sqrt, scale=1.0 / D, bias=epsc))
            for i, (kind, k) in enumerate([("c", k) for k in range(KT)] + [("x", k) for k in range(KT)]):
                S.wait(act, "dve", ("normed", kind, k))
                n, hi, m = (TC, hc[0], 1) if kind == "c" else (T, H[0], 0)
                S.mark("act", ("hi", kind, k), act.activation(hi[:, k, :], sq[:, i % 2, 0:n], ACT.Identity, bias=mod[:, k, m:m + 1]))
                if i == 1:
                    for j in range(2):
                        split_hi(act, j, j, 1, first=True)
            act.dma_start(xT_d.rearrange("k p t -> p k t"), xT).then_inc(xT_stored, 16)
            act.wait_ge(xT_stored, 16)
            barrier("act", 1)

            def evac(j):
                act.wait_ge(gemm_done, j + 1)
                src = G[j % 2][:, 0:TC]
                if j == 0:
                    src, dst = src[0:2 * RANK], lrc
                elif j < 5:
                    dst = kc[:, (j - 1) * TC:j * TC]
                else:
                    i = j - 5
                    if i >= 4:
                        S.wait(act, "pe", ("vc turned", i // 2 - 2))
                    dst = vcT[:, (i // 2) % 2, i % 2, :]
                S.mark("act", ("ctx job", j), act.activation(dst, src, ACT.Copy))

            def gate_logs():
                for d in range(2):
                    for hh in range(2):
                        S.wait(act, "pe", ("ctx gates", d, hh))
                        for h in range(2):
                            head = 2 * hh + h
                            i = act.activation(c_g[d][:, d + head * TC:d + (head + 1) * TC], U[hh][:, h * TC:(h + 1) * TC],
                                               ACT.Identity, bias=col("bgb" if d else "bgf", head))
                        S.mark("act", ("ctx gates", d, hh), i)
                S.wait(act, "act", ("ctx gates", 1, 1))
                for d in range(2):
                    i = act.activation(c_l[d], c_g[d][:, d:d + T], ACT.Abs)
                S.mark("act", "ctx gates abs", i)
                S.wait(act, "act", "ctx gates abs")
                for d in range(2):
                    i = act.activation(c_l[d], c_l[d], ACT.Exp, scale=-1.0)
                S.mark("act", "ctx gates exp", i)
                S.wait(act, "act", "ctx gates exp")
                for d in range(2):
                    S.mark("act", ("ctx gate logs", d), act.activation(c_l[d], c_l[d], ACT.Ln, bias=1.0))
            evac(0)
            evac(1)
            for j in range(2, J_LR):
                split_hi(act, j, j % 2, j // 2 + 1)
                if j == 2:
                    gate_logs()
                evac(j)
            S.wait(act, "dve", "ctx scans")
            S.mark("act", ("ctx exps", 0), act.activation(c_l[0], c_l[0], ACT.Exp, scale=1.0 / GATE_NORM))
            S.mark("act", ("ctx exps", 1), act.activation(c_l[1], c_F[1], ACT.Exp, scale=1.0 / GATE_NORM))
            S.mark("act", "ctx totals", act.activation(c_t, c_t, ACT.Exp, scale=1.0 / GATE_NORM))
            for d in range(2):
                for h in range(2):
                    S.wait(act, "pe", ("ctx keys turned", d, h))
                    S.mark("act", ("ctx keys turned", d, h), act.activation(c_kn[d][:, 4 * h:4 * h + 4, :], U[h].rearrange("p (i t) -> p i t", i=4), ACT.Copy))
            S.wait(act, "dve", ("ctx state", 1, 3))
            act.dma_start(s0_d.rearrange("h d p v -> p h d v"), c_S).then_inc(s0_stored, 16)
            act.wait_ge(s0_stored, 16)
            barrier("act", 2)

        @block.vector
        def _(v):
            for t in range(10):
                S.wait(v, "pe", ("turned", t, 1))
                dst = cT[:, 4:8, t * P:(t + 1) * P] if t < 2 else xT[:, 4:8, (t - 2) * P:(t - 1) * P]
                S.mark("dve", ("turned copied", t), v.tensor_copy(dst, U[1].rearrange("p (i t) -> p i t", i=4)))
            S.wait(v, "act", "parameters")
            S.wait(v, "pe", ("modulation", 3))
            S.mark("dve", "shift, scale", v.tensor_tensor(mod[:, 0:16, :], G[1][:, NB:NB + 32].rearrange("p (m c) -> p m c", c=2),
                                                          broadcast(par[:, R0["bm"]:R0["bm"] + 16].unsqueeze(2), 2), ALU.add))
            S.wait(v, "dve", "shift, scale")
            S.mark("dve", "norm scales", v.scalar_tensor_tensor(gsc, mod[:, 8:16, :], 1.0, broadcast(par[:, R0["ng"]:R0["ng"] + KT].unsqueeze(2), 2), ALU.add, ALU.mult))
            for kind in ("c", "x"):
                r = rb[:, T:T + TC] if kind == "c" else rb[:, 0:T]
                S.wait(v, "act", "ctx root" if kind == "c" else "root")
                S.mark("dve", ("rstd", kind), v.reciprocal(r, r))
            S.wait(v, "dve", ("rstd", "x"))
            i = 0
            for kind in ("c", "x"):
                n, src, hi, lo, m, r = (TC, cT, *hc, 1, rb[:, T:T + TC]) if kind == "c" else (T, xT, *H, 0, rb[:, 0:T])
                for k in range(KT):
                    t = sq[:, i % 2, 0:n]
                    if i == 0:
                        S.wait(v, "pe", ("squares summed", KT - 1))
                    if i >= 2:
                        S.wait(v, "dve", ("scaled", *(("c" if i - 2 < KT else "x"), (i - 2) % KT)))
                    S.mark("dve", ("normed", kind, k), v.scalar_tensor_tensor(t, src[:, k, :], gsc[:, k, m:m + 1], r, ALU.mult, ALU.mult))
                    S.wait(v, "act", ("hi", kind, k))
                    S.mark("dve", ("scaled", kind, k), v.scalar_tensor_tensor(lo[:, k, :], t, mod[:, k, m:m + 1], hi[:, k, :].bitcast(F32), ALU.add, ALU.subtract))
                    i += 1
            S.wait(v, "pe", ("modulation", 5))
            S.mark("dve", "gate", v.tensor_tensor(mod[:, 16:24, :], G[1][:, NB + 32:NB + 48].rearrange("p (m c) -> p m c", c=2),
                                                  broadcast(par[:, R0["bm"] + 16:R0["bm"] + 24].unsqueeze(2), 2), ALU.add))
            v.wait_ge(const_landed, 48)
            for name, dst, src in (("levels", lvl, lvl_in), ("masks", maskb, mask_in), ("identity", identb, ident)):
                S.mark("dve", name, v.tensor_copy(dst, src))
            barrier("dve", 1)
            S.wait(v, "pool", "chunk mask")
            for d in range(2):
                S.wait(v, "act", ("ctx gate logs", d))
                S.mark("dve", ("ctx logs", d), v.scalar_tensor_tensor(c_g[d][:, d:d + T], c_g[d][:, d:d + T], 0.0, c_l[d], ALU.min, ALU.subtract))
            S.wait(v, "dve", ("ctx logs", 1))
            S.mark("dve", "ctx last logs", v.tensor_copy(c_t[:, 1, :].unsqueeze(2), chunks(c_g[1][:, 1:T + 1])[:, :, CH - 1:CH]))
            S.wait(v, "dve", "ctx last logs")
            S.mark("dve", "ctx starts", v.memset(chunks(c_g[1][:, 0:T])[:, :, 0:1], 0.0))
            S.wait(v, "dve", "ctx starts")
            for d in range(2):
                i = v.tensor_tensor_scan(c_F[d], smask, c_g[d][:, 0:T], 0.0, ALU.mult, ALU.add)
            S.mark("dve", "ctx sums", i)
            S.wait(v, "dve", "ctx sums")
            S.mark("dve", "ctx ends f", v.tensor_copy(c_t[:, 0, :].unsqueeze(2), chunks(c_F[0])[:, :, CH - 1:CH]))
            S.mark("dve", "ctx ends b", v.tensor_tensor(c_t[:, 1, :].unsqueeze(2), c_t[:, 1, :].unsqueeze(2), chunks(c_F[1])[:, :, CH - 1:CH], ALU.add))
            S.mark("dve", "ctx scans", v.tensor_tensor(chunks(c_l[0]), broadcast(chunks(c_F[0])[:, :, CH - 1:CH], CH), chunks(c_F[0]), ALU.subtract))
            for i in range(4):
                S.wait(v, "pe", ("vc turned", i))
                S.mark("dve", ("vc", i), v.tensor_copy(vc[:, :, i * DV:(i + 1) * DV], U[i % 2].rearrange("p (c m) -> p c m", c=2)))
            for d in range(2):
                S.wait(v, "act", ("ctx exps", d))
                S.mark("dve", ("ctx keys", d), v.tensor_tensor(c_k[d], kc, c_l[d], ALU.mult))
            S.wait(v, "act", "ctx totals")
            for d in range(2):
                for h in range(HEADS):
                    S.wait(v, "pe", ("ctx updates", d, h))
                    far, near = (0, 1) if d == 0 else (1, 0)
                    u = U[h % 2]
                    S.mark("dve", ("ctx far", d, h), v.tensor_copy(c_S[:, h, d, :], u[:, far * DV:(far + 1) * DV]))
                    S.wait(v, "dve", ("ctx far", d, h))
                    S.mark("dve", ("ctx state", d, h), v.scalar_tensor_tensor(
                        c_S[:, h, d, :], c_S[:, h, d, :], c_t[:, d, 2 * h + near:2 * h + near + 1], u[:, near * DV:(near + 1) * DV], ALU.mult, ALU.add))
            barrier("dve", 2)

    o = W0
    smask3 = take("smask3", [P, T], BF16)
    cos, sin = take("cos_t", [P, T]), take("sin_t", [P, T])
    lr = take("lr", [2 * RANK, T])
    wuph = take("wup_head", [2 * RANK, 2, DK])
    K, Q = take("keys", [P, T]), take("queries", [P, T])
    raw, sw = take("raw", [P, T]), take("swapped", [P, T])
    L = [take("sums_f", [P, T + 8]), take("sums_b", [P, T + 8])]
    vT = take("vT", [P, T])
    V = take("V", [P, TT, DV])
    E = [take("exps0", [P, T]), take("exps1", [P, T])]
    X = [take(f"scaled{i}", [P, T]) for i in range(4)]
    probs = take("scores", [P, TT, CH])
    gz = take("silu_zA", [P, 2, T])
    ST = [take("states_f", [P, TT, DV]), take("states_b", [P, TT, DV])]
    KN = [take("keysT_f", [P, TT, P]), take("keysT_b", [P, TT, P])]
    te = take("ends", [P, 2, 8])
    tx = take("end_decays", [P, 2, 8])
    tab_landed, wup_landed, s_landed, swapped = sem("tables_landed"), sem("wup_landed"), sem("states_landed"), sem("swap_landed")
    gate_stored, a_stored = sem("gates_stored"), sem("a_stored")
    PAIRS = len(LEVELS) + 2
    o_T = X[2:4]

    def gla_job(h, i):
        return J_GLA + GLA_JOBS * h + i

    def block_view(t, s):
        v = t.rearrange("p (b u) -> p b u", u=2 * s)
        return v, v[:, :, 0:s], v[:, :, s:2 * s]

    def row(d, k):
        return d[bass.ds(k, 1)].rearrange("k p t -> p (k t)")

    GLA_COLS = (lambda h: C_K + P * h, lambda h: C_Q + P * h, lambda h: C_V + 2 * P * h, lambda h: C_V + 2 * P * h + P,
                lambda h: C_ZA + 2 * P * h, lambda h: C_ZA + 2 * P * h + P, lambda h: C_GA + 2 * P * h,
                lambda h: C_GA + 2 * P * h + P, lambda h: C_GB + 2 * P * h, lambda h: C_GB + 2 * P * h + P)

    def dslab(w, c0, kt=KT, r0=0):
        return w[r0:r0 + kt * P, bass.ds(c0, P)].rearrange("(k p) c -> p k c", p=P)

    with nc.Block() as block:
        @block.sync
        def _(sp):
            load_w(J_LR, J_LR % 2, slab(w_in, C_LR))
            after_phase(sp, 2)
            sp.dma_start(cos, a["cos"]).then_inc(tab_landed, 16)
            sp.dma_start(sin, a["sin"]).then_inc(tab_landed, 16)
            S.wait(sp, "pool", "head gate weights cleared")
            with sp.Fori(0, HEADS) as h:
                S.wait(sp, "pe", "gates b1", h - 1)
                sp.dma_start(wuph[0:RANK, 0, :], a["w_gate_up_f"][0][:, bass.ds(h * DK, DK)]).then_inc(wup_landed, 16)
                sp.dma_start(wuph[RANK:2 * RANK, 1, :], a["w_gate_up_b"][0][:, bass.ds(h * DK, DK)]).then_inc(wup_landed, 16)
                for i in range(GLA_JOBS):
                    load_w(gla_job(h, i), i % 2, dslab(w_in, GLA_COLS[i](h)))
                    if i == 5:
                        S.wait(sp, "pe", "o 3", h - 1)
                        for d in range(2):
                            sp.dma_start(ST[d][:, 7 * d, :], s0_d[bass.ds(h, 1), d].rearrange("h p v -> p (h v)")).then_inc(s_landed, 16)

        @block.gpsimd
        def _(g):
            split(J_LR, J_LR % 2, J_LR // 2 + 1)
            after_phase(g, 2)
            S.mark("pool", "head gate weights cleared", g.memset(wuph, 0.0))
            chunk_mask(smask3, "head chunk mask")
            with g.Fori(0, HEADS) as h:
                for i in range(GLA_JOBS):
                    split(gla_job(h, i), i % 2, J_GLA // 2 + GLA_JOBS // 2 * h + i // 2 + 1)

        @block.tensor
        def _(pe):
            gemm(J_LR, J_LR % 2, H)
            S.wait(pe, "act", "lr")
            pe.wait_ge(tab_landed, 32)
            S.enter("pe", "gla")
            with pe.Fori(0, HEADS) as h:
                def turn_to(dst_free, name, src, blocks):
                    s = turn_to.n % 2
                    turn_to.n += 1
                    S.wait(pe, *dst_free)
                    for i, b in enumerate(blocks):
                        mm = pe.transpose(U[s][:, i * P:(i + 1) * P], src[:, b * P:(b + 1) * P], ident)
                    S.mark("pe", name, mm)
                turn_to.n = 0

                def job(i):
                    freed = {0: ("act", "gate evac 2", h - 1), 1: ("act", "gate evac 3", h - 1), 2: ("act", "raw k", h),
                             3: ("act", "raw q", h), 4: ("act", "vT 0", h), 5: ("act", "vT 1", h), 6: ("act", "zA 0", h),
                             7: ("act", "zA 1", h), 8: ("act", "gate evac 0", h), 9: ("act", "gate evac 1", h)}[i]
                    gemm(gla_job(h, i), i % 2, H, freed)

                def level(w):
                    S.wait(pe, "dve", f"stage {w}", h)
                    S.wait(pe, "dve", f"placed {w - 1}", h)
                    kx, qx = X[2 * (w % 2)], X[2 * (w % 2) + 1]
                    for c in range(TT):
                        mm = pe.matmul(S2[:, c * CH:(c + 1) * CH], kx[:, c * CH:(c + 1) * CH], qx[:, c * CH:(c + 1) * CH], start=True, stop=True)
                    S.mark("pe", f"level {w}", mm)

                pe.wait_ge(wup_landed, 32 * h + 32)
                for d in range(2):
                    for n in range(2):
                        S.wait(pe, "act", *((f"gates f{n}", h) if d else (f"summed r{n}", h - 1)))
                        S.mark("pe", f"gates {'fb'[d]}{n}", pe.matmul(U[n], wuph[:, d, :], lr[:, n * NB:(n + 1) * NB], start=True, stop=True))
                job(0)
                job(1)
                job(2)
                job(3)
                S.wait(pe, "act", "vT 0", h)
                turn_to(("act", "gates b0", h), "v turned 00", vT, range(0, 4))
                turn_to(("act", "gates b1", h), "v turned 01", vT, range(4, 8))
                job(4)
                S.wait(pe, "act", "vT 1", h)
                turn_to(("act", "V 00", h), "v turned 10", vT, range(0, 4))
                turn_to(("act", "V 01", h), "v turned 11", vT, range(4, 8))
                S.wait(pe, "dve", "stage 0", h)
                for d in range(2):
                    for n in range(2):
                        turn_to(("act", f"V 1{n}" if d == 0 else f"KN 0{n}", h), f"keys turned {d}{n}", X[d], range(4 * n, 4 * n + 4))
                job(5)
                for d in range(2):
                    for i in range(4):
                        S.wait(pe, "act", f"KN {d}1", h)
                        if d == 0 and i < 2:
                            S.wait(pe, "act", f"KN 1{i}", h)
                        else:
                            S.wait(pe, "dve", f"state {d if i >= 2 else 0}{(i - 2) % 4}", h)
                        for n in range(2):
                            c = 2 * i + n if d == 0 else 7 - 2 * i - n
                            mm = pe.matmul(U[i % 2][:, n * DV:(n + 1) * DV], KN[d][:, c, :], V[:, c, :], start=True, stop=True)
                        S.mark("pe", f"updates {d}{i}", mm)
                    if d == 0:
                        job(6)
                S.wait(pe, "dve", "rope q", h)
                S.wait(pe, "dve", "rope k", h)
                for c in range(TT):
                    mm = pe.matmul(S2[:, c * CH:(c + 1) * CH], K[:, c * CH:(c + 1) * CH], Q[:, c * CH:(c + 1) * CH], start=True, stop=True)
                S.mark("pe", "level 0", mm)
                level(1)
                job(7)
                level(2)
                level(3)
                job(8)
                level(4)
                level(5)
                job(9)
                level(6)
                level(7)
                S.wait(pe, "dve", "placed 7", h)
                S.wait(pe, "dve", f"stage {PAIRS - 1}", h)
                for m in range(2):
                    for n in range(2):
                        i = 2 * m + n
                        S.wait(pe, *(("dve", f"state 1{2 + i}", h) if i < 2 else ("act", f"o {i - 2}", h)))
                        for c in range(4 * n, 4 * n + 4):
                            dst = U[n][:, (c % 4) * CH:(c % 4 + 1) * CH]
                            cols, f = slice(c * CH, (c + 1) * CH), slice(m * P, (m + 1) * P)
                            pe.matmul(dst, V[:, c, f], probs[:, c, :], start=True, stop=False)
                            pe.matmul(dst, ST[0][:, c, f], X[0][:, cols], start=False, stop=False)
                            mm = pe.matmul(dst, ST[1][:, c, f], X[1][:, cols], start=False, stop=True)
                        S.mark("pe", f"o {i}", mm)
                S.wait(pe, "dve", "o squares", h)
                for n in range(2):
                    S.wait(pe, "act", f"o {2 + n}", h)
                    mm = pe.matmul(U[n], ones, E[0][:, n * NB:(n + 1) * NB], start=True, stop=True)
                    S.mark("pe", f"o summed {n}", mm)
            S.leave("pe", HEADS)
            barrier("pe", 3)

        @block.scalar
        def _(act):
            act.wait_ge(gemm_done, J_LR + 1)
            S.mark("act", "lr", act.activation(lr, G[J_LR % 2][0:2 * RANK, :], ACT.Copy))
            S.enter("act", "gla")
            with act.Fori(0, HEADS) as h:
                for d in range(2):
                    b = par[:, bass.ds(h + (R0["bgb"] if d else R0["bgf"]), 1)]
                    for n in range(2):
                        S.wait(act, "pe", f"gates {'fb'[d]}{n}", h)
                        if d == 0 and n == 0:
                            S.wait(act, "dve", "stage 8", h - 1)
                        settle(act, h)
                        S.mark("act", f"gates {'fb'[d]}{n}", act.activation(L[d][:, d + n * NB:d + (n + 1) * NB], U[n], ACT.Identity, bias=b))
                S.wait(act, "act", "gates b1", h)
                S.wait(act, "dve", "o scaled 1", h - 1)
                for d in range(2):
                    i = act.activation(E[d], L[d][:, d:d + T], ACT.Abs)
                S.mark("act", "gates abs", i)
                S.wait(act, "act", "gates abs", h)
                for d in range(2):
                    i = act.activation(E[d], E[d], ACT.Exp, scale=-1.0)
                S.mark("act", "gates exp", i)
                S.wait(act, "act", "gates exp", h)
                for d in range(2):
                    S.mark("act", f"gate logs {d}", act.activation(E[d], E[d], ACT.Ln, bias=1.0))

                def evac(i, name, dst, func=ACT.Copy, **more):
                    act.wait_ge(gemm_done, gla_job(h, i) + 1)
                    S.mark("act", name, act.activation(dst, G[i % 2], func, **more))

                def swap(turn):
                    for q in range(4):
                        src = q ^ 1
                        act.dma_start(sw[32 * q:32 * q + 32, :], raw[32 * src:32 * src + 32, :]).then_inc(swapped, 16)
                evac(0, "raw k", raw)
                S.wait(act, "act", "raw k", h)
                swap(0)
                S.wait(act, "dve", "rope k", h)
                evac(1, "raw q", raw, scale=float(DK) ** -0.5)
                S.wait(act, "act", "raw q", h)
                swap(1)
                S.wait(act, "dve", "exponents 0", h)
                i = act.activation(E[0], E[0], ACT.Exp, scale=1.0 / GATE_NORM)
                S.mark("act", "exps 0 0", i)
                S.mark("act", "exps 0 1", act.activation(E[1], L[1][:, 0:T], ACT.Exp, scale=1.0 / GATE_NORM))
                S.mark("act", "end decays", act.activation(tx, te, ACT.Exp, scale=1.0 / GATE_NORM))
                evac(2, "vT 0", vT)

                def copy_v(m):
                    for n in range(2):
                        S.wait(act, "pe", f"v turned {m}{n}", h)
                        S.mark("act", f"V {m}{n}", act.activation(V[:, 4 * n:4 * n + 4, m * P:(m + 1) * P], U[n].rearrange("p (c f) -> p c f", f=P), ACT.Copy))
                copy_v(0)
                evac(3, "vT 1", vT)
                copy_v(1)
                for d in range(2):
                    for n in range(2):
                        S.wait(act, "pe", f"keys turned {d}{n}", h)
                        S.mark("act", f"KN {d}{n}", act.activation(KN[d][:, 4 * n:4 * n + 4, :], U[n].rearrange("p (c f) -> p c f", f=P), ACT.Copy))

                def exps(w):
                    for e in range(2):
                        if w < PAIRS - 1 or e == 1:
                            S.wait(act, "dve", f"exponents {w} {e}", h)
                        else:
                            S.wait(act, "dve", f"stage {w - 1}", h)
                        src = L[0][:, 0:T] if w == PAIRS - 1 and e == 0 else E[e]
                        S.mark("act", f"exps {w} {e}", act.activation(E[e], src, ACT.Exp, scale=1.0 / GATE_NORM))
                exps(1)
                evac(4, "zA 0", gz[:, 0, :], ACT.Silu)
                evac(5, "zA 1", gz[:, 1, :], ACT.Silu)

                def gate(i):
                    dst = (raw, sw)[i % 2]
                    if i < 2:
                        S.wait(act, "dve", "rope q", h)
                    else:
                        act.wait_ge(gate_stored, 64 * h + 32)
                    evac(6 + i, f"gate evac {i}", dst, ACT.Sigmoid)
                    S.wait(act, "act", f"gate evac {i}", h)
                    act.dma_start(row((sga_d, sgb_d)[i // 2], 2 * h + i % 2), dst).then_inc(gate_stored, 16)
                exps(2)
                gate(0)
                exps(3)
                exps(4)
                gate(1)
                exps(5)
                exps(6)
                gate(2)
                exps(7)
                exps(8)
                gate(3)
                act.wait_ge(gate_stored, 64 * h + 64)
                for m in range(2):
                    for n in range(2):
                        i = 2 * m + n
                        S.wait(act, "pe", f"o {i}", h)
                        S.mark("act", f"o {i}", act.activation(o_T[m][:, n * NB:(n + 1) * NB], U[n], ACT.Copy))
                for m in range(2):
                    S.wait(act, "act", f"o {2 * m + 1}", h)
                    S.mark("act", f"o squares {m}", act.activation(E[m], o_T[m], ACT.Square))
                for n in range(2):
                    S.wait(act, "pe", f"o summed {n}", h)
                    S.mark("act", f"summed r{n}", act.activation(E[1][:, n * NB:(n + 1) * NB], U[n], ACT.Sqrt, scale=1.0 / DV, bias=epsc))
                S.wait(act, "dve", "o scaled 1", h)
                for m in range(2):
                    act.dma_start(row(a_d, 2 * h + m), o_T[m]).then_inc(a_stored, 16)
                act.wait_ge(a_stored, 32 * h + 32)
            S.leave("act", HEADS)
            barrier("act", 3)

        @block.vector
        def _(v):
            def do(name, ins):
                return S.mark("dve", name, ins)
            v.wait_ge(tab_landed, 32)
            S.wait(v, "pool", "head chunk mask")
            v.wait_ge(const_landed, 48)
            S.enter("dve", "gla")
            with v.Fori(0, HEADS) as h:
                def me(name, turn=None):
                    S.wait(v, "dve", name, h if turn is None else turn)
                for d in range(2):
                    S.wait(v, "act", f"gate logs {d}", h)
                    do(f"logs {d}", v.scalar_tensor_tensor(L[d][:, d:d + T], L[d][:, d:d + T], 0.0, E[d], ALU.min, ALU.subtract))
                me("logs 1")
                do("last logs", v.tensor_copy(te[:, 1, :].unsqueeze(2), chunks(L[1][:, 1:T + 1])[:, :, CH - 1:CH]))
                me("last logs")
                do("starts", v.memset(chunks(L[1][:, 0:T])[:, :, 0:1], 0.0))
                me("starts")
                for d in range(2):
                    i = v.tensor_tensor_scan(L[d][:, 0:T], smask3, L[d][:, 0:T], 0.0, ALU.mult, ALU.add)
                do("sums", i)
                me("sums")
                do("ends f", v.tensor_copy(te[:, 0, :].unsqueeze(2), chunks(L[0][:, 0:T])[:, :, CH - 1:CH]))
                do("ends b", v.tensor_tensor(te[:, 1, :].unsqueeze(2), te[:, 1, :].unsqueeze(2), chunks(L[1][:, 0:T])[:, :, CH - 1:CH], ALU.add))
                F, B = L[0][:, 0:T], L[1][:, 0:T]
                do("exponents 0", v.tensor_tensor(chunks(E[0]), broadcast(chunks(F)[:, :, CH - 1:CH], CH), chunks(F), ALU.subtract))

                def rope(name, n, dst):
                    S.wait(v, "act", f"raw {name}", h)
                    do(f"cos {name}", v.tensor_tensor(dst, raw, cos, ALU.mult))
                    v.wait_ge(swapped, 128 * h + 64 * (n + 1))
                    do(f"sin {name}", v.tensor_tensor(sw, sw, sin, ALU.mult))
                    me(f"sin {name}")
                    do(f"rope {name}", v.tensor_tensor(dst, dst, sw, ALU.add))
                S.wait(v, "pe", "level 0", h - 1)
                rope("k", 0, K)
                rope("q", 1, Q)
                me("rope q")

                def stage(w, first, second):
                    if w >= 2:
                        S.wait(v, "pe", f"level {w - 2}" if w > 2 else "keys turned 11", h)
                    elif w == 0:
                        S.wait(v, "pe", "o 3", h - 1)
                    for e, src in enumerate((first, second)):
                        S.wait(v, "act", f"exps {w} {e}", h)
                        i = v.tensor_tensor(X[2 * (w % 2) + e], src, E[e], ALU.mult)
                        do(f"stage {w}" if e else f"stage {w} k", i)

                def exponents(w):
                    s = LEVELS[w - 1]
                    me(f"stage {w - 1} k")
                    fv, fl, fr = block_view(F, s)
                    bv, bl, br = block_view(B, s)
                    fb, bb = broadcast(fv[:, :, s - 1:s], s), broadcast(bv[:, :, s:s + 1], s)
                    _, kl, kr = block_view(E[0], s)
                    _, ql, qr = block_view(E[1], s)
                    v.tensor_tensor(kl, fb, fl, ALU.subtract)
                    do(f"exponents {w} 0", v.tensor_tensor(kr, br, bb, ALU.subtract))
                    me(f"stage {w - 1}")
                    v.tensor_tensor(ql, bb, bl, ALU.subtract)
                    do(f"exponents {w} 1", v.tensor_tensor(qr, fr, fb, ALU.subtract))

                def place(w):
                    S.wait(v, "pe", f"level {w}", h)
                    s2 = chunks(S2)
                    if w == 0:
                        do("placed 0", v.scalar_tensor_tensor(probs, s2, 2.0, ident.unsqueeze(1).to_broadcast([P, TT, P]), ALU.mult, ALU.mult))
                    else:
                        me(f"placed {w - 1}")
                        settle(v, h)
                        do(f"placed {w}", v.copy_predicated(probs, lvl[:, w - 1, :].unsqueeze(1).to_broadcast([P, TT, P]), s2))
                stage(0, K, K)
                exponents(1)
                v.wait_ge(s_landed, 32 * h + 32)
                S.wait(v, "act", "end decays", h)
                for d in range(2):
                    for i in range(4):
                        S.wait(v, "pe", f"updates {d}{i}", h)
                        for n in range(2):
                            c = 2 * i + n if d == 0 else 7 - 2 * i - n
                            if i == 3 and n == 1:
                                continue
                            to = c + 1 if d == 0 else c - 1
                            if (i, n) != (0, 0):
                                me(f"state {d}{i} {0}" if n else f"state {d}{i - 1}")
                            do(f"state {d}{i}" if n or i == 3 else f"state {d}{i} 0",
                               v.scalar_tensor_tensor(ST[d][:, to, :], ST[d][:, c, :], tx[:, d, c:c + 1], U[i % 2][:, n * DV:(n + 1) * DV], ALU.mult, ALU.add))
                S.wait(v, "act", "gates f0", h)
                stage(1, K, Q)
                S.wait(v, "pe", "o 3", h - 1)
                for w in range(1, len(LEVELS) + 1):
                    if w < len(LEVELS):
                        exponents(w + 1)
                    place(w - 1)
                    if w < len(LEVELS):
                        stage(w + 1, K, Q)
                me(f"stage {PAIRS - 2}")
                do(f"exponents {PAIRS - 1} 1", v.tensor_tensor(chunks(E[1]), broadcast(te[:, 1, :].unsqueeze(2), CH), chunks(B), ALU.subtract))
                place(len(LEVELS))
                stage(PAIRS - 1, Q, Q)
                S.wait(v, "act", "o squares 1", h)
                do("o squares", v.tensor_tensor(E[0], E[0], E[1], ALU.add))
                S.wait(v, "act", "summed r1", h)
                do("o rstd", v.reciprocal(E[1], E[1]))
                me("o rstd")
                for m in range(2):
                    do(f"o normed {m}", v.scalar_tensor_tensor(o_T[m], o_T[m], col("gg", m), E[1], ALU.mult, ALU.mult))
                for m in range(2):
                    me(f"o normed {m}")
                    if m == 0:
                        S.wait(v, "act", "zA 1", h)
                    do(f"o scaled {m}", v.tensor_tensor(o_T[m], o_T[m], gz[:, m, :], ALU.mult))
            S.leave("dve", HEADS)
            barrier("dve", 3)

    o = W0
    A = [take("A_hi", [P, KT, T], F32R), take("A_lo", [P, KT, T], F32R)]
    o4 = o
    PAD = 8
    u_in = take("pool_in", [P, T + PAD])
    cs = take("pool_sums", [P, T + 2 * PAD + 1])
    d_mov = [take("pooled_hi", [P, 2, T], F32R), take("pooled_lo", [P, 2, T], F32R)]
    pz = take("silu_zB", [P, 2, T])
    inv = take("inv_count", [P, T])
    pw = take("pool_work", [P, T])
    a_in = take("a_in", [P, 2, T])
    o = o4
    X2 = take("x2", [P, KT, T])
    gs, bs = take("tiles_in", [P, 2, T]), take("tiles_made", [P, 2, T])

    POOL_ORDER = [(g, w) for g in range(4) for w in ("u0", "u1", "z0", "z1", "p0", "p1")]
    inv_landed, ain_landed, b_stored = sem("inv_landed"), sem("a_in_landed"), sem("b_stored")
    gs_landed, bs_landed = [sem("gs_landed0"), sem("gs_landed1")], [sem("bs_landed0"), sem("bs_landed1")]

    def pool_src(g, what):
        m = int(what[1])
        if what[0] == "p":
            return a["w_pool"][0, g][:, m * P:(m + 1) * P].rearrange("(k p) c -> p k c", p=P), 2
        return slab(w_in, (C_UB if what[0] == "u" else C_ZB) + (2 * g + m) * P), KT

    def pool_freed(n):
        if n < 0:
            return None
        g, what = POOL_ORDER[n]
        return "dve" if what[0] == "p" else "act", ("pool job", g, what)

    def tile2(t, k):
        return t[:, bass.ds(k, 1), :].rearrange("p k t -> p (k t)")

    BRANCHES = (("bra", J_BRA, a["w_branch_a"][0], A), ("brb", J_BRB, a["w_branch_b"][0], H), ("out", J_OUT, a["w_out"][0], A))

    def loads_of_8(j0, w, kt=KT, r0=0):
        with nc.sync.Fori(0, KT // 2) as i:
            for m in range(2):
                load_w(j0 + 2 * i + m, (j0 + m) % 2, dslab(w, (2 * i + m) * P, kt, r0), kt)

    def splits_of(j0, pairs=KT // 2, kt=KT):
        with nc.gpsimd.Fori(0, pairs) as i:
            for m in range(2):
                split(j0 + 2 * i + m, (j0 + m) % 2, i + ((j0 + m) // 2 + 1), kt)

    def products_of_8(name, j0, mov, kt=KT):
        S.enter("pe", name)
        with nc.tensor.Fori(0, KT // 2) as i:
            for m in range(2):
                gemm(j0 + 2 * i + m, (j0 + m) % 2, mov, ("dve", f"{name} job {m}", i - 1), kt=kt)
        S.leave("pe", KT // 2)

    def residual_act(name, first_wait, fetch=None, squares=True):
        act = nc.scalar
        for w in first_wait:
            S.wait(act, *w)
        S.enter("act", name)
        with act.Fori(0, KT // 2) as i:
            for m in range(2):
                if fetch is not None:
                    S.wait(act, "dve", f"{name} job {m}", i - 1)
                    act.dma_start(gs[:, m, :], row(fetch, 2 * i + m)).then_inc(gs_landed[m], 16)
                if squares:
                    S.wait(act, "dve", f"{name} sum {m}", i - 1)
                    S.wait(act, "dve", f"{name} job {m}", i)
                    settle(act, i)
                    S.mark("act", f"{name} square {m}", act.activation(bs[:, m, :], tile2(X2, 2 * i + m), ACT.Square))
        S.leave("act", KT // 2)

    def residual_dve(name, j0, fetched=None, gate=False, squares=True):
        v = nc.vector
        if squares:
            S.mark("dve", f"{name} zero", v.memset(S2, 0.0))
            S.wait(v, "dve", f"{name} zero")
        S.enter("dve", name)
        with v.Fori(0, KT // 2) as i:
            for m in range(2):
                v.wait_ge(gemm_done, j0 + 2 * i + m + 1)
                if fetched is not None:
                    v.wait_ge(gs_landed[m], 16 * (fetched + i + 1))
                k = 2 * i + m
                other = gs[:, m, :] if fetched is not None else tile2(X2, k)
                by = mod[:, bass.ds(16 + k, 1), 0:1].rearrange("p a b -> p (a b)") if gate else 1.0
                S.mark("dve", f"{name} job {m}", v.scalar_tensor_tensor(tile2(X2, k), G[(j0 + m) % 2], by, other, ALU.mult, ALU.add))
                if squares:
                    S.wait(v, "act", f"{name} square {m}", i)
                    S.mark("dve", f"{name} sum {m}", v.tensor_tensor(S2, S2, bs[:, m, :], ALU.add))
                    S.wait(v, "dve", f"{name} sum {m}", i)
        S.leave("dve", KT // 2)
        if squares:
            S.mark("dve", f"{name} squares", v.tensor_copy(bs[:, 1, :], S2))

    def norm_pe(name):
        S.wait(nc.tensor, "dve", f"{name} squares")
        for n in range(2):
            mm = nc.tensor.matmul(S2[:, n * NB:(n + 1) * NB], ones, bs[:, 1, n * NB:(n + 1) * NB], start=True, stop=True)
        S.mark("pe", f"{name} summed", mm)

    def norm_act(name, dst):
        act = nc.scalar
        S.wait(act, "pe", f"{name} summed")
        S.mark("act", f"{name} root", act.activation(gs[:, 0, :], S2, ACT.Sqrt, scale=1.0 / D, bias=epsc))
        for k in range(KT):
            S.wait(act, "dve", (name, "t", k))
            S.mark("act", (name, "hi", k), act.activation(dst[0][:, k, :], bs[:, k % 2, :], ACT.Copy))

    def norm_dve(name, gain, dst):
        v = nc.vector
        S.wait(v, "act", f"{name} root")
        S.mark("dve", f"{name} rstd", v.reciprocal(gs[:, 0, :], gs[:, 0, :]))
        S.wait(v, "dve", f"{name} rstd")
        for k in range(KT):
            if k >= 2:
                S.wait(v, "dve", (name, "lo", k - 2))
            S.mark("dve", (name, "t", k), v.scalar_tensor_tensor(bs[:, k % 2, :], X2[:, k, :], col(gain, k), gs[:, 0, :], ALU.mult, ALU.mult))
            S.wait(v, "act", (name, "hi", k))
            S.mark("dve", (name, "lo", k), v.tensor_tensor(dst[1][:, k, :], bs[:, k % 2, :], dst[0][:, k, :].bitcast(F32), ALU.subtract))

    with nc.Block() as block:
        @block.sync
        def _(sp):
            for n, (g, what) in enumerate(POOL_ORDER):
                src, kt = pool_src(g, what)
                load_w(J_POOL + n, n % 2, src, kt)
                if n == 1:
                    after_phase(sp, 3)
                    for k in range(2):
                        sp.dma_start(a_in[:, k, :], a_d[k]).then_inc(ain_landed, 16)
                    sp.dma_start(inv, a["inv_count"][0]).then_inc(inv_landed, 16)
                if n >= 3 and n % 3 == 0 and n // 3 + 1 < KT:
                    k = n // 3 + 1
                    S.wait(sp, "dve", ("a split", k - 2))
                    sp.dma_start(a_in[:, k % 2, :], a_d[k]).then_inc(ain_landed, 16)
                if what == "p0" and g < 3:
                    S.wait(sp, "dve", ("pooled", g, 1))
                    sp.dma_start(inv, a["inv_count"][g + 1]).then_inc(inv_landed, 16)
            for _, j0, w, _ in BRANCHES:
                loads_of_8(j0, w)

        @block.gpsimd
        def _(g):
            for n, (grp, what) in enumerate(POOL_ORDER):
                split(J_POOL + n, n % 2, (J_POOL + n) // 2 + 1, pool_src(grp, what)[1])
            for _, j0, _, _ in BRANCHES:
                splits_of(j0)

        @block.tensor
        def _(pe):
            for n, (g, what) in enumerate(POOL_ORDER):
                if what == "p0":
                    S.wait(pe, "dve", ("pooled lo", g, 1))
                gemm(J_POOL + n, n % 2, d_mov if what[0] == "p" else H, pool_freed(n - 2), kt=pool_src(g, what)[1])
            barrier("pe", 4)
            for name, j0, _, mov in BRANCHES:
                if name == "brb":
                    S.wait(pe, "dve", "bra job 1", KT // 2 - 1)
                    S.wait(pe, "dve", "b split 1", KT // 2 - 1)
                if name == "out":
                    S.wait(pe, "dve", "mix split 1", KT // 2 - 1)
                products_of_8(name, j0, mov)

        @block.scalar
        def _(act):
            for n, (g, what) in enumerate(POOL_ORDER):
                m = int(what[1])
                if what[0] == "u":
                    act.wait_ge(gemm_done, J_POOL + n + 1)
                    if (g, m) != (0, 0):
                        S.wait(act, "dve", ("pooled", *((g, 0) if m else (g - 1, 1))))
                    S.mark("act", ("pool job", g, what), act.activation(u_in[:, 0:T], G[n % 2], ACT.Copy))
                elif what[0] == "z":
                    act.wait_ge(gemm_done, J_POOL + n + 1)
                    if g:
                        act.wait_ge(b_stored, 32 * g)
                    S.mark("act", ("pool job", g, what), act.activation(pz[:, m, :], G[n % 2], ACT.Silu))
                else:
                    S.wait(act, "dve", ("pool job", g, what))
                    act.dma_start(b_d[2 * g + m], pz[:, m, :]).then_inc(b_stored, 16)
                if n % 3 == 0:
                    k = n // 3
                    act.wait_ge(ain_landed, 16 * max(k + 1, 2))
                    S.mark("act", ("a hi", k), act.activation(A[0][:, k, :], a_in[:, k % 2, :], ACT.Copy))
            act.wait_ge(b_stored, 16 * KT)
            barrier("act", 4)
            S.enter("act", "bra")
            with act.Fori(0, KT // 2) as i:
                for m in range(2):
                    S.wait(act, "dve", f"bra job {m}", i - 1)
                    act.dma_start(gs[:, m, :], row(sga_d, 2 * i + m)).then_inc(gs_landed[m], 16)
                    S.wait(act, "dve", f"b split {m}", i - 1)
                    act.dma_start(bs[:, m, :], row(b_d, 2 * i + m)).then_inc(bs_landed[m], 16)
                    act.wait_ge(bs_landed[m], 16 * i + 16)
                    settle(act, i)
                    S.mark("act", f"b hi {m}", act.activation(tile2(H[0], 2 * i + m), bs[:, m, :], ACT.Copy))
            S.leave("act", KT // 2)
            S.wait(act, "dve", "bra job 1", KT // 2 - 1)
            S.enter("act", "brb")
            with act.Fori(0, KT // 2) as i:
                for m in range(2):
                    S.wait(act, "dve", f"mix {m}", i - 1)
                    act.dma_start(gs[:, m, :], row(sgb_d, 2 * i + m)).then_inc(gs_landed[m], 16)
                    S.wait(act, "dve", f"mix {m}", i)
                    settle(act, i)
                    S.mark("act", f"mix hi {m}", act.activation(tile2(A[0], 2 * i + m), bs[:, m, :], ACT.Copy))
            S.leave("act", KT // 2)
            residual_act("out", [("dve", "mix split 1", KT // 2 - 1)], fetch=xT_d)

        @block.vector
        def _(v):
            def do(name, ins):
                S.mark("dve", name, ins)
                return name
            def me(name, turn=None):
                S.wait(v, "dve", name, turn)
            v.memset(u_in[:, T:T + PAD], 0.0)
            do("pool pads", v.memset(cs[:, 0:PAD + 1], 0.0))
            me("pool pads")
            for n, (g, what) in enumerate(POOL_ORDER):
                m, half = int(what[1]), POOL_WINDOWS[g] // 2
                if what[0] == "u":
                    S.wait(v, "act", ("pool job", g, what))
                    me(do(("pool sums", g, m), v.tensor_tensor_scan(cs[:, PAD + 1:], u_in, u_in, 0.0, ALU.add, ALU.bypass)))
                    me(do(("pool windows", g, m), v.tensor_tensor(pw, cs[:, PAD + half:PAD + half + T], cs[:, PAD - half:PAD - half + T], ALU.subtract)))
                    v.wait_ge(inv_landed, 16 * (g + 1))
                    me(do(("pool means", g, m), v.tensor_tensor(pw, pw, inv, ALU.mult)))
                    me(do(("pooled", g, m), v.tensor_tensor(pw, pw, u_in[:, 0:T], ALU.subtract)))
                    if g and m == 0:
                        v.wait_ge(gemm_done, J_POOL + 6 * g)
                    me(do(("pooled hi", g, m), v.tensor_copy(d_mov[0][:, m, :], pw)))
                    me(do(("pooled lo", g, m), v.tensor_tensor(d_mov[1][:, m, :], pw, d_mov[0][:, m, :].bitcast(F32), ALU.subtract)))
                elif what[0] == "p":
                    v.wait_ge(gemm_done, J_POOL + n + 1)
                    S.wait(v, "act", ("pool job", g, f"z{m}"))
                    do(("pool job", g, what), v.scalar_tensor_tensor(pz[:, m, :], G[n % 2], col("ps", 2 * g + m), pz[:, m, :], ALU.mult, ALU.mult))
                if n % 3 == 0:
                    k = n // 3
                    S.wait(v, "act", ("a hi", k))
                    do(("a split", k), v.tensor_tensor(A[1][:, k, :], a_in[:, k % 2, :], A[0][:, k, :].bitcast(F32), ALU.subtract))
            barrier("dve", 4)
            S.enter("dve", "bra")
            with v.Fori(0, KT // 2) as i:
                for m in range(2):
                    k = 2 * i + m
                    S.wait(v, "act", f"b hi {m}", i)
                    do(f"b split {m}", v.tensor_tensor(tile2(H[1], k), bs[:, m, :], tile2(H[0], k).bitcast(F32), ALU.subtract))
                    v.wait_ge(gemm_done, J_BRA + k + 1)
                    v.wait_ge(gs_landed[m], 16 * i + 16)
                    do(f"bra job {m}", v.tensor_tensor(tile2(X2, k), G[m], gs[:, m, :], ALU.mult))
            S.leave("dve", KT // 2)
            me("bra job 1", KT // 2 - 1)
            S.enter("dve", "brb")
            with v.Fori(0, KT // 2) as i:
                for m in range(2):
                    k = 2 * i + m
                    v.wait_ge(gemm_done, J_BRB + k + 1)
                    v.wait_ge(gs_landed[m], 16 * i + 16 + 16 * KT // 2)
                    do(f"brb job {m}", v.tensor_tensor(gs[:, m, :], G[m], gs[:, m, :], ALU.mult))
                    me(f"brb job {m}", i)
                    me(f"mix split {m}", i - 1)
                    do(f"mix {m}", v.tensor_tensor(bs[:, m, :], gs[:, m, :], tile2(X2, k), ALU.add))
                    S.wait(v, "act", f"mix hi {m}", i)
                    do(f"mix split {m}", v.tensor_tensor(tile2(A[1], k), bs[:, m, :], tile2(A[0], k).bitcast(F32), ALU.subtract))
            S.leave("dve", KT // 2)
            residual_dve("out", J_OUT, fetched=KT, gate=True)

    o = W0
    qk = {x: [take(f"{x}_q", [P, T]), take(f"{x}_k", [P, T])] for x in "fs"}
    av = {x: take(f"{x}_v", [P, TT, P]) for x in "fs"}
    ON = take("att_out", [P, TT, P])
    avT = ON.rearrange("p t d -> p (t d)")
    OT = take("att_outT", [P, KT, T])
    pT = [take("probsT0", [P, 4, P]), take("probsT1", [P, 4, P])]
    assert o <= W0 + 64 * KB, o
    o = W0 + 96 * KB
    pr = [take("probs0", [P, T]), take("probs1", [P, T])]
    nots = take("not_taken", [P, T])
    left = take("left_over", [P, T + 8])
    rs = take("row_sums", [P, 2, 1])
    mn = take("row_mins", [P, 2, 1])
    nf_d = scratch("forget_sums", (S_HEADS, T))
    w_in2 = a["w_in_2"][0]
    nf_stored, nf_landed, out_stored = sem("forget_sums_stored"), sem("forget_sums_landed"), [sem("out_stored0"), sem("out_stored1")]
    Z = [S2, G[1]]
    fsum = [nots, left[:, 0:T]]
    TILES = [(hh, tt) for hh in range(2) for tt in range(TT)]
    GROUPS = [(n, g) for n, (hh, tt) in enumerate(TILES) for g in range(tt // 4 + 1)]
    SCORE_READER = {"f": ("dve", "f scores"), "s": ("act", "s not")}

    def groups_of(n):
        return [(c, g) for c, (m, g) in enumerate(GROUPS) if m == n]

    def before(x, i):
        return ("s", i - 1) if x == "f" else ("f", i)

    ATT_COLS = (S_FQ, S_FK, S_FV, S_SQ, S_SK, S_SV)

    def sum_squares(pe, name, src, n0, n1, dst):
        for k in range(n0, n1):
            S.wait(pe, "act", (name, "square", k))
            for n in range(2):
                mm = pe.matmul(dst[:, n * NB:(n + 1) * NB], ones, src[k % 2][:, n * NB:(n + 1) * NB], start=k == n0, stop=k == n1 - 1)
            S.mark("pe", (name, "square summed", k), mm)

    def normed(k, src, gain, scale, name, dst, tmp):
        v = nc.vector
        if k >= 2:
            S.wait(v, "dve", (name, "lo", k - 2))
        S.mark("dve", (name, "t", k), v.scalar_tensor_tensor(tmp[k % 2], src[:, k, :], gain, scale, ALU.mult, ALU.mult))
        S.wait(v, "act", (name, "hi", k))
        S.mark("dve", (name, "lo", k), v.tensor_tensor(dst[1][:, k, :], tmp[k % 2], dst[0][:, k, :].bitcast(F32), ALU.subtract))

    def hi_part(k, name, dst, tmp):
        S.wait(nc.scalar, "dve", (name, "t", k))
        S.mark("act", (name, "hi", k), nc.scalar.activation(dst[0][:, k, :], tmp[k % 2], ACT.Copy))

    with nc.Block() as block:
        @block.sync
        def _(sp):
            load_w(J_FL, J_FL % 2, slab(w_in2, S_FL))
            with sp.Fori(0, HEADS) as i:
                for m, c in enumerate(ATT_COLS):
                    load_w(J_ATT + ATT_JOBS * i + m, (J_ATT + m) % 2, dslab(w_in2, i * P + c))
            loads_of_8(J_OUT2, a["w_out_2"][0])

        @block.gpsimd
        def _(g):
            split(J_FL, J_FL % 2, J_FL // 2 + 1)
            with g.Fori(0, HEADS) as i:
                for m in range(ATT_JOBS):
                    split(J_ATT + ATT_JOBS * i + m, (J_ATT + m) % 2, i * (ATT_JOBS // 2) + ((J_ATT + m) // 2 + 1))
            splits_of(J_OUT2)

        @block.tensor
        def _(pe):
            norm_pe("out")
            S.wait(pe, "act", "out root")
            tiles = [bs[:, 0, :], bs[:, 1, :]]
            sum_squares(pe, "x3", tiles, 0, KT, S2)
            S.mark("pe", "x3 summed", pe.drain())
            S.wait(pe, "dve", ("x3", "lo", KT - 1))
            gemm(J_FL, J_FL % 2, H)
            S.wait(pe, "act", "f logit")

            def job(i, x, m):
                y, turn = before(x, i)
                freed = {0: (*SCORE_READER[y][:1], f"{SCORE_READER[y][1]} {15}", turn), 1: ("dve", f"{y} out 15", turn), 2: ("act", f"{x} q", i)}[m]
                mm = m + (3 if x == "s" else 0)
                gemm(J_ATT + ATT_JOBS * i + mm, (J_ATT + mm) % 2, H, freed, pair=(1, 0, 1)[m])

            def scores(i, x, n):
                (hh, tt), (q, k) = TILES[n], qk[x]
                z, w, part = Z[n % 2], (TILES[n][1] + 1) * P, slice(HD * TILES[n][0], HD * TILES[n][0] + HD)
                if n == 0:
                    S.wait(pe, "act", f"{x} k", i)
                    if x == "s":
                        S.wait(pe, "dve", "f scores 14", i)
                elif n == 1:
                    S.wait(pe, "act", f"{x} vT", i)
                else:
                    S.wait(pe, SCORE_READER[x][0], f"{SCORE_READER[x][1]} {n - 2}", i)
                for b in range((w + NB - 1) // NB):
                    cols = slice(b * NB, min(w, (b + 1) * NB))
                    pe.matmul(z[:, cols], q[part, tt * P:(tt + 1) * P], k[part, cols], start=True, stop=tt // 4 != b)
                mm = pe.matmul(z[:, tt * P:w], identb, maskb[:, "fs".index(x), :], start=False, stop=True)
                S.mark("pe", f"{x} z {n}", mm)

            def turned(i, x, n):
                maker, made = ("act", f"f probs {n}") if x == "f" else ("dve", f"s probs {n}")
                for c, g in groups_of(n):
                    reader, read = ("act", "dve")[c % 2], f"{x} v {c}" if c < 2 else f"{x} pT {c - 2}"
                    if g == 0 and reader == maker:
                        S.wait_last(pe, maker, (made, read), i)
                    else:
                        if g == 0:
                            S.wait(pe, maker, made, i)
                        S.wait(pe, reader, read, i)
                    tt = TILES[n][1]
                    for b in range(4 * g, min(4 * g + 4, tt + 1)):
                        mm = pe.transpose(U[c % 2][:, (b % 4) * P:(b % 4 + 1) * P], pr[n % 2][:, b * P:(b + 1) * P], ident)
                    S.mark("pe", f"{x} turned {c}", mm)

            def values(i, x, n):
                hh, tt = TILES[n]
                if n >= 2 and groups_of(n)[0][0] % 2 == 0:
                    S.wait(pe, "dve", f"{x} out {n - 2}", i)
                elif n == 0:
                    S.wait(pe, "dve", f"{x} v 1", i)
                for c, g in groups_of(n):
                    S.wait(pe, ("act", "dve")[c % 2], f"{x} pT {c}", i)
                    for b in range(4 * g, min(4 * g + 4, tt + 1)):
                        mm = pe.matmul(G[0][:, (n % 2) * NB:(n % 2) * NB + HD], pT[c % 2][:, b % 4, :], av[x][:, b, HD * hh:HD * hh + HD],
                                       start=b == 0, stop=b == tt)
                    S.mark("pe", f"{x} values {c}", mm)

            S.enter("pe", "att")
            with pe.Fori(0, HEADS) as i:
                for x in "fs":
                    if x == "f":
                        job(i, x, 0)
                    job(i, x, 1)
                    job(i, x, 2)
                    scores(i, x, 0)
                    scores(i, x, 1)
                    for n in range(2):
                        S.wait(pe, "dve", f"{before(x, i)[0]} outT {n}", before(x, i)[1])
                        for b in range(4):
                            mm = pe.transpose(U[n][:, b * P:(b + 1) * P], avT[:, (4 * n + b) * P:(4 * n + b + 1) * P], ident)
                        S.mark("pe", f"{x} v turned {n}", mm)
                    for n in range(len(TILES)):
                        if n == len(TILES) - 1 and x == "f":
                            job(i, "s", 0)
                        turned(i, x, n)
                        if n + 2 < len(TILES):
                            scores(i, x, n + 2)
                        values(i, x, n)
                    S.wait(pe, "dve", f"{x} out {len(TILES) - 1}", i)
                    last = len(GROUPS) - 1
                    S.wait(pe, "act", f"{x} pT {last - last % 2}", i)
                    for n in range(2):
                        for b in range(4):
                            mm = pe.transpose(U[n][:, b * P:(b + 1) * P], ON[:, 4 * n + b, :], ident)
                        S.mark("pe", f"{x} outT {n}", mm)
            S.leave("pe", HEADS)
            S.wait(pe, *("dve", "f scores 15", HEADS - 1))
            S.wait(pe, *("act", "s not 15", HEADS - 1))
            sum_squares(pe, "heads", pr, 0, HEADS, S2)
            sum_squares(pe, "heads", pr, HEADS, KT, G[1])
            S.wait(pe, "dve", ("heads", "lo", KT - 1))
            S.wait(pe, "act", "heads root s")
            products_of_8("out2", J_OUT2, H)
            norm_pe("out2")

        @block.scalar
        def _(act):
            S.wait(act, "pe", "out summed")
            S.mark("act", "out root", act.activation(gs[:, 0, :], S2, ACT.Sqrt, scale=1.0 / D, bias=epsc))
            for k in range(KT):
                S.wait(act, "dve", ("x3 scaled", k))
                S.wait(act, "pe", *(("x3", "square summed", k - 2),) if k >= 2 else ("out summed",))
                S.mark("act", ("x3", "square", k), act.activation(bs[:, k % 2, :], X2[:, k, :], ACT.Square))
            norm_act("x3", H)
            act.wait_ge(gemm_done, J_FL + 1)
            S.wait(act, "dve", ("x3", "lo", KT - 1))
            g8, l8 = pr[0][0:S_HEADS, :], pr[1][0:S_HEADS, :]
            S.mark("act", "f logit", act.activation(g8, G[J_FL % 2][0:S_HEADS, :], ACT.Identity, bias=fbias[0:S_HEADS, :]))
            S.wait(act, "act", "f logit")
            S.mark("act", "f abs", act.activation(l8, g8, ACT.Abs))
            S.wait(act, "act", "f abs")
            S.mark("act", "f exp", act.activation(l8, l8, ACT.Exp, scale=-1.0))
            S.wait(act, "act", "f exp")
            S.mark("act", "f ln", act.activation(l8, l8, ACT.Ln, bias=1.0))
            S.wait(act, "dve", "forget sums")
            act.dma_start(nf_d, nots[0:S_HEADS, :]).then_inc(nf_stored, 16)
            act.wait_ge(nf_stored, 16)
            S.enter("act", "att")
            with act.Fori(0, HEADS) as i:
                def evac(x, m):
                    j = J_ATT + ATT_JOBS * i + (m + (3 if x == "s" else 0) + 1)
                    act.wait_ge(gemm_done, j)
                    if m < 2:
                        dst, more = qk[x][m], dict(scale=float(HD) ** -0.5 * (-1 if x == "f" else 1)) if m == 0 else {}
                    else:
                        dst, more = avT, {}
                    S.mark("act", f"{x} {('q', 'k', 'vT')[m]}", act.activation(dst, G[(1, 0, 1)[m]], ACT.Copy, **more))

                def chain(x, n):
                    hh, tt = TILES[n]
                    w = (tt + 1) * P
                    if x == "f":
                        S.wait(act, "dve", f"f scores {n}", i)
                        S.mark("act", f"f probs {n}", act.activation(pr[n % 2][:, 0:w], pr[n % 2][:, 0:w], ACT.Exp, scale=-1.0,
                                                                     bias=mn[:, n % 2, :], accum_out=rs[:, n % 2, :]))
                    else:
                        S.wait(act, "pe", f"s z {n}", i)
                        S.mark("act", f"s taken {n}", act.activation(pr[n % 2][:, 0:w], Z[n % 2][:, 0:w], ACT.Sigmoid))
                        if n:
                            S.wait(act, "dve", f"s left {n - 1}", i)
                        S.mark("act", f"s not {n}", act.activation(nots[:, 0:w], Z[n % 2][:, 0:w], ACT.Sigmoid, scale=-1.0))

                def copy_turned(x, n):
                    for c, g in groups_of(n):
                        if c % 2 == 0:
                            w = min(4, TILES[n][1] + 1 - 4 * g)
                            S.wait(act, "pe", f"{x} turned {c}", i)
                            S.mark("act", f"{x} pT {c}", act.activation(pT[0][:, 0:w, :], U[0][:, 0:w * P].rearrange("p (b t) -> p b t", t=P), ACT.Copy))

                for x in "fs":
                    if x == "f":
                        S.wait(act, "dve", "s probs 15", i - 1)
                        for hh in range(2):
                            act.dma_start(fsum[hh], nf_d[bass.ds(2 * i + hh, 1), :].to_broadcast([P, T])).then_inc(nf_landed, 16)
                        evac(x, 0)
                    evac(x, 1)
                    evac(x, 2)
                    if x == "s":
                        S.wait(act, "dve", "f scores 15", i)
                    chain(x, 0)
                    S.wait(act, "pe", f"{x} v turned 0", i)
                    S.mark("act", f"{x} v 0", act.activation(av[x][:, 0:4, :], U[0].rearrange("p (b t) -> p b t", t=P), ACT.Copy))
                    for n in range(len(TILES)):
                        if x == "f" and n == len(TILES) - 1:
                            copy_turned(x, n)
                            evac("s", 0)
                        else:
                            if n + 1 < len(TILES):
                                chain(x, n + 1)
                            copy_turned(x, n)
            S.leave("act", HEADS)
            for k in range(KT):
                S.wait(act, "dve", "s outT 1", HEADS - 1)
                if k >= 2:
                    S.wait(act, "pe", ("heads", "square summed", k - 2))
                S.mark("act", ("heads", "square", k), act.activation(pr[k % 2], OT[:, k, :], ACT.Square))
            S.wait(act, "pe", ("heads", "square summed", HEADS - 1))
            S.mark("act", "heads root f", act.activation(nots, S2, ACT.Sqrt, scale=2.0 / D, bias=epsc))
            S.wait(act, "pe", ("heads", "square summed", KT - 1))
            S.mark("act", "heads root s", act.activation(left[:, 0:T], G[1], ACT.Sqrt, scale=2.0 / D, bias=epsc))
            for k in range(KT):
                hi_part(k, "heads", H, pr)
            residual_act("out2", [("dve", ("heads", "lo", KT - 1))])
            norm_act("out2", A)

        @block.vector
        def _(v):
            def do(name, ins):
                S.mark("dve", name, ins)
                return name

            S.wait(v, "act", "out root")
            do("out rstd", v.reciprocal(gs[:, 0, :], gs[:, 0, :]))
            S.wait(v, "dve", "out rstd")
            for k in range(KT):
                do(("x3 scaled", k), v.scalar_tensor_tensor(X2[:, k, :], X2[:, k, :], col("f1", k), gs[:, 0, :], ALU.mult, ALU.mult))
            norm_dve("x3", "ag", H)
            g8, l8, F8 = pr[0][0:S_HEADS, :], pr[1][0:S_HEADS, :], nots[0:S_HEADS, :]
            S.wait(v, "act", "f ln")
            do("forget logs", v.scalar_tensor_tensor(g8, g8, 0.0, l8, ALU.min, ALU.subtract))
            S.wait(v, "dve", "forget logs")
            do("forget sums", v.tensor_tensor_scan(F8, g8, g8, 0.0, ALU.add, ALU.bypass))
            do("left all", v.memset(left[:, T:T + 1], 1.0))
            S.enter("dve", "att")
            with v.Fori(0, HEADS) as i:
                def me(name):
                    S.wait(v, "dve", name, i)

                def chain(x, n):
                    hh, tt = TILES[n]
                    w = (tt + 1) * P
                    p = pr[n % 2][:, 0:w]
                    if x == "f":
                        S.wait(v, "pe", f"f z {n}", i)
                        if n == 0:
                            v.wait_ge(nf_landed, 32 * i + 32)
                        settle(v, i)
                        do(f"f scores {n}", v.tensor_tensor_reduce(out=p, in0=fsum[hh][:, 0:w], in1=Z[n % 2][:, 0:w], scale=1.0, scalar=1e30,
                                                                   op0=ALU.add, op1=ALU.min, accum_out=mn[:, n % 2, :]))
                    else:
                        S.wait(v, "act", f"s not {n}", i)
                        if n:
                            me(f"s probs {n - 1}")
                        do(f"s left {n}", v.tensor_tensor_scan(left[:, T - w:T][:, ::-1], nots[:, 0:w][:, ::-1], nots[:, 0:w], 1.0, ALU.mult, ALU.bypass))
                        me(f"s left {n}")
                        do(f"s probs {n}", v.tensor_tensor(p, p, left[:, T - w + 1:T + 1], ALU.mult))

                def copy_turned(x, n):
                    for c, g in groups_of(n):
                        if c % 2 == 1:
                            w = min(4, TILES[n][1] + 1 - 4 * g)
                            S.wait(v, "pe", f"{x} turned {c}", i)
                            do(f"{x} pT {c}", v.tensor_copy(pT[1][:, 0:w, :], U[1][:, 0:w * P].rearrange("p (b t) -> p b t", t=P)))

                def out_of(x, n):
                    hh, tt = TILES[n]
                    src, dst = G[0][:, (n % 2) * NB:(n % 2) * NB + HD], ON[:, tt, HD * hh:HD * hh + HD]
                    if x == "f":
                        S.wait(v, "act", f"f probs {n}", i)
                        do(f"f sums {n}", v.reciprocal(rs[:, n % 2, :], rs[:, n % 2, :]))
                        me(f"f sums {n}")
                    S.wait(v, "pe", f"{x} values {groups_of(n)[-1][0]}", i)
                    do(f"{x} out {n}", v.tensor_scalar(dst, src, rs[:, n % 2, :], None, ALU.mult) if x == "f" else v.tensor_copy(dst, src))

                for x in "fs":
                    chain(x, 0)
                    if x == "f":
                        chain(x, 1)
                    S.wait(v, "pe", f"{x} v turned 1", i)
                    do(f"{x} v 1", v.tensor_copy(av[x][:, 4:8, :], U[1].rearrange("p (b t) -> p b t", t=P)))
                    for n in range(len(TILES)):
                        if x == "s" and n + 1 < len(TILES):
                            chain(x, n + 1)
                        copy_turned(x, n)
                        if n:
                            out_of(x, n - 1)
                        if x == "f" and n >= 1 and n + 1 < len(TILES):
                            chain(x, n + 1)
                    out_of(x, len(TILES) - 1)
                    for n in range(2):
                        S.wait(v, "pe", f"{x} outT {n}", i)
                        do(f"{x} outT {n}", v.tensor_copy(OT[:, bass.ds(i + 4 * "fs".index(x), 1), n * NB:(n + 1) * NB].rearrange("p k t -> p (k t)"), U[n]))
            S.leave("dve", HEADS)
            for x, r in (("f", nots), ("s", left[:, 0:T])):
                S.wait(v, "act", f"heads root {x}")
                do(f"heads rstd {x}", v.reciprocal(r, r))
            S.wait(v, "dve", "heads rstd s")
            for k in range(KT):
                normed(k, OT, col("fg", k), nots if k < HEADS else left[:, 0:T], "heads", H, pr)
            residual_dve("out2", J_OUT2)
            norm_dve("out2", "fn", A)

    w_up, w_down = a["w_up_2"][0], a["w_down_2"][0]

    def ffn_jobs():
        j = J_FFN
        for g, (f0, nf) in enumerate(FFN_GROUPS):
            yield g, f0, nf, j, j + 2 * nf
            j += 2 * nf + KT

    with nc.Block() as block:
        @block.sync
        def _(sp):
            for g, f0, nf, up, down in ffn_jobs():
                with sp.Fori(0, nf) as f:
                    for m in range(2):
                        load_w(up + 2 * f + m, (up + m) % 2, dslab(w_up, f * P + (f0 * P + m * DFF)))
                loads_of_8(down, w_down, nf, f0 * P)
            for t in range(TT):
                for h in range(2):
                    S.wait(sp, ("act", "dve")[h], f"staged {t}")
                sp.dma_start(out[0, t * P:(t + 1) * P, :], (gs, bs)[t % 2][:, 1, :]).then_inc(out_stored[t % 2], 16)
            for s in range(2):
                sp.wait_ge(out_stored[s], 16 * TT // 2)

        @block.gpsimd
        def _(g_):
            for g, f0, nf, up, down in ffn_jobs():
                splits_of(up, pairs=nf)
                splits_of(down, kt=nf)

        @block.tensor
        def _(pe):
            S.wait(pe, "dve", ("out2", "lo", KT - 1))
            S.wait(pe, "dve", "out2 job 1", KT // 2 - 1)
            for g, f0, nf, up, down in ffn_jobs():
                if g:
                    for m in range(2):
                        S.wait(pe, "dve", f"down{g - 1} job {m}", KT // 2 - 1)
                S.enter("pe", f"up{g}")
                with pe.Fori(0, nf) as f:
                    for m in range(2):
                        gemm(up + 2 * f + m, (up + m) % 2, A, ("dve", f"up{g} conv {m}", f - 1))
                S.leave("pe", nf)
                for m in range(2):
                    S.wait(pe, "dve", f"up{g} conv {m}", nf - 1)
                S.wait(pe, "dve", f"up{g} lo", nf - 1)
                products_of_8(f"down{g}", down, H, nf)
            norm_pe("down2")
            for t in range(TT):
                for h in range(2):
                    if t:
                        S.wait(pe, ("act", "dve")[h], f"staged {t - 1}")
                    for b in range(4):
                        k = 4 * h + b
                        if t == 0:
                            S.wait(pe, "dve", ("x4 scaled", k))
                        mm = pe.transpose(U[h][:, b * P:(b + 1) * P], X2[:, k, t * P:(t + 1) * P], ident)
                    S.mark("pe", f"out turned {t} {h}", mm)

        @block.scalar
        def _(act):
            for g, f0, nf, up, down in ffn_jobs():
                if g:
                    S.wait(act, "dve", f"down{g - 1} job 1", KT // 2 - 1)
                S.enter("act", f"up{g}")
                with act.Fori(0, nf) as f:
                    for m in range(2):
                        act.wait_ge(gemm_done, up + 2 * f + m + 1)
                        if m == 0:
                            S.wait(act, "dve", f"up{g} act", f - 1)
                        settle(act, f)
                        S.mark("act", f"up{g} tap {m}", act.activation(gs[:, m, :], G[(up + m) % 2], ACT.Identity, bias=conv_col(0, f + (f0 + m * FT)), scale=conv_col(3, f + (f0 + m * FT))))
                        if m == 0:
                            S.wait(act, "dve", f"up{g} conv 0", f)
                            S.mark("act", f"up{g} silu", act.activation(bs[:, 0, :], gs[:, 0, :], ACT.Silu))
                    S.wait(act, "dve", f"up{g} act", f)
                    settle(act, f)
                    S.mark("act", f"up{g} hi", act.activation(tile2(H[0], f), bs[:, 1, :], ACT.Copy))
                S.leave("act", nf)
                residual_act(f"down{g}", [], squares=g == len(FFN_GROUPS) - 1)
            S.wait(act, "pe", "down2 summed")
            S.mark("act", "down2 root", act.activation(gs[:, 0, :], S2, ACT.Sqrt, scale=1.0 / D, bias=epsc))
            for t in range(TT):
                S.wait(act, "pe", f"out turned {t} 0")
                if t >= 2:
                    act.wait_ge(out_stored[t % 2], 16 * (t // 2))
                S.mark("act", f"staged {t}", act.activation((gs, bs)[t % 2][:, 1, 0:NB], U[0], ACT.Copy))

        @block.vector
        def _(v):
            def do(name, ins):
                S.mark("dve", name, ins)
                return name
            for g, f0, nf, up, down in ffn_jobs():
                S.enter("dve", f"up{g}")
                with v.Fori(0, nf) as f:
                    for m in range(2):
                        k = f + (f0 + m * FT)
                        y, u = gs[:, m, :], G[(up + m) % 2]
                        S.wait(v, "act", f"up{g} tap {m}", f)
                        do(f"up{g} near {m}", v.scalar_tensor_tensor(y[:, 1:T], u[:, 0:T - 1], conv_col(2, k), y[:, 1:T], ALU.mult, ALU.add))
                        S.wait(v, "dve", f"up{g} near {m}", f)
                        do(f"up{g} conv {m}", v.scalar_tensor_tensor(y[:, 2:T], u[:, 0:T - 2], conv_col(1, k), y[:, 2:T], ALU.mult, ALU.add))
                    S.wait(v, "act", f"up{g} silu", f)
                    S.wait(v, "dve", f"up{g} conv 1", f)
                    do(f"up{g} act", v.tensor_tensor(bs[:, 1, :], bs[:, 0, :], gs[:, 1, :], ALU.mult))
                    S.wait(v, "act", f"up{g} hi", f)
                    do(f"up{g} lo", v.tensor_tensor(tile2(H[1], f), bs[:, 1, :], tile2(H[0], f).bitcast(F32), ALU.subtract))
                S.leave("dve", nf)
                residual_dve(f"down{g}", down, squares=g == len(FFN_GROUPS) - 1)
            S.wait(v, "act", "down2 root")
            do("down2 rstd", v.reciprocal(gs[:, 0, :], gs[:, 0, :]))
            S.wait(v, "dve", "down2 rstd")
            for k in range(KT):
                do(("x4 scaled", k), v.scalar_tensor_tensor(X2[:, k, :], X2[:, k, :], col("fin", k), gs[:, 0, :], ALU.mult, ALU.mult))
            for t in range(TT):
                S.wait(v, "pe", f"out turned {t} 1")
                if t >= 2:
                    v.wait_ge(out_stored[t % 2], 16 * (t // 2))
                do(f"staged {t}", v.tensor_copy((gs, bs)[t % 2][:, 1, NB:D], U[1]))

    with nc.Block() as block:
        @block.scalar
        def _(act):
            for engine in ("act", "dve"):
                act.wait_ge(S.settled[engine], S.n[engine, "settled"])
    return S.at


INPUTS = ("x", "c", "ctx", "c_ctx", "w_mod", "b_mod", "norm_g", "w_in", "w_gate_up_f", "b_gate_f", "w_gate_up_b",
          "b_gate_b", "gla_norm_g", "w_pool", "pool_scale", "w_branch_a", "w_branch_b", "w_out", "final_norm_g", "attn_norm_g_2",
          "w_in_2", "forget_bias_2", "fox_out_g_2", "sb_out_g_2", "w_out_2", "ffn_norm_g_2", "w_up_2", "conv_w_2",
          "conv_b_2", "w_down_2", "final_norm_g_2")


def constants():
    t = np.arange(T)
    i = np.arange(P)
    j = i[:, None]
    levels = np.stack([((j // (2 * s)) == (i // (2 * s))) & ((j % (2 * s) < s) != (i % (2 * s) < s)) for s in LEVELS], 1)
    nf = DK // 4
    freqs = np.power(np.float32(10000.0), -np.arange(nf, dtype=np.float32) / nf).astype(np.float32)
    pos = np.where(i[:, None] < DK // 2, (t // GRID_W)[None], (t % GRID_W)[None]).astype(np.float32)
    angle = (pos * freqs[i % nf][:, None]).astype(np.float32).astype(np.float64)
    sign = np.where(i % (2 * nf) < nf, -1.0, 1.0)[:, None]
    half = np.array([1, 2, 4, 8])[:, None]
    count = np.clip(t + half, 0, T) - np.clip(t - half, 0, T)
    inv = np.broadcast_to((1.0 / count)[:, None, :], (4, P, T))
    mask = np.where(i[None, :] > j, np.float32(1e30), 0.0)
    strict = np.where(i[None, :] >= j, np.float32(-1e30), 0.0)
    return {
        "identity": np.eye(P, dtype=np.float32),
        "causal": np.stack([mask, strict], 1).astype(np.float32),
        "levels": levels.astype(np.float32),
        "cos": np.cos(angle).astype(np.float32),
        "sin": (np.sin(angle) * sign).astype(np.float32),
        "inv_count": np.ascontiguousarray(inv).astype(np.float32),
    }


def kernel(**inputs):
    import concourse.bacc as bacc
    from concourse.bass_utils import run_bass_kernel_spmd as run

    arrays = {n: np.ascontiguousarray(value) for n, value in [(n, inputs[n]) for n in INPUTS] + list(constants().items())}

    def write_down(known):
        nc = bacc.Bacc("TRN2", target_bir_lowering=False, num_devices=1)
        aps = {n: nc.dram_tensor(n, value.shape, mybir.dt.from_np(value.dtype), kind="ExternalInput").ap() for n, value in arrays.items()}
        out = nc.dram_tensor("out", (1, T, D), F32, kind="ExternalOutput").ap()
        return nc, program(nc, aps, out, known)
    _, steps = write_down({})
    nc, _ = write_down(steps)
    return run(nc, [arrays], core_ids=[0]).results[0]["out"]
```

```python
import numpy as np
import concourse.bass as bass
from concourse import mybir

F32 = mybir.dt.float32
F32R = mybir.dt.float32r
BF16 = mybir.dt.bfloat16
U8 = mybir.dt.uint8
ALU = mybir.AluOpType
ACT = mybir.ActivationFunctionType
AX = mybir.AxisListType

P = 128
D = 1024
KT = D // P
T = 1024
TT = T // P
TC = 256
NB = 512
EPS = 1e-6
HEADS, DK, DV = 4, 128, 256
RANK = 16
GATE_NORM = 16.0
GRID_W = 64
CH = 128
POOL_WINDOWS = (2, 4, 8, 16)
LEVELS = (64, 32, 16, 8, 4, 2, 1)
C_Q, C_K, C_V, C_ZA = 0, 512, 1024, 2048
C_LR, C_UB, C_ZB, C_GA, C_GB = 3072, 3104, 4128, 5152, 6176
HD = 64
S_HEADS = 8
S_FQ, S_FK, S_FV, S_FL, S_SQ, S_SK, S_SV = 0, 512, 1024, 1536, 1544, 2056, 2568
DFF = 2816
FT = DFF // P

R0 = dict(c=0, cc=8, ng=16, bm=24, bgf=48, bgb=52, gg=56, ps=58, ag=66, fg=74, sg=78, fn=82, fin=90, f1=98)
R0_ROWS = 106
R1_ROWS = 88
R2_ROWS = 88

J_CTX = 0
J_LR = 13
J_GLA = 14
GLA_JOBS = 10
J_POOL = J_GLA + HEADS * GLA_JOBS
POOL_JOBS = 6
J_BRA = J_POOL + 4 * POOL_JOBS
J_BRB = J_BRA + KT
J_OUT = J_BRB + KT
J_FL = J_OUT + KT
J_ATT = J_FL + 1
ATT_JOBS = 6
J_OUT2 = J_ATT + 4 * ATT_JOBS
J_FFN = J_OUT2 + KT
FFN_GROUPS = ((0, 8), (8, 8), (16, 6))



class Steps:

    def __init__(self, known):
        self.known, self.at, self.n, self.loop, self.sems = known, {}, {}, {}, {}

    def start(self, nc, names):
        self.sems = {n: nc.alloc_semaphore(f"{n}_steps") for n in names}
        self.n = dict.fromkeys(names, 0) | {(n, "settled"): 0 for n in names}
        self.settled = {n: nc.alloc_semaphore(f"{n}_waits_taken") for n in ("act", "dve")}

    def mark(self, engine, name, ins):
        ins.then_inc(self.sems[engine], 1)
        self.n[engine] += 1
        key = (engine, name)
        assert key not in self.at, key
        self.at[key] = (self.n[engine], self.loop.get(engine))
        return ins

    def value(self, engine, name, turn=None):
        table = self.at if (engine, name) in self.at else self.known
        if (engine, name) not in table:
            assert not self.known, (engine, name)
            return 1
        n, loop = table[engine, name]
        if loop is None:
            return n
        before, per = self.known.get(loop, (0, 1))
        return before + (n - before) + turn * per

    def wait(self, eng, engine, name, turn=None):
        eng.wait_ge(self.sems[engine], self.value(engine, name, turn))

    def wait_last(self, eng, engine, names, turn=None):
        self.wait(eng, engine, max(names, key=lambda name: self.value(engine, name, 0)), turn)

    def settle(self, engine, eng):
        eng.sem_inc(self.settled[engine], 1)
        self.n[engine, "settled"] += 1

    def enter(self, engine, name):
        self.loop[engine] = ("loop", engine, name)
        self.before = self.n[engine]
        self.before_settled = self.n[engine, "settled"]

    def leave(self, engine, turns):
        per = self.n[engine] - self.before
        self.at[self.loop[engine]] = (self.before, per)
        self.n[engine] += (turns - 1) * per
        self.n[engine, "settled"] += (turns - 1) * (self.n[engine, "settled"] - self.before_settled)
        self.loop[engine] = None


def program(nc, a, out, known):
    base = (nc.sbuf_base + 31) // 32 * 32
    KB = 1024
    END = 229344 - base

    def sb(name, off, shape, dt=F32):
        return nc.alloc_sbuf_tensor_at(name, shape, dt, offset=base + off)[tuple(slice(None) for _ in shape)]

    H = [sb("H_hi", 0, [P, KT, T], F32R), sb("H_lo", 32 * KB, [P, KT, T], F32R)]
    w_raw = sb("w_raw", 64 * KB, [P, 2, KT, P])
    w_hi = sb("w_hi", 72 * KB, [P, 2, KT, P], F32R)
    w_lo = sb("w_lo", 80 * KB, [P, 2, KT, P], F32R)
    C0 = 88 * KB
    par = sb("par", C0, [P, R0_ROWS + R1_ROWS + R2_ROWS])
    ident = sb("ident", C0 + 1152, [P, P])
    ones = sb("ones", C0 + 1664, [P, P])
    lvl = sb("lvl", C0 + 2176, [P, len(LEVELS), P], U8)
    mod = sb("mod", C0 + 3072, [P, 24, 2])
    gsc = sb("gsc", C0 + 3264, [P, KT, 2])
    identb = sb("identb", C0 + 3328, [P, P], BF16)
    maskb = sb("maskb", C0 + 3584, [P, 2, P], BF16)
    fbias = sb("fbias", C0 + 4096, [P, 1])
    epsc = sb("epsc", C0 + 4128, [P, 1])
    gains = sb("gains", C0 + 4160, [P, KT])
    W0 = C0 + 4192

    def col(name, i=0):
        return par[:, R0[name] + i:R0[name] + i + 1]

    def conv_col(which, i):
        o = R0_ROWS + which * (2 * FT) + i
        return par[:, bass.ds(o, 1)]

    G = [nc.alloc_psum_tensor(f"G{s}", [P, 2 * NB], F32)[:, :] for s in range(2)]
    S2 = nc.alloc_psum_tensor("S2", [P, 2 * NB], F32)[:, :]
    U2 = nc.alloc_psum_tensor("U2", [P, 2 * NB], F32)[:, :]
    U = [U2[:, 0:NB], U2[:, NB:2 * NB]]

    def scratch(name, shape):
        return nc.dram_tensor(name, shape, F32, kind="Internal").ap()

    xT_d, s0_d = scratch("xT_d", (KT, P, T)), scratch("s0_d", (HEADS, 2, P, DV))
    a_d, b_d = scratch("a_d", (KT, P, T)), scratch("b_d", (KT, P, T))
    sga_d, sgb_d = scratch("sga_d", (KT, P, T)), scratch("sgb_d", (KT, P, T))
    o_d = scratch("o_d", (KT, P, T))

    sem = nc.alloc_semaphore
    w_landed = [sem("w_landed0"), sem("w_landed1")]
    w_hi_made, w_ready, gemm_done = sem("w_hi_made"), sem("w_ready"), sem("gemm_done")
    S = Steps(known)
    S.start(nc, ("pe", "act", "dve", "pool"))
    engines = {"pe": nc.tensor, "act": nc.scalar, "dve": nc.vector, "pool": nc.gpsimd}

    def passes(slot, mov, tiles, dst, n_cols=T):
        hi, lo = mov
        halves = [(n, min(NB, n_cols - n * NB)) for n in range((n_cols + NB - 1) // NB)]
        for k in tiles:
            for w, m, first, last in ((w_hi, hi, k == tiles[0], False), (w_hi, lo, False, False),
                                      (w_lo, hi, False, k == tiles[-1])):
                for n, c in halves:
                    mm = nc.tensor.matmul(dst[:, n * NB:n * NB + c], w[:, slot, k, :], m[:, k, n * NB:n * NB + c],
                                          start=first, stop=last)
        return mm

    def gemm(j, slot, mov, freed=None, n_cols=T, kt=KT, pair=None):
        pe = nc.tensor
        pe.wait_ge(w_ready, j + 1)
        if freed:
            S.wait(pe, *freed)
        passes(slot, mov, range(kt), G[slot] if pair is None else pair, n_cols).then_inc(gemm_done, 1)

    def load_w(j, slot, src, kt=KT, first=False):
        if not first:
            nc.sync.wait_ge(w_ready, j - 1)
        nc.sync.dma_start(w_raw[:, slot, 0:kt, :], src).then_inc(w_landed[slot], 16)

    def split_hi(eng, j, slot, landed, kt=KT, first=False):
        eng.wait_ge(w_landed[slot], 16 * landed)
        if not first:
            eng.wait_ge(gemm_done, j - 1)
        dst, src = w_hi[:, slot, 0:kt, :], w_raw[:, slot, 0:kt, :]
        i = eng.activation(dst, src, ACT.Copy) if eng is nc.scalar else \
            eng.tensor_tensor(dst, src, ones.unsqueeze(1).to_broadcast([P, kt, P]), ALU.mult)
        i.then_inc(w_hi_made, 1)

    def split_lo(j, slot, kt=KT):
        nc.gpsimd.wait_ge(w_hi_made, j + 1)
        nc.gpsimd.tensor_tensor(w_lo[:, slot, 0:kt, :], w_raw[:, slot, 0:kt, :],
                                w_hi[:, slot, 0:kt, :].bitcast(F32), ALU.subtract).then_inc(w_ready, 1)

    def split(j, slot, landed, kt=KT):
        split_hi(nc.gpsimd, j, slot, landed, kt)
        split_lo(j, slot, kt)

    def slab(w, c0, kt=KT, r0=0):
        return w[r0:r0 + kt * P, c0:c0 + P].rearrange("(k p) c -> p k c", p=P)

    def settle(eng, turn=None):
        S.settle({nc.scalar: "act", nc.vector: "dve"}[eng], eng)

    def barrier(engine, n):
        eng = engines[engine]
        S.mark(engine, f"phase {n} ended", eng.drain())
        for other in ("pe", "act", "dve"):
            S.wait(eng, other, f"phase {n} ended")

    def after_phase(eng, n):
        for other in ("pe", "act", "dve"):
            S.wait(eng, other, f"phase {n} ended")

    w_in, w_mod = a["w_in"][0], a["w_mod"][0]

    o = W0
    def take(name, shape, dt=F32, size=None):
        nonlocal o
        at = o
        n = int(np.prod(shape[1:])) * {F32: 4, F32R: 4, BF16: 2, U8: 1}[dt]
        o = (o + n + 31) // 32 * 32
        assert o <= END, (name, o, END)
        return sb(name, at, shape, dt)

    xT = take("xT", [P, KT, T])
    wm = take("wm", [P, 2, KT, NB])
    cT = take("cT", [P, KT, TC])
    hc = [take("hc_hi", [P, KT, TC], F32R), take("hc_lo", [P, KT, TC], F32R)]
    x_in = take("x_in", [P, 2, D])
    sq = take("sq", [P, 2, T])
    rb = take("rb", [P, T + TC])
    prow = take("prow", [P, 3, P])
    silc = take("silc", [P, 16])
    lvl_in = take("levels_in", [P, len(LEVELS), P])
    mask_in = take("masks_in", [P, 2, P])
    o = W0
    lrc = take("lrc", [2 * RANK, TC])
    wup = take("wup", [2 * RANK, 2, HEADS * DK])
    smask = take("smask", [P, T], BF16)
    kc = take("kc", [P, T])
    vcT = take("vcT", [P, 2, 2, TC])
    vc = take("vc", [P, 2, HEADS * DV])
    c_g = [take("c_gf", [P, T + 8]), take("c_gb", [P, T + 8])]
    c_l = [take("c_lf", [P, T]), take("c_lb", [P, T])]
    c_F = [take("c_F", [P, T]), take("c_X", [P, T])]
    c_k = [take("c_kf", [P, T]), take("c_kb", [P, T])]
    c_kn = [take("c_kfT", [P, 8, P]), take("c_kbT", [P, 8, P])]
    c_t = take("c_t", [P, 2, 8])
    assert o <= W0 + 72 * KB, o
    o = W0 + 88 * KB
    c_S = take("c_S", [P, HEADS, 2, DV])

    par_landed, const_landed = sem("params_landed"), sem("constants_landed")
    x_landed, wm_landed = [sem("x_landed0"), sem("x_landed1")], [sem("wm_landed0"), sem("wm_landed1")]
    xT_stored, s0_stored, cpar_landed = sem("xT_stored"), sem("s0_stored"), sem("ctx_params_landed")

    def ctx_col(j):
        return C_LR if j == 0 else C_K + (j - 1) * P if j < 5 else C_V + (j - 5) * P

    def rows(v):
        return v.rearrange("(r c) -> r c", c=P)

    def broadcast(ap, n):
        return ap.to_broadcast([ap.shape[0], ap.shape[1], n])

    def chunks(v, n=8):
        return v.rearrange("p (c t) -> p c t", c=n)

    def chunk_mask(dst, name):
        g = nc.gpsimd
        S.mark("pool", f"{name} ones", g.memset(dst, 1.0))
        S.wait(g, "pool", f"{name} ones")
        S.mark("pool", name, g.memset(chunks(dst)[:, :, 0:1], 0.0))

    with nc.Block() as block:
        @block.sync
        def _(sp):
            vectors = (("c", a["c"][0]), ("cc", a["c_ctx"]), ("ng", a["norm_g"][0]), ("bm", a["b_mod"][0]),
                       ("bgf", a["b_gate_f"][0]), ("bgb", a["b_gate_b"][0]), ("gg", a["gla_norm_g"][0]),
                       ("ps", a["pool_scale"][0]), ("ag", a["attn_norm_g_2"][0]), ("fg", a["fox_out_g_2"][0]),
                       ("sg", a["sb_out_g_2"][0]), ("fn", a["ffn_norm_g_2"][0]), ("fin", a["final_norm_g_2"]), ("f1", a["final_norm_g"]))
            for name, src in vectors:
                sp.dma_start(prow[R0[name]:R0[name] + src.shape[0] // P, 0, :], rows(src)).then_inc(par_landed, 16)
            cw = a["conv_w_2"][0]
            for row, g, src in ((0, 1, a["conv_b_2"][0]), (44, 1, cw[0]), (0, 2, cw[1]), (44, 2, cw[2])):
                sp.dma_start(prow[row:row + 44, g, :], rows(src)).then_inc(par_landed, 16)
            sp.dma_start(ident, a["identity"]).then_inc(par_landed, 16)
            tiles = [a["ctx"][0, t * P:(t + 1) * P, :] for t in range(2)] + \
                    [a["x"][0, t * P:(t + 1) * P, :] for t in range(TT)]

            def load_tile(t):
                if t >= 2:
                    S.wait(sp, "pe", ("turned", t - 2, 1))
                sp.dma_start(x_in[:, t % 2, :], tiles[t]).then_inc(x_landed[t % 2], 16)

            def load_mod(q):
                if q >= 2:
                    S.wait(sp, "pe", ("modulation", q - 2))
                sp.dma_start(wm[:, q % 2, :, :], w_mod[:, q * NB:(q + 1) * NB].rearrange("(k p) c -> p k c", p=P))\
                    .then_inc(wm_landed[q % 2], 16)
            load_tile(0)
            load_tile(1)
            load_mod(0)
            for t in range(2, 6):
                load_tile(t)
            load_mod(1)
            for t in range(6, 10):
                load_tile(t)
            load_mod(2)
            load_mod(3)
            for j in range(2):
                load_w(J_CTX + j, j, slab(w_in, ctx_col(j)), first=True)
            load_mod(4)
            load_mod(5)
            sp.dma_start(lvl_in, a["levels"]).then_inc(const_landed, 16)
            sp.dma_start(mask_in, a["causal"]).then_inc(const_landed, 16)
            sp.dma_start(fbias[0:S_HEADS, :], a["forget_bias_2"].rearrange("a h -> h a")).then_inc(const_landed, 16)
            after_phase(sp, 1)
            sp.wait_ge(const_landed, 48)
            S.wait(sp, "pool", "gate weights cleared")
            sp.dma_start(wup[0:RANK, 0, :], a["w_gate_up_f"][0]).then_inc(cpar_landed, 16)
            sp.dma_start(wup[RANK:2 * RANK, 1, :], a["w_gate_up_b"][0]).then_inc(cpar_landed, 16)
            for j in range(2, J_LR):
                load_w(j, j % 2, slab(w_in, ctx_col(j)))

        @block.gpsimd
        def _(g):
            S.mark("pool", "ones made", g.memset(ones, 1.0))
            S.mark("pool", "eps made", g.memset(epsc, EPS))
            split_lo(0, 0)
            split_lo(1, 1)
            after_phase(g, 1)
            S.mark("pool", "gate weights cleared", g.memset(wup, 0.0))
            chunk_mask(smask, "chunk mask")
            for j in range(2, J_LR):
                split_lo(j, j % 2)

        @block.tensor
        def _(pe):
            pe.wait_ge(par_landed, 16 * 19)
            for g, (n, at) in enumerate(((R0_ROWS, 0), (R1_ROWS, R0_ROWS), (R2_ROWS, R0_ROWS + R1_ROWS))):
                mm = pe.transpose(G[1][:, at:at + n], prow[0:n, g, :], ident[0:n, 0:n])
            S.mark("pe", "parameters turned", mm)

            def turn(t):
                pe.wait_ge(x_landed[t % 2], 16 * (t // 2 + 1))
                for h in range(2):
                    if t >= 1:
                        S.wait(pe, "act" if h == 0 else "dve", ("turned copied", t - 1))
                    for i in range(4):
                        mm = pe.transpose(U[h][:, i * P:(i + 1) * P], x_in[:, t % 2, (4 * h + i) * P:(4 * h + i + 1) * P], ident)
                    S.mark("pe", ("turned", t, h), mm)

            def modulation(q):
                pe.wait_ge(wm_landed[q % 2], 16 * (q // 2 + 1))
                if q == 0:
                    S.wait(pe, "act", "silu made")
                for m in range(4):
                    c = (NB if q < 4 else 0) + (4 * q + m) * 2
                    for k in range(KT):
                        mm = pe.matmul(G[1][:, c:c + 2], wm[:, q % 2, k, m * P:(m + 1) * P], silc[:, k:16:8],
                                       start=k == 0, stop=k == KT - 1)
                S.mark("pe", ("modulation", q), mm)
            turn(0)
            turn(1)
            modulation(0)
            for t in range(2, 6):
                turn(t)
            modulation(1)
            for t in range(6, 10):
                turn(t)
            S.wait(pe, "pool", "ones made")
            S.wait(pe, "act", ("turned copied", 9))
            for k in range(KT):
                S.wait(pe, "act", ("ctx squares", k // 4))
                mm = pe.matmul(U[0][:, 0:TC], ones, sq[:, k // 4, (k % 4) * TC:(k % 4 + 1) * TC], start=k == 0, stop=k == KT - 1)
                if k % 4 == 3:
                    S.mark("pe", ("ctx squares summed", k // 4), mm)
            for k in range(KT):
                S.wait(pe, "act", ("squares", k))
                for n in range(2):
                    mm = pe.matmul(S2[:, n * NB:(n + 1) * NB], ones, sq[:, k % 2, n * NB:(n + 1) * NB], start=k == 0, stop=k == KT - 1)
                S.mark("pe", ("squares summed", k), mm)
            modulation(2)
            modulation(3)
            for j in range(2):
                if j == 0:
                    S.wait(pe, "dve", ("scaled", "c", KT - 1))
                    gemm(0, 0, hc, n_cols=TC)
            modulation(4)
            modulation(5)
            barrier("pe", 1)
            gemm(1, 1, hc, n_cols=TC)
            S.wait(pe, "act", ("ctx job", 0))
            pe.wait_ge(cpar_landed, 32)
            for d in range(2):
                for hh in range(2):
                    if d:
                        S.wait(pe, "act", ("ctx gates", 0, hh))
                    for h in range(2):
                        w = wup[:, d, (2 * hh + h) * DK:(2 * hh + h + 1) * DK]
                        mm = pe.matmul(U[hh][:, h * TC:(h + 1) * TC], w, lrc, start=True, stop=True)
                    S.mark("pe", ("ctx gates", d, hh), mm)

            def turn_values(i):
                S.wait(pe, "act", ("ctx job", 6 + 2 * i))
                S.wait(pe, *(("act", ("ctx gates", 1, i)) if i < 2 else ("dve", ("vc", i - 2))))
                for c in range(2):
                    for m in range(2):
                        mm = pe.transpose(U[i % 2][:, (2 * c + m) * P:(2 * c + m + 1) * P], vcT[:, i % 2, m, c * P:(c + 1) * P], ident)
                S.mark("pe", ("vc turned", i), mm)
            for j in range(2, J_LR):
                gemm(j, j % 2, hc, ("act", ("ctx job", j - 2)), n_cols=TC)
                if j in (8, 10, 12):
                    turn_values((j - 8) // 2)
            turn_values(3)
            for d in range(2):
                S.wait(pe, "dve", ("ctx keys", d))
                for h in range(2):
                    S.wait(pe, *(("dve", ("vc", 2 + h)) if d == 0 else ("act", ("ctx keys turned", 0, h))))
                    for i in range(4):
                        mm = pe.transpose(U[h][:, i * P:(i + 1) * P], c_k[d][:, (4 * h + i) * P:(4 * h + i + 1) * P], ident)
                    S.mark("pe", ("ctx keys turned", d, h), mm)
            for d in range(2):
                for h in range(HEADS):
                    S.wait(pe, "act", ("ctx keys turned", d, h // 2))
                    if d == 0 and h < 2:
                        S.wait(pe, "act", ("ctx keys turned", 1, h))
                    else:
                        S.wait(pe, "dve", ("ctx state", d - (h < 2), (h - 2) % 4))
                    for c in range(2):
                        mm = pe.matmul(U[h % 2][:, c * DV:(c + 1) * DV], c_kn[d][:, 2 * h + c, :], vc[:, c, h * DV:(h + 1) * DV], start=True, stop=True)
                    S.mark("pe", ("ctx updates", d, h), mm)
            barrier("pe", 2)

        @block.scalar
        def _(act):
            S.wait(act, "pe", "parameters turned")
            S.mark("act", "parameters", act.activation(par, G[1][:, 0:R0_ROWS + R1_ROWS + R2_ROWS], ACT.Copy))
            S.wait(act, "act", "parameters")
            S.mark("act", "silu made", act.activation(silc, par[:, 0:16], ACT.Silu))
            for t in range(10):
                S.wait(act, "pe", ("turned", t, 0))
                dst = cT[:, 0:4, t * P:(t + 1) * P] if t < 2 else xT[:, 0:4, (t - 2) * P:(t - 1) * P]
                S.mark("act", ("turned copied", t), act.activation(dst, U[0].rearrange("p (i t) -> p i t", i=4), ACT.Copy))
            S.wait(act, "act", ("turned copied", 9))
            S.wait(act, "dve", ("turned copied", 9))
            for i in range(2):
                S.mark("act", ("ctx squares", i), act.activation(sq[:, i, :].rearrange("p (k t) -> p k t", k=4), cT[:, 4 * i:4 * i + 4, :], ACT.Square))
            for k in range(KT):
                S.wait(act, "pe", ("ctx squares summed", k) if k < 2 else ("squares summed", k - 2))
                S.mark("act", ("squares", k), act.activation(sq[:, k % 2, :], xT[:, k, :], ACT.Square))
            S.wait(act, "pe", ("ctx squares summed", 1))
            S.wait(act, "pool", "eps made")
            S.mark("act", "ctx root", act.activation(rb[:, T:T + TC], U[0][:, 0:TC], ACT.Sqrt, scale=1.0 / D, bias=epsc))
            S.wait(act, "pe", ("squares summed", KT - 1))
            S.mark("act", "root", act.activation(rb[:, 0:T], S2, ACT.Sqrt, scale=1.0 / D, bias=epsc))
            for i, (kind, k) in enumerate([("c", k) for k in range(KT)] + [("x", k) for k in range(KT)]):
                S.wait(act, "dve", ("normed", kind, k))
                n, hi, m = (TC, hc[0], 1) if kind == "c" else (T, H[0], 0)
                S.mark("act", ("hi", kind, k), act.activation(hi[:, k, :], sq[:, i % 2, 0:n], ACT.Identity, bias=mod[:, k, m:m + 1]))
                if i == 1:
                    for j in range(2):
                        split_hi(act, j, j, 1, first=True)
            act.dma_start(xT_d.rearrange("k p t -> p k t"), xT).then_inc(xT_stored, 16)
            act.wait_ge(xT_stored, 16)
            barrier("act", 1)

            def evac(j):
                act.wait_ge(gemm_done, j + 1)
                src = G[j % 2][:, 0:TC]
                if j == 0:
                    src, dst = src[0:2 * RANK], lrc
                elif j < 5:
                    dst = kc[:, (j - 1) * TC:j * TC]
                else:
                    i = j - 5
                    if i >= 4:
                        S.wait(act, "pe", ("vc turned", i // 2 - 2))
                    dst = vcT[:, (i // 2) % 2, i % 2, :]
                S.mark("act", ("ctx job", j), act.activation(dst, src, ACT.Copy))

            def gate_logs():
                for d in range(2):
                    for hh in range(2):
                        S.wait(act, "pe", ("ctx gates", d, hh))
                        for h in range(2):
                            head = 2 * hh + h
                            i = act.activation(c_g[d][:, d + head * TC:d + (head + 1) * TC], U[hh][:, h * TC:(h + 1) * TC],
                                               ACT.Identity, bias=col("bgb" if d else "bgf", head))
                        S.mark("act", ("ctx gates", d, hh), i)
                S.wait(act, "act", ("ctx gates", 1, 1))
                for d in range(2):
                    i = act.activation(c_l[d], c_g[d][:, d:d + T], ACT.Abs)
                S.mark("act", "ctx gates abs", i)
                S.wait(act, "act", "ctx gates abs")
                for d in range(2):
                    i = act.activation(c_l[d], c_l[d], ACT.Exp, scale=-1.0)
                S.mark("act", "ctx gates exp", i)
                S.wait(act, "act", "ctx gates exp")
                for d in range(2):
                    S.mark("act", ("ctx gate logs", d), act.activation(c_l[d], c_l[d], ACT.Ln, bias=1.0))
            evac(0)
            evac(1)
            for j in range(2, J_LR):
                split_hi(act, j, j % 2, j // 2 + 1)
                if j == 2:
                    gate_logs()
                evac(j)
            S.wait(act, "dve", "ctx scans")
            S.mark("act", ("ctx exps", 0), act.activation(c_l[0], c_l[0], ACT.Exp, scale=1.0 / GATE_NORM))
            S.mark("act", ("ctx exps", 1), act.activation(c_l[1], c_F[1], ACT.Exp, scale=1.0 / GATE_NORM))
            S.mark("act", "ctx totals", act.activation(c_t, c_t, ACT.Exp, scale=1.0 / GATE_NORM))
            for d in range(2):
                for h in range(2):
                    S.wait(act, "pe", ("ctx keys turned", d, h))
                    S.mark("act", ("ctx keys turned", d, h), act.activation(c_kn[d][:, 4 * h:4 * h + 4, :], U[h].rearrange("p (i t) -> p i t", i=4), ACT.Copy))
            S.wait(act, "dve", ("ctx state", 1, 3))
            act.dma_start(s0_d.rearrange("h d p v -> p h d v"), c_S).then_inc(s0_stored, 16)
            act.wait_ge(s0_stored, 16)
            barrier("act", 2)

        @block.vector
        def _(v):
            for t in range(10):
                S.wait(v, "pe", ("turned", t, 1))
                dst = cT[:, 4:8, t * P:(t + 1) * P] if t < 2 else xT[:, 4:8, (t - 2) * P:(t - 1) * P]
                S.mark("dve", ("turned copied", t), v.tensor_copy(dst, U[1].rearrange("p (i t) -> p i t", i=4)))
            S.wait(v, "act", "parameters")
            S.wait(v, "pe", ("modulation", 3))
            S.mark("dve", "shift, scale", v.tensor_tensor(mod[:, 0:16, :], G[1][:, NB:NB + 32].rearrange("p (m c) -> p m c", c=2),
                                                          broadcast(par[:, R0["bm"]:R0["bm"] + 16].unsqueeze(2), 2), ALU.add))
            S.wait(v, "dve", "shift, scale")
            S.mark("dve", "norm scales", v.scalar_tensor_tensor(gsc, mod[:, 8:16, :], 1.0, broadcast(par[:, R0["ng"]:R0["ng"] + KT].unsqueeze(2), 2), ALU.add, ALU.mult))
            for kind in ("c", "x"):
                r = rb[:, T:T + TC] if kind == "c" else rb[:, 0:T]
                S.wait(v, "act", "ctx root" if kind == "c" else "root")
                S.mark("dve", ("rstd", kind), v.reciprocal(r, r))
            S.wait(v, "dve", ("rstd", "x"))
            i = 0
            for kind in ("c", "x"):
                n, src, hi, lo, m, r = (TC, cT, *hc, 1, rb[:, T:T + TC]) if kind == "c" else (T, xT, *H, 0, rb[:, 0:T])
                for k in range(KT):
                    t = sq[:, i % 2, 0:n]
                    if i == 0:
                        S.wait(v, "pe", ("squares summed", KT - 1))
                    if i >= 2:
                        S.wait(v, "dve", ("scaled", *(("c" if i - 2 < KT else "x"), (i - 2) % KT)))
                    S.mark("dve", ("normed", kind, k), v.scalar_tensor_tensor(t, src[:, k, :], gsc[:, k, m:m + 1], r, ALU.mult, ALU.mult))
                    S.wait(v, "act", ("hi", kind, k))
                    S.mark("dve", ("scaled", kind, k), v.scalar_tensor_tensor(lo[:, k, :], t, mod[:, k, m:m + 1], hi[:, k, :].bitcast(F32), ALU.add, ALU.subtract))
                    i += 1
            S.wait(v, "pe", ("modulation", 5))
            S.mark("dve", "gate", v.tensor_tensor(mod[:, 16:24, :], G[1][:, 32:48].rearrange("p (m c) -> p m c", c=2),
                                                  broadcast(par[:, R0["bm"] + 16:R0["bm"] + 24].unsqueeze(2), 2), ALU.add))
            v.wait_ge(const_landed, 48)
            S.mark("dve", "gains", v.tensor_tensor(gains, par[:, R0["f1"]:R0["f1"] + KT], par[:, R0["ag"]:R0["ag"] + KT], ALU.mult))
            for name, dst, src in (("levels", lvl, lvl_in), ("masks", maskb, mask_in), ("identity", identb, ident)):
                S.mark("dve", name, v.tensor_copy(dst, src))
            barrier("dve", 1)
            S.wait(v, "pool", "chunk mask")
            for d in range(2):
                S.wait(v, "act", ("ctx gate logs", d))
                S.mark("dve", ("ctx logs", d), v.scalar_tensor_tensor(c_g[d][:, d:d + T], c_g[d][:, d:d + T], 0.0, c_l[d], ALU.min, ALU.subtract))
            S.wait(v, "dve", ("ctx logs", 1))
            S.mark("dve", "ctx last logs", v.tensor_copy(c_t[:, 1, :].unsqueeze(2), chunks(c_g[1][:, 1:T + 1])[:, :, CH - 1:CH]))
            S.wait(v, "dve", "ctx last logs")
            S.mark("dve", "ctx starts", v.memset(chunks(c_g[1][:, 0:T])[:, :, 0:1], 0.0))
            S.wait(v, "dve", "ctx starts")
            for d in range(2):
                i = v.tensor_tensor_scan(c_F[d], smask, c_g[d][:, 0:T], 0.0, ALU.mult, ALU.add)
            S.mark("dve", "ctx sums", i)
            S.wait(v, "dve", "ctx sums")
            S.mark("dve", "ctx ends f", v.tensor_copy(c_t[:, 0, :].unsqueeze(2), chunks(c_F[0])[:, :, CH - 1:CH]))
            S.mark("dve", "ctx ends b", v.tensor_tensor(c_t[:, 1, :].unsqueeze(2), c_t[:, 1, :].unsqueeze(2), chunks(c_F[1])[:, :, CH - 1:CH], ALU.add))
            S.mark("dve", "ctx scans", v.tensor_tensor(chunks(c_l[0]), broadcast(chunks(c_F[0])[:, :, CH - 1:CH], CH), chunks(c_F[0]), ALU.subtract))
            for i in range(4):
                S.wait(v, "pe", ("vc turned", i))
                S.mark("dve", ("vc", i), v.tensor_copy(vc[:, :, i * DV:(i + 1) * DV], U[i % 2].rearrange("p (c m) -> p c m", c=2)))
            for d in range(2):
                S.wait(v, "act", ("ctx exps", d))
                S.mark("dve", ("ctx keys", d), v.tensor_tensor(c_k[d], kc, c_l[d], ALU.mult))
            S.wait(v, "act", "ctx totals")
            for d in range(2):
                for h in range(HEADS):
                    S.wait(v, "pe", ("ctx updates", d, h))
                    far, near = (0, 1) if d == 0 else (1, 0)
                    u = U[h % 2]
                    S.mark("dve", ("ctx far", d, h), v.tensor_copy(c_S[:, h, d, :], u[:, far * DV:(far + 1) * DV]))
                    S.wait(v, "dve", ("ctx far", d, h))
                    S.mark("dve", ("ctx state", d, h), v.scalar_tensor_tensor(
                        c_S[:, h, d, :], c_S[:, h, d, :], c_t[:, d, 2 * h + near:2 * h + near + 1], u[:, near * DV:(near + 1) * DV], ALU.mult, ALU.add))
            barrier("dve", 2)

        o = W0
        smask3 = take("smask3", [P, T], BF16)
        cos, sin = take("cos_t", [P, T]), take("sin_t", [P, T])
        lr = take("lr", [2 * RANK, T])
        wuph = take("wup_head", [2 * RANK, 2, DK])
        K, Q = take("keys", [P, T]), take("queries", [P, T])
        raw, sw = take("raw", [P, T]), take("swapped", [P, T])
        L = [take("sums_f", [P, T + 8]), take("sums_b", [P, T + 8])]
        vT = take("vT", [P, T])
        V = take("V", [P, TT, DV])
        E = [take("exps0", [P, T]), take("exps1", [P, T])]
        X = [take(f"scaled{i}", [P, T]) for i in range(4)]
        probs = take("scores", [P, TT, CH])
        gz = take("silu_zA", [P, 2, T])
        ST = [take("states_f", [P, TT, DV]), take("states_b", [P, TT, DV])]
        KN = [take("keysT_f", [P, TT, P]), take("keysT_b", [P, TT, P])]
        te = take("ends", [P, 2, 8])
        tx = take("end_decays", [P, 2, 8])
        tab_landed, wup_landed, s_landed, swapped = sem("tables_landed"), sem("wup_landed"), sem("states_landed"), sem("swap_landed")
        gate_stored, a_stored = sem("gates_stored"), sem("a_stored")
        PAIRS = len(LEVELS) + 2
        o_T = X[2:4]

        def gla_job(h, i):
            return J_GLA + GLA_JOBS * h + i

        def block_view(t, s):
            v = t.rearrange("p (b u) -> p b u", u=2 * s)
            return v, v[:, :, 0:s], v[:, :, s:2 * s]

        def row(d, k):
            return d[bass.ds(k, 1)].rearrange("k p t -> p (k t)")

        GLA_COLS = (lambda h: C_K + P * h, lambda h: C_Q + P * h, lambda h: C_V + 2 * P * h, lambda h: C_V + 2 * P * h + P,
                    lambda h: C_ZA + 2 * P * h, lambda h: C_ZA + 2 * P * h + P, lambda h: C_GA + 2 * P * h,
                    lambda h: C_GA + 2 * P * h + P, lambda h: C_GB + 2 * P * h, lambda h: C_GB + 2 * P * h + P)

        def dslab(w, c0, kt=KT, r0=0):
            return w[r0:r0 + kt * P, bass.ds(c0, P)].rearrange("(k p) c -> p k c", p=P)

        @block.sync
        def _(sp):
            load_w(J_LR, J_LR % 2, slab(w_in, C_LR))
            after_phase(sp, 2)
            sp.dma_start(cos, a["cos"]).then_inc(tab_landed, 16)
            sp.dma_start(sin, a["sin"]).then_inc(tab_landed, 16)
            S.wait(sp, "pool", "head gate weights cleared")
            with sp.Fori(0, HEADS) as h:
                S.wait(sp, "pe", "gates b1", h - 1)
                sp.dma_start(wuph[0:RANK, 0, :], a["w_gate_up_f"][0][:, bass.ds(h * DK, DK)]).then_inc(wup_landed, 16)
                sp.dma_start(wuph[RANK:2 * RANK, 1, :], a["w_gate_up_b"][0][:, bass.ds(h * DK, DK)]).then_inc(wup_landed, 16)
                for i in range(GLA_JOBS):
                    load_w(gla_job(h, i), i % 2, dslab(w_in, GLA_COLS[i](h)))
                    if i == 5:
                        S.wait(sp, "pe", "o 3", h - 1)
                        for d in range(2):
                            sp.dma_start(ST[d][:, 7 * d, :], s0_d[bass.ds(h, 1), d].rearrange("h p v -> p (h v)")).then_inc(s_landed, 16)

        @block.gpsimd
        def _(g):
            split(J_LR, J_LR % 2, J_LR // 2 + 1)
            after_phase(g, 2)
            S.mark("pool", "head gate weights cleared", g.memset(wuph, 0.0))
            chunk_mask(smask3, "head chunk mask")
            with g.Fori(0, HEADS) as h:
                for i in range(GLA_JOBS):
                    split(gla_job(h, i), i % 2, J_GLA // 2 + GLA_JOBS // 2 * h + i // 2 + 1)

        @block.tensor
        def _(pe):
            gemm(J_LR, J_LR % 2, H)
            S.wait(pe, "act", "lr")
            pe.wait_ge(tab_landed, 32)
            S.enter("pe", "gla")
            with pe.Fori(0, HEADS) as h:
                def turn_to(dst_free, name, src, blocks):
                    s = turn_to.n % 2
                    turn_to.n += 1
                    S.wait(pe, *dst_free)
                    for i, b in enumerate(blocks):
                        mm = pe.transpose(U[s][:, i * P:(i + 1) * P], src[:, b * P:(b + 1) * P], ident)
                    S.mark("pe", name, mm)
                turn_to.n = 0

                def job(i):
                    freed = {0: ("act", "gate evac 2", h - 1), 1: ("act", "gate evac 3", h - 1), 2: ("act", "raw k", h),
                             3: ("act", "raw q", h), 4: ("act", "vT 0", h), 5: ("act", "vT 1", h), 6: ("act", "zA 0", h),
                             7: ("act", "zA 1", h), 8: ("act", "gate evac 0", h), 9: ("act", "gate evac 1", h)}[i]
                    gemm(gla_job(h, i), i % 2, H, freed)

                def level(w):
                    S.wait(pe, "dve", f"stage {w}", h)
                    S.wait(pe, "dve", f"placed {w - 1}", h)
                    kx, qx = X[2 * (w % 2)], X[2 * (w % 2) + 1]
                    for c in range(TT):
                        mm = pe.matmul(S2[:, c * CH:(c + 1) * CH], kx[:, c * CH:(c + 1) * CH], qx[:, c * CH:(c + 1) * CH], start=True, stop=True)
                    S.mark("pe", f"level {w}", mm)

                pe.wait_ge(wup_landed, 32 * h + 32)
                for d in range(2):
                    for n in range(2):
                        S.wait(pe, "act", *((f"gates f{n}", h) if d else (f"summed r{n}", h - 1)))
                        S.mark("pe", f"gates {'fb'[d]}{n}", pe.matmul(U[n], wuph[:, d, :], lr[:, n * NB:(n + 1) * NB], start=True, stop=True))
                job(0)
                job(1)
                job(2)
                job(3)
                S.wait(pe, "act", "vT 0", h)
                turn_to(("act", "gates b0", h), "v turned 00", vT, range(0, 4))
                turn_to(("act", "gates b1", h), "v turned 01", vT, range(4, 8))
                job(4)
                S.wait(pe, "act", "vT 1", h)
                turn_to(("act", "V 00", h), "v turned 10", vT, range(0, 4))
                turn_to(("act", "V 01", h), "v turned 11", vT, range(4, 8))
                S.wait(pe, "dve", "stage 0", h)
                for d in range(2):
                    for n in range(2):
                        turn_to(("act", f"V 1{n}" if d == 0 else f"KN 0{n}", h), f"keys turned {d}{n}", X[d], range(4 * n, 4 * n + 4))
                job(5)
                for d in range(2):
                    for i in range(4):
                        S.wait(pe, "act", f"KN {d}1", h)
                        if d == 0 and i < 2:
                            S.wait(pe, "act", f"KN 1{i}", h)
                        else:
                            S.wait(pe, "dve", f"state {d if i >= 2 else 0}{(i - 2) % 4}", h)
                        for n in range(2):
                            c = 2 * i + n if d == 0 else 7 - 2 * i - n
                            mm = pe.matmul(U[i % 2][:, n * DV:(n + 1) * DV], KN[d][:, c, :], V[:, c, :], start=True, stop=True)
                        S.mark("pe", f"updates {d}{i}", mm)
                    if d == 0:
                        job(6)
                S.wait(pe, "dve", "rope q", h)
                S.wait(pe, "dve", "rope k", h)
                for c in range(TT):
                    mm = pe.matmul(S2[:, c * CH:(c + 1) * CH], K[:, c * CH:(c + 1) * CH], Q[:, c * CH:(c + 1) * CH], start=True, stop=True)
                S.mark("pe", "level 0", mm)
                level(1)
                job(7)
                level(2)
                level(3)
                job(8)
                level(4)
                level(5)
                job(9)
                level(6)
                level(7)
                S.wait(pe, "dve", "placed 7", h)
                S.wait(pe, "dve", f"stage {PAIRS - 1}", h)
                for m in range(2):
                    for n in range(2):
                        i = 2 * m + n
                        S.wait(pe, *(("dve", f"state 1{2 + i}", h) if i < 2 else ("act", f"o {i - 2}", h)))
                        for c in range(4 * n, 4 * n + 4):
                            dst = U[n][:, (c % 4) * CH:(c % 4 + 1) * CH]
                            cols, f = slice(c * CH, (c + 1) * CH), slice(m * P, (m + 1) * P)
                            pe.matmul(dst, V[:, c, f], probs[:, c, :], start=True, stop=False)
                            pe.matmul(dst, ST[0][:, c, f], X[0][:, cols], start=False, stop=False)
                            mm = pe.matmul(dst, ST[1][:, c, f], X[1][:, cols], start=False, stop=True)
                        S.mark("pe", f"o {i}", mm)
                S.wait(pe, "dve", "o squares", h)
                for n in range(2):
                    S.wait(pe, "act", f"o {2 + n}", h)
                    mm = pe.matmul(U[n], ones, E[0][:, n * NB:(n + 1) * NB], start=True, stop=True)
                    S.mark("pe", f"o summed {n}", mm)
            S.leave("pe", HEADS)
            barrier("pe", 3)

        @block.scalar
        def _(act):
            act.wait_ge(gemm_done, J_LR + 1)
            S.mark("act", "lr", act.activation(lr, G[J_LR % 2][0:2 * RANK, :], ACT.Copy))
            S.enter("act", "gla")
            with act.Fori(0, HEADS) as h:
                for d in range(2):
                    b = par[:, bass.ds(h + (R0["bgb"] if d else R0["bgf"]), 1)]
                    for n in range(2):
                        S.wait(act, "pe", f"gates {'fb'[d]}{n}", h)
                        if d == 0 and n == 0:
                            S.wait(act, "dve", "stage 8", h - 1)
                        settle(act, h)
                        S.mark("act", f"gates {'fb'[d]}{n}", act.activation(L[d][:, d + n * NB:d + (n + 1) * NB], U[n], ACT.Identity, bias=b))
                S.wait(act, "act", "gates b1", h)
                S.wait(act, "dve", "o scaled 1", h - 1)
                for d in range(2):
                    i = act.activation(E[d], L[d][:, d:d + T], ACT.Abs)
                S.mark("act", "gates abs", i)
                S.wait(act, "act", "gates abs", h)
                for d in range(2):
                    i = act.activation(E[d], E[d], ACT.Exp, scale=-1.0)
                S.mark("act", "gates exp", i)
                S.wait(act, "act", "gates exp", h)
                for d in range(2):
                    S.mark("act", f"gate logs {d}", act.activation(E[d], E[d], ACT.Ln, bias=1.0))

                def evac(i, name, dst, func=ACT.Copy, **more):
                    act.wait_ge(gemm_done, gla_job(h, i) + 1)
                    S.mark("act", name, act.activation(dst, G[i % 2], func, **more))

                def swap(turn):
                    for q in range(4):
                        src = q ^ 1
                        act.dma_start(sw[32 * q:32 * q + 32, :], raw[32 * src:32 * src + 32, :]).then_inc(swapped, 16)
                evac(0, "raw k", raw)
                S.wait(act, "act", "raw k", h)
                swap(0)
                S.wait(act, "dve", "rope k", h)
                evac(1, "raw q", raw, scale=float(DK) ** -0.5)
                S.wait(act, "act", "raw q", h)
                swap(1)
                S.wait(act, "dve", "exponents 0", h)
                i = act.activation(E[0], E[0], ACT.Exp, scale=1.0 / GATE_NORM)
                S.mark("act", "exps 0 0", i)
                S.mark("act", "exps 0 1", act.activation(E[1], L[1][:, 0:T], ACT.Exp, scale=1.0 / GATE_NORM))
                S.mark("act", "end decays", act.activation(tx, te, ACT.Exp, scale=1.0 / GATE_NORM))
                evac(2, "vT 0", vT)

                def copy_v(m):
                    for n in range(2):
                        S.wait(act, "pe", f"v turned {m}{n}", h)
                        S.mark("act", f"V {m}{n}", act.activation(V[:, 4 * n:4 * n + 4, m * P:(m + 1) * P], U[n].rearrange("p (c f) -> p c f", f=P), ACT.Copy))
                copy_v(0)
                evac(3, "vT 1", vT)
                copy_v(1)
                for d in range(2):
                    for n in range(2):
                        S.wait(act, "pe", f"keys turned {d}{n}", h)
                        S.mark("act", f"KN {d}{n}", act.activation(KN[d][:, 4 * n:4 * n + 4, :], U[n].rearrange("p (c f) -> p c f", f=P), ACT.Copy))

                def exps(w):
                    for e in range(2):
                        if w < PAIRS - 1 or e == 1:
                            S.wait(act, "dve", f"exponents {w} {e}", h)
                        else:
                            S.wait(act, "dve", f"stage {w - 1}", h)
                        src = L[0][:, 0:T] if w == PAIRS - 1 and e == 0 else E[e]
                        S.mark("act", f"exps {w} {e}", act.activation(E[e], src, ACT.Exp, scale=1.0 / GATE_NORM))
                exps(1)
                evac(4, "zA 0", gz[:, 0, :], ACT.Silu)
                evac(5, "zA 1", gz[:, 1, :], ACT.Silu)

                def gate(i):
                    dst = (raw, sw)[i % 2]
                    if i < 2:
                        S.wait(act, "dve", "rope q", h)
                    else:
                        act.wait_ge(gate_stored, 64 * h + 32)
                    evac(6 + i, f"gate evac {i}", dst, ACT.Sigmoid)
                    S.wait(act, "act", f"gate evac {i}", h)
                    act.dma_start(row((sga_d, sgb_d)[i // 2], 2 * h + i % 2), dst).then_inc(gate_stored, 16)
                exps(2)
                gate(0)
                exps(3)
                exps(4)
                gate(1)
                exps(5)
                exps(6)
                gate(2)
                exps(7)
                exps(8)
                gate(3)
                act.wait_ge(gate_stored, 64 * h + 64)
                for m in range(2):
                    for n in range(2):
                        i = 2 * m + n
                        S.wait(act, "pe", f"o {i}", h)
                        S.mark("act", f"o {i}", act.activation(o_T[m][:, n * NB:(n + 1) * NB], U[n], ACT.Copy))
                for m in range(2):
                    S.wait(act, "act", f"o {2 * m + 1}", h)
                    S.mark("act", f"o squares {m}", act.activation(E[m], o_T[m], ACT.Square))
                for n in range(2):
                    S.wait(act, "pe", f"o summed {n}", h)
                    S.mark("act", f"summed r{n}", act.activation(E[1][:, n * NB:(n + 1) * NB], U[n], ACT.Sqrt, scale=1.0 / DV, bias=epsc))
                S.wait(act, "dve", "o scaled 1", h)
                for m in range(2):
                    act.dma_start(row(a_d, 2 * h + m), o_T[m]).then_inc(a_stored, 16)
                act.wait_ge(a_stored, 32 * h + 32)
            S.leave("act", HEADS)
            barrier("act", 3)

        @block.vector
        def _(v):
            def do(name, ins):
                return S.mark("dve", name, ins)
            v.wait_ge(tab_landed, 32)
            S.wait(v, "pool", "head chunk mask")
            v.wait_ge(const_landed, 48)
            S.enter("dve", "gla")
            with v.Fori(0, HEADS) as h:
                def me(name, turn=None):
                    S.wait(v, "dve", name, h if turn is None else turn)
                for d in range(2):
                    S.wait(v, "act", f"gate logs {d}", h)
                    do(f"logs {d}", v.scalar_tensor_tensor(L[d][:, d:d + T], L[d][:, d:d + T], 0.0, E[d], ALU.min, ALU.subtract))
                me("logs 1")
                do("last logs", v.tensor_copy(te[:, 1, :].unsqueeze(2), chunks(L[1][:, 1:T + 1])[:, :, CH - 1:CH]))
                me("last logs")
                do("starts", v.memset(chunks(L[1][:, 0:T])[:, :, 0:1], 0.0))
                me("starts")
                for d in range(2):
                    i = v.tensor_tensor_scan(L[d][:, 0:T], smask3, L[d][:, 0:T], 0.0, ALU.mult, ALU.add)
                do("sums", i)
                me("sums")
                do("ends f", v.tensor_copy(te[:, 0, :].unsqueeze(2), chunks(L[0][:, 0:T])[:, :, CH - 1:CH]))
                do("ends b", v.tensor_tensor(te[:, 1, :].unsqueeze(2), te[:, 1, :].unsqueeze(2), chunks(L[1][:, 0:T])[:, :, CH - 1:CH], ALU.add))
                F, B = L[0][:, 0:T], L[1][:, 0:T]
                do("exponents 0", v.tensor_tensor(chunks(E[0]), broadcast(chunks(F)[:, :, CH - 1:CH], CH), chunks(F), ALU.subtract))

                def rope(name, n, dst):
                    S.wait(v, "act", f"raw {name}", h)
                    do(f"cos {name}", v.tensor_tensor(dst, raw, cos, ALU.mult))
                    v.wait_ge(swapped, 128 * h + 64 * (n + 1))
                    do(f"sin {name}", v.tensor_tensor(sw, sw, sin, ALU.mult))
                    me(f"sin {name}")
                    do(f"rope {name}", v.tensor_tensor(dst, dst, sw, ALU.add))
                S.wait(v, "pe", "level 0", h - 1)
                rope("k", 0, K)
                rope("q", 1, Q)
                me("rope q")

                def stage(w, first, second):
                    if w >= 2:
                        S.wait(v, "pe", f"level {w - 2}" if w > 2 else "keys turned 11", h)
                    elif w == 0:
                        S.wait(v, "pe", "o 3", h - 1)
                    for e, src in enumerate((first, second)):
                        S.wait(v, "act", f"exps {w} {e}", h)
                        i = v.tensor_tensor(X[2 * (w % 2) + e], src, E[e], ALU.mult)
                        do(f"stage {w}" if e else f"stage {w} k", i)

                def exponents(w):
                    s = LEVELS[w - 1]
                    me(f"stage {w - 1} k")
                    fv, fl, fr = block_view(F, s)
                    bv, bl, br = block_view(B, s)
                    fb, bb = broadcast(fv[:, :, s - 1:s], s), broadcast(bv[:, :, s:s + 1], s)
                    _, kl, kr = block_view(E[0], s)
                    _, ql, qr = block_view(E[1], s)
                    v.tensor_tensor(kl, fb, fl, ALU.subtract)
                    do(f"exponents {w} 0", v.tensor_tensor(kr, br, bb, ALU.subtract))
                    me(f"stage {w - 1}")
                    v.tensor_tensor(ql, bb, bl, ALU.subtract)
                    do(f"exponents {w} 1", v.tensor_tensor(qr, fr, fb, ALU.subtract))

                def place(w):
                    S.wait(v, "pe", f"level {w}", h)
                    s2 = chunks(S2)
                    if w == 0:
                        do("placed 0", v.scalar_tensor_tensor(probs, s2, 2.0, ident.unsqueeze(1).to_broadcast([P, TT, P]), ALU.mult, ALU.mult))
                    else:
                        me(f"placed {w - 1}")
                        settle(v, h)
                        do(f"placed {w}", v.copy_predicated(probs, lvl[:, w - 1, :].unsqueeze(1).to_broadcast([P, TT, P]), s2))
                stage(0, K, K)
                exponents(1)
                v.wait_ge(s_landed, 32 * h + 32)
                S.wait(v, "act", "end decays", h)
                for d in range(2):
                    for i in range(4):
                        S.wait(v, "pe", f"updates {d}{i}", h)
                        for n in range(2):
                            c = 2 * i + n if d == 0 else 7 - 2 * i - n
                            if i == 3 and n == 1:
                                continue
                            to = c + 1 if d == 0 else c - 1
                            if (i, n) != (0, 0):
                                me(f"state {d}{i} {0}" if n else f"state {d}{i - 1}")
                            do(f"state {d}{i}" if n or i == 3 else f"state {d}{i} 0",
                               v.scalar_tensor_tensor(ST[d][:, to, :], ST[d][:, c, :], tx[:, d, c:c + 1], U[i % 2][:, n * DV:(n + 1) * DV], ALU.mult, ALU.add))
                S.wait(v, "act", "gates f0", h)
                stage(1, K, Q)
                S.wait(v, "pe", "o 3", h - 1)
                for w in range(1, len(LEVELS) + 1):
                    if w < len(LEVELS):
                        exponents(w + 1)
                    place(w - 1)
                    if w < len(LEVELS):
                        stage(w + 1, K, Q)
                me(f"stage {PAIRS - 2}")
                do(f"exponents {PAIRS - 1} 1", v.tensor_tensor(chunks(E[1]), broadcast(te[:, 1, :].unsqueeze(2), CH), chunks(B), ALU.subtract))
                place(len(LEVELS))
                stage(PAIRS - 1, Q, Q)
                S.wait(v, "act", "o squares 1", h)
                do("o squares", v.tensor_tensor(E[0], E[0], E[1], ALU.add))
                S.wait(v, "act", "summed r1", h)
                do("o rstd", v.reciprocal(E[1], E[1]))
                me("o rstd")
                for m in range(2):
                    do(f"o normed {m}", v.scalar_tensor_tensor(o_T[m], o_T[m], col("gg", m), E[1], ALU.mult, ALU.mult))
                for m in range(2):
                    me(f"o normed {m}")
                    if m == 0:
                        S.wait(v, "act", "zA 1", h)
                    do(f"o scaled {m}", v.tensor_tensor(o_T[m], o_T[m], gz[:, m, :], ALU.mult))
            S.leave("dve", HEADS)
            barrier("dve", 3)

        o = W0
        A = [take("A_hi", [P, KT, T], F32R), take("A_lo", [P, KT, T], F32R)]
        o4 = o
        PAD = 8
        u_in = take("pool_in", [P, T + PAD])
        cs = take("pool_sums", [P, T + 2 * PAD + 1])
        d_mov = [take("pooled_hi", [P, 2, T], F32R), take("pooled_lo", [P, 2, T], F32R)]
        pz = take("silu_zB", [P, 2, T])
        inv = take("inv_count", [P, T])
        pw = take("pool_work", [P, T])
        a_in = take("a_in", [P, 2, T])
        o = o4
        X2 = take("x2", [P, KT, T])
        gs, bs = take("tiles_in", [P, 2, T]), take("tiles_made", [P, 2, T])

        POOL_ORDER = [(g, w) for g in range(4) for w in ("u0", "u1", "z0", "z1", "p0", "p1")]
        inv_landed, ain_landed, b_stored = sem("inv_landed"), sem("a_in_landed"), sem("b_stored")
        gs_landed, bs_landed = [sem("gs_landed0"), sem("gs_landed1")], [sem("bs_landed0"), sem("bs_landed1")]

        def pool_src(g, what):
            m = int(what[1])
            if what[0] == "p":
                return a["w_pool"][0, g][:, m * P:(m + 1) * P].rearrange("(k p) c -> p k c", p=P), 2
            return slab(w_in, (C_UB if what[0] == "u" else C_ZB) + (2 * g + m) * P), KT

        def pool_freed(n):
            if n < 0:
                return None
            g, what = POOL_ORDER[n]
            return "dve" if what[0] == "p" else "act", ("pool job", g, what)

        def tile2(t, k):
            return t[:, bass.ds(k, 1), :].rearrange("p k t -> p (k t)")

        BRANCHES = (("bra", J_BRA, a["w_branch_a"][0], A), ("brb", J_BRB, a["w_branch_b"][0], H), ("out", J_OUT, a["w_out"][0], A))

        def loads_of_8(j0, w, kt=KT, r0=0):
            with nc.sync.Fori(0, KT // 2) as i:
                for m in range(2):
                    load_w(j0 + 2 * i + m, (j0 + m) % 2, dslab(w, (2 * i + m) * P, kt, r0), kt)

        def splits_of(j0, pairs=KT // 2, kt=KT):
            with nc.gpsimd.Fori(0, pairs) as i:
                for m in range(2):
                    split(j0 + 2 * i + m, (j0 + m) % 2, i + ((j0 + m) // 2 + 1), kt)

        def products_of_8(name, j0, mov, kt=KT):
            S.enter("pe", name)
            with nc.tensor.Fori(0, KT // 2) as i:
                for m in range(2):
                    gemm(j0 + 2 * i + m, (j0 + m) % 2, mov, ("dve", f"{name} job {m}", i - 1), kt=kt)
            S.leave("pe", KT // 2)

        def residual_act(name, first_wait, fetch=None, squares=True):
            act = nc.scalar
            for w in first_wait:
                S.wait(act, *w)
            S.enter("act", name)
            with act.Fori(0, KT // 2) as i:
                for m in range(2):
                    if fetch is not None:
                        S.wait(act, "dve", f"{name} job {m}", i - 1)
                        act.dma_start(gs[:, m, :], row(fetch, 2 * i + m)).then_inc(gs_landed[m], 16)
                    if squares:
                        S.wait(act, "dve", f"{name} sum {m}", i - 1)
                        S.wait(act, "dve", f"{name} job {m}", i)
                        settle(act, i)
                        S.mark("act", f"{name} square {m}", act.activation(bs[:, m, :], tile2(X2, 2 * i + m), ACT.Square))
            S.leave("act", KT // 2)

        def residual_dve(name, j0, fetched=None, gate=False, squares=True):
            v = nc.vector
            if squares:
                S.mark("dve", f"{name} zero", v.memset(S2, 0.0))
                S.wait(v, "dve", f"{name} zero")
            S.enter("dve", name)
            with v.Fori(0, KT // 2) as i:
                for m in range(2):
                    v.wait_ge(gemm_done, j0 + 2 * i + m + 1)
                    if fetched is not None:
                        v.wait_ge(gs_landed[m], 16 * (fetched + i + 1))
                    k = 2 * i + m
                    other = gs[:, m, :] if fetched is not None else tile2(X2, k)
                    by = mod[:, bass.ds(16 + k, 1), 0:1].rearrange("p a b -> p (a b)") if gate else 1.0
                    S.mark("dve", f"{name} job {m}", v.scalar_tensor_tensor(tile2(X2, k), G[(j0 + m) % 2], by, other, ALU.mult, ALU.add))
                    if squares:
                        S.wait(v, "act", f"{name} square {m}", i)
                        S.mark("dve", f"{name} sum {m}", v.tensor_tensor(S2, S2, bs[:, m, :], ALU.add))
                        S.wait(v, "dve", f"{name} sum {m}", i)
            S.leave("dve", KT // 2)
            if squares:
                S.mark("dve", f"{name} squares", v.tensor_copy(bs[:, 1, :], S2))

        def norm_pe(name):
            S.wait(nc.tensor, "dve", f"{name} squares")
            for n in range(2):
                mm = nc.tensor.matmul(S2[:, n * NB:(n + 1) * NB], ones, bs[:, 1, n * NB:(n + 1) * NB], start=True, stop=True)
            S.mark("pe", f"{name} summed", mm)

        def norm_act(name, dst):
            act = nc.scalar
            S.wait(act, "pe", f"{name} summed")
            S.mark("act", f"{name} root", act.activation(gs[:, 0, :], S2, ACT.Sqrt, scale=1.0 / D, bias=epsc))
            for k in range(KT):
                S.wait(act, "dve", (name, "t", k))
                S.mark("act", (name, "hi", k), act.activation(dst[0][:, k, :], bs[:, k % 2, :], ACT.Copy))

        def norm_dve(name, gain, dst):
            v = nc.vector
            S.wait(v, "act", f"{name} root")
            S.mark("dve", f"{name} rstd", v.reciprocal(gs[:, 0, :], gs[:, 0, :]))
            S.wait(v, "dve", f"{name} rstd")
            for k in range(KT):
                if k >= 2:
                    S.wait(v, "dve", (name, "lo", k - 2))
                S.mark("dve", (name, "t", k), v.scalar_tensor_tensor(bs[:, k % 2, :], X2[:, k, :], col(gain, k), gs[:, 0, :], ALU.mult, ALU.mult))
                S.wait(v, "act", (name, "hi", k))
                S.mark("dve", (name, "lo", k), v.tensor_tensor(dst[1][:, k, :], bs[:, k % 2, :], dst[0][:, k, :].bitcast(F32), ALU.subtract))

        @block.sync
        def _(sp):
            for n, (g, what) in enumerate(POOL_ORDER):
                src, kt = pool_src(g, what)
                load_w(J_POOL + n, n % 2, src, kt)
                if n == 1:
                    after_phase(sp, 3)
                    for k in range(2):
                        sp.dma_start(a_in[:, k, :], a_d[k]).then_inc(ain_landed, 16)
                    sp.dma_start(inv, a["inv_count"][0]).then_inc(inv_landed, 16)
                if n >= 3 and n % 3 == 0 and n // 3 + 1 < KT:
                    k = n // 3 + 1
                    S.wait(sp, "dve", ("a split", k - 2))
                    sp.dma_start(a_in[:, k % 2, :], a_d[k]).then_inc(ain_landed, 16)
                if what == "p0" and g < 3:
                    S.wait(sp, "dve", ("pooled", g, 1))
                    sp.dma_start(inv, a["inv_count"][g + 1]).then_inc(inv_landed, 16)
            for _, j0, w, _ in BRANCHES:
                loads_of_8(j0, w)

        @block.gpsimd
        def _(g):
            for n, (grp, what) in enumerate(POOL_ORDER):
                split(J_POOL + n, n % 2, (J_POOL + n) // 2 + 1, pool_src(grp, what)[1])
            for _, j0, _, _ in BRANCHES:
                splits_of(j0)

        @block.tensor
        def _(pe):
            for n, (g, what) in enumerate(POOL_ORDER):
                if what == "p0":
                    S.wait(pe, "dve", ("pooled lo", g, 1))
                gemm(J_POOL + n, n % 2, d_mov if what[0] == "p" else H, pool_freed(n - 2), kt=pool_src(g, what)[1])
            barrier("pe", 4)
            for name, j0, _, mov in BRANCHES:
                if name == "brb":
                    S.wait(pe, "dve", "bra job 1", KT // 2 - 1)
                    S.wait(pe, "dve", "b split 1", KT // 2 - 1)
                if name == "out":
                    S.wait(pe, "dve", "mix split 1", KT // 2 - 1)
                products_of_8(name, j0, mov)

        @block.scalar
        def _(act):
            for n, (g, what) in enumerate(POOL_ORDER):
                m = int(what[1])
                if what[0] == "u":
                    act.wait_ge(gemm_done, J_POOL + n + 1)
                    if (g, m) != (0, 0):
                        S.wait(act, "dve", ("pooled", *((g, 0) if m else (g - 1, 1))))
                    S.mark("act", ("pool job", g, what), act.activation(u_in[:, 0:T], G[n % 2], ACT.Copy))
                elif what[0] == "z":
                    act.wait_ge(gemm_done, J_POOL + n + 1)
                    if g:
                        act.wait_ge(b_stored, 32 * g)
                    S.mark("act", ("pool job", g, what), act.activation(pz[:, m, :], G[n % 2], ACT.Silu))
                else:
                    S.wait(act, "dve", ("pool job", g, what))
                    act.dma_start(b_d[2 * g + m], pz[:, m, :]).then_inc(b_stored, 16)
                if n % 3 == 0:
                    k = n // 3
                    act.wait_ge(ain_landed, 16 * max(k + 1, 2))
                    S.mark("act", ("a hi", k), act.activation(A[0][:, k, :], a_in[:, k % 2, :], ACT.Copy))
            act.wait_ge(b_stored, 16 * KT)
            barrier("act", 4)
            S.enter("act", "bra")
            with act.Fori(0, KT // 2) as i:
                for m in range(2):
                    S.wait(act, "dve", f"bra job {m}", i - 1)
                    act.dma_start(gs[:, m, :], row(sga_d, 2 * i + m)).then_inc(gs_landed[m], 16)
                    S.wait(act, "dve", f"b split {m}", i - 1)
                    act.dma_start(bs[:, m, :], row(b_d, 2 * i + m)).then_inc(bs_landed[m], 16)
                    act.wait_ge(bs_landed[m], 16 * i + 16)
                    settle(act, i)
                    S.mark("act", f"b hi {m}", act.activation(tile2(H[0], 2 * i + m), bs[:, m, :], ACT.Copy))
            S.leave("act", KT // 2)
            S.wait(act, "dve", "bra job 1", KT // 2 - 1)
            S.enter("act", "brb")
            with act.Fori(0, KT // 2) as i:
                for m in range(2):
                    S.wait(act, "dve", f"mix {m}", i - 1)
                    act.dma_start(gs[:, m, :], row(sgb_d, 2 * i + m)).then_inc(gs_landed[m], 16)
                    S.wait(act, "dve", f"mix {m}", i)
                    settle(act, i)
                    S.mark("act", f"mix hi {m}", act.activation(tile2(A[0], 2 * i + m), bs[:, m, :], ACT.Copy))
            S.leave("act", KT // 2)
            S.wait(act, "dve", "mix split 1", KT // 2 - 1)
            S.enter("act", "out")
            with act.Fori(0, KT // 2) as i:
                for m in range(2):
                    k = 2 * i + m
                    S.wait(act, "dve", f"out job {m}", i - 1)
                    act.dma_start(gs[:, m, :], row(xT_d, k)).then_inc(gs_landed[m], 16)
                    S.wait(act, "dve", f"out job {m}", i)
                    settle(act, i)
                    S.mark("act", f"out square {m}", act.activation(bs[:, 0, :], tile2(X2, k), ACT.Square))
                    S.mark("act", f"out scaled square {m}", act.activation(bs[:, 1, :], tile2(X2, k), ACT.Square, scale=par[:, bass.ds(k + R0["f1"], 1)]))
                    S.wait(act, "dve", f"out operand {m}", i)
                    settle(act, i)
                    S.mark("act", f"out hi {m}", act.activation(tile2(H[0], k), tile2(H[1], k).bitcast(F32), ACT.Copy))
            S.leave("act", KT // 2)

        @block.vector
        def _(v):
            def do(name, ins):
                S.mark("dve", name, ins)
                return name
            def me(name, turn=None):
                S.wait(v, "dve", name, turn)
            v.memset(u_in[:, T:T + PAD], 0.0)
            do("pool pads", v.memset(cs[:, 0:PAD + 1], 0.0))
            me("pool pads")
            for n, (g, what) in enumerate(POOL_ORDER):
                m, half = int(what[1]), POOL_WINDOWS[g] // 2
                if what[0] == "u":
                    S.wait(v, "act", ("pool job", g, what))
                    me(do(("pool sums", g, m), v.tensor_tensor_scan(cs[:, PAD + 1:], u_in, u_in, 0.0, ALU.add, ALU.bypass)))
                    me(do(("pool windows", g, m), v.tensor_tensor(pw, cs[:, PAD + half:PAD + half + T], cs[:, PAD - half:PAD - half + T], ALU.subtract)))
                    v.wait_ge(inv_landed, 16 * (g + 1))
                    me(do(("pool means", g, m), v.tensor_tensor(pw, pw, inv, ALU.mult)))
                    me(do(("pooled", g, m), v.tensor_tensor(pw, pw, u_in[:, 0:T], ALU.subtract)))
                    if g and m == 0:
                        v.wait_ge(gemm_done, J_POOL + 6 * g)
                    me(do(("pooled hi", g, m), v.tensor_copy(d_mov[0][:, m, :], pw)))
                    me(do(("pooled lo", g, m), v.tensor_tensor(d_mov[1][:, m, :], pw, d_mov[0][:, m, :].bitcast(F32), ALU.subtract)))
                elif what[0] == "p":
                    v.wait_ge(gemm_done, J_POOL + n + 1)
                    S.wait(v, "act", ("pool job", g, f"z{m}"))
                    do(("pool job", g, what), v.scalar_tensor_tensor(pz[:, m, :], G[n % 2], col("ps", 2 * g + m), pz[:, m, :], ALU.mult, ALU.mult))
                if n % 3 == 0:
                    k = n // 3
                    S.wait(v, "act", ("a hi", k))
                    do(("a split", k), v.tensor_tensor(A[1][:, k, :], a_in[:, k % 2, :], A[0][:, k, :].bitcast(F32), ALU.subtract))
            barrier("dve", 4)
            S.enter("dve", "bra")
            with v.Fori(0, KT // 2) as i:
                for m in range(2):
                    k = 2 * i + m
                    S.wait(v, "act", f"b hi {m}", i)
                    do(f"b split {m}", v.tensor_tensor(tile2(H[1], k), bs[:, m, :], tile2(H[0], k).bitcast(F32), ALU.subtract))
                    v.wait_ge(gemm_done, J_BRA + k + 1)
                    v.wait_ge(gs_landed[m], 16 * i + 16)
                    do(f"bra job {m}", v.tensor_tensor(tile2(X2, k), G[m], gs[:, m, :], ALU.mult))
            S.leave("dve", KT // 2)
            me("bra job 1", KT // 2 - 1)
            S.enter("dve", "brb")
            with v.Fori(0, KT // 2) as i:
                for m in range(2):
                    k = 2 * i + m
                    v.wait_ge(gemm_done, J_BRB + k + 1)
                    v.wait_ge(gs_landed[m], 16 * i + 16 + 16 * KT // 2)
                    do(f"brb job {m}", v.tensor_tensor(gs[:, m, :], G[m], gs[:, m, :], ALU.mult))
                    me(f"brb job {m}", i)
                    me(f"mix split {m}", i - 1)
                    do(f"mix {m}", v.tensor_tensor(bs[:, m, :], gs[:, m, :], tile2(X2, k), ALU.add))
                    S.wait(v, "act", f"mix hi {m}", i)
                    do(f"mix split {m}", v.tensor_tensor(tile2(A[1], k), bs[:, m, :], tile2(A[0], k).bitcast(F32), ALU.subtract))
            S.leave("dve", KT // 2)
            v.memset(U2, 0.0)
            me(do("out zero", v.memset(S2, 0.0)))
            S.enter("dve", "out")
            with v.Fori(0, KT // 2) as i:
                for m in range(2):
                    k = 2 * i + m
                    v.wait_ge(gemm_done, J_OUT + k + 1)
                    v.wait_ge(gs_landed[m], 16 * i + 16 * (KT + 1))
                    do(f"out job {m}", v.scalar_tensor_tensor(tile2(X2, k), G[(J_OUT + m) % 2], mod[:, bass.ds(16 + k, 1), 0:1].rearrange("p a b -> p (a b)"),
                                                              gs[:, m, :], ALU.mult, ALU.add))
                    me(f"out job {m}", i)
                    do(f"out operand {m}", v.tensor_scalar(tile2(H[1], k).bitcast(F32), tile2(X2, k), gains[:, bass.ds(k, 1)], None, ALU.mult))
                    S.wait(v, "act", f"out square {m}", i)
                    do(f"out sum {m}", v.tensor_tensor(S2, S2, bs[:, 0, :], ALU.add))
                    S.wait(v, "act", f"out scaled square {m}", i)
                    do(f"out scaled sum {m}", v.tensor_tensor(U2, U2, bs[:, 1, :], ALU.add))
                    S.wait(v, "act", f"out hi {m}", i)
                    do(f"out lo {m}", v.tensor_tensor(tile2(H[1], k), tile2(H[1], k).bitcast(F32), tile2(H[0], k).bitcast(F32), ALU.subtract))
                    me(f"out lo {m}", i)
            S.leave("dve", KT // 2)
            v.tensor_copy(bs[:, 0, :], U2)
            do("out squares", v.tensor_copy(bs[:, 1, :], S2))

        o = W0
        Qh = [take(f"q_hi{h}", [P, T], F32R) for h in range(2)]
        Ql = [take(f"q_lo{h}", [P, T], F32R) for h in range(2)]
        Ks = [take(f"k_parts{h}", [P, T], F32R) for h in range(2)]
        av = take("att_v", [P, TT, P])
        ON = take("att_out", [P, TT, P])
        avT = ON.rearrange("p t d -> p (t d)")
        OT = take("att_outT", [P, T])
        osq = take("att_squares", [P, T])
        SQ = [take("fox_squares", [P, T]), take("sb_squares", [P, T])]
        R1 = take("rstd1", [P, T])
        SC = take("rstd12", [P, T])
        qt = take("projected", [P, T])
        pT = [take("probsT0", [P, 4, P]), take("probsT1", [P, 4, P])]
        assert o <= W0 + 64 * KB, o
        o = W0 + 96 * KB
        pr = [take("probs0", [P, T]), take("probs1", [P, T])]
        nots = take("not_taken", [P, T])
        left = take("left_over", [P, T + 8])
        rs = take("row_sums", [P, 4, 1])
        mn = take("row_mins", [P, 2, 1])
        nf_d = scratch("forget_sums", (S_HEADS, T))
        w_in2 = a["w_in_2"][0]
        o_stored, o_landed = sem("heads_out_stored"), sem("heads_out_landed")
        nf_stored, nf_landed, out_stored = sem("forget_sums_stored"), sem("forget_sums_landed"), [sem("out_stored0"), sem("out_stored1")]
        Z = [S2, G[1]]
        fsum = [nots, left[:, 0:T]]
        TILES = [(hh, tt) for hh in range(2) for tt in range(TT)]
        GROUPS = [(n, g) for n, (hh, tt) in enumerate(TILES) for g in range(tt // 4 + 1)]
        SCORE_READER = {"f": ("dve", "f scores"), "s": ("act", "s not")}

        def groups_of(n):
            return [(c, g) for c, (m, g) in enumerate(GROUPS) if m == n]

        def before(x, i):
            return ("s", i - 1) if x == "f" else ("f", i)

        ATT_COLS = (S_FQ, S_FK, S_FV, S_SQ, S_SK, S_SV)

        def low_part(v, k):
            return v.tensor_tensor(H[1][:, k, :], H[1][:, k, :].bitcast(F32), H[0][:, k, :].bitcast(F32), ALU.subtract)

        def over_features(dst, src):
            for n in range(2):
                mm = nc.tensor.matmul(dst[n], ones, src[:, n * NB:(n + 1) * NB], start=True, stop=True)
            return mm

        def halves_of(pair):
            return [pair[:, 0:NB], pair[:, NB:2 * NB]]

        EARLY = KT - 1

        @block.sync
        def _(sp):
            load_w(J_FL, J_FL % 2, slab(w_in2, S_FL))
            with sp.Fori(0, HEADS) as i:
                for m, c in enumerate(ATT_COLS):
                    load_w(J_ATT + ATT_JOBS * i + m, (J_ATT + m) % 2, dslab(w_in2, i * P + c))
            sp.wait_ge(gemm_done, J_OUT2)
            sp.wait_ge(o_stored, 16 * EARLY)
            for k in range(EARLY):
                sp.dma_start(H[1][:, k, :].bitcast(F32), o_d[k]).then_inc(o_landed, 16)
            loads_of_8(J_OUT2, a["w_out_2"][0])

        @block.gpsimd
        def _(g):
            split(J_FL, J_FL % 2, J_FL // 2 + 1)

            def add_squares(x, i):
                for n in range(2):
                    S.wait(g, "act", f"{x} squares {n}", i)
                s = SQ["fs".index(x)]
                S.mark("pool", f"{x} squares added", g.tensor_tensor(s, s, osq, ALU.add))
            g.wait_ge(gemm_done, J_FL)
            S.mark("pool", "square sums cleared", g.memset(SQ[0], 0.0))
            S.mark("pool", "square sums cleared 2", g.memset(SQ[1], 0.0))
            S.wait(g, "pool", "square sums cleared 2")
            S.enter("pool", "att")
            with g.Fori(0, HEADS) as i:
                for m in range(ATT_JOBS):
                    split(J_ATT + ATT_JOBS * i + m, (J_ATT + m) % 2, i * (ATT_JOBS // 2) + ((J_ATT + m) // 2 + 1))
                    if m == 3:
                        add_squares("f", i)
                add_squares("s", i)
            S.leave("pool", HEADS)
            g.wait_ge(o_landed, 16 * EARLY)
            for k in range(EARLY - 1):
                S.mark("pool", ("heads hi", k), g.tensor_tensor(H[0][:, k, :].rearrange("p (c t) -> p c t", t=P), H[1][:, k, :].bitcast(F32).rearrange("p (c t) -> p c t", t=P), ones.unsqueeze(1).to_broadcast([P, KT, P]), ALU.mult))
                S.wait(g, "pool", ("heads hi", k))
                S.mark("pool", ("heads lo", k), low_part(g, k))
            splits_of(J_OUT2)

        @block.tensor
        def _(pe):
            S.wait(pe, "dve", "out squares")
            S.mark("pe", "out summed", over_features(halves_of(S2), bs[:, 1, :]))
            S.mark("pe", "out scaled summed", over_features(halves_of(G[1]), bs[:, 0, :]))
            gemm(J_FL, J_FL % 2, H, pair=U2)
            S.wait(pe, "dve", "mean2 half")

            def job(i, x, m):
                y, turn = before(x, i)
                freed = {0: (SCORE_READER[y][0], f"{SCORE_READER[y][1]} 15", turn), 1: ("dve", f"{y} out 15", turn), 2: ("dve", f"{x} q", i)}[m]
                mm = m + (3 if x == "s" else 0)
                gemm(J_ATT + ATT_JOBS * i + mm, (J_ATT + mm) % 2, H, freed, pair=G[(1, 0, 1)[m]])

            def scores(i, x, n):
                hh, tt = TILES[n]
                z, w = Z[n % 2], (tt + 1) * P
                if n == 0:
                    S.wait(pe, "dve", f"{x} k low 1", i)
                    S.wait(pe, "act", f"{x} k high 1", i)
                elif n == 1:
                    S.wait(pe, "dve", f"{x} vT", i)
                else:
                    S.wait(pe, SCORE_READER[x][0], f"{SCORE_READER[x][1]} {n - 2}", i)
                for b in range((w + NB - 1) // NB):
                    cols = slice(b * NB, min(w, (b + 1) * NB))
                    for q in (Qh[hh], Ql[hh]):
                        pe.matmul(z[:, cols], q[:, tt * P:(tt + 1) * P], Ks[hh][:, cols], start=q is Qh[hh], stop=q is Ql[hh] and tt // 4 != b)
                mm = pe.matmul(z[:, tt * P:w], identb, maskb[:, "fs".index(x), :], start=False, stop=True)
                S.mark("pe", f"{x} z {n}", mm)

            def turned(i, x, n):
                maker, made = ("act", f"f probs {n}") if x == "f" else ("dve", f"s probs {n}")
                for c, g in groups_of(n):
                    reader, read = ("act", "dve")[c % 2], f"{x} v {c}" if c < 2 else f"{x} pT {c - 2}"
                    if g == 0 and reader == maker:
                        S.wait_last(pe, maker, (made, read), i)
                    else:
                        if g == 0:
                            S.wait(pe, maker, made, i)
                        S.wait(pe, reader, read, i)
                    tt = TILES[n][1]
                    for b in range(4 * g, min(4 * g + 4, tt + 1)):
                        mm = pe.transpose(U[c % 2][:, (b % 4) * P:(b % 4 + 1) * P], pr[n % 2][:, b * P:(b + 1) * P], ident)
                    S.mark("pe", f"{x} turned {c}", mm)

            def values(i, x, n):
                hh, tt = TILES[n]
                if n >= 2 and groups_of(n)[0][0] % 2 == 0:
                    S.wait(pe, "dve", f"{x} out {n - 2}", i)
                elif n == 0:
                    S.wait(pe, "dve", f"{x} v 1", i)
                for c, g in groups_of(n):
                    S.wait(pe, ("act", "dve")[c % 2], f"{x} pT {c}", i)
                    for b in range(4 * g, min(4 * g + 4, tt + 1)):
                        mm = pe.matmul(G[0][:, (n % 2) * NB:(n % 2) * NB + P], pT[c % 2][:, b % 4, :], av[:, b, :],
                                       start=b == 0, stop=b == tt)
                    S.mark("pe", f"{x} values {c}", mm)

            S.enter("pe", "att")
            with pe.Fori(0, HEADS) as i:
                for x in "fs":
                    if x == "f":
                        job(i, x, 0)
                    job(i, x, 1)
                    job(i, x, 2)
                    scores(i, x, 0)
                    scores(i, x, 1)
                    for n in range(2):
                        S.wait(pe, "dve", f"{before(x, i)[0]} outT {n}", before(x, i)[1])
                        for b in range(4):
                            mm = pe.transpose(U[n][:, b * P:(b + 1) * P], avT[:, (4 * n + b) * P:(4 * n + b + 1) * P], ident)
                        S.mark("pe", f"{x} v turned {n}", mm)
                    for n in range(len(TILES)):
                        if n == len(TILES) - 1 and x == "f":
                            job(i, "s", 0)
                        turned(i, x, n)
                        if n + 2 < len(TILES):
                            scores(i, x, n + 2)
                        values(i, x, n)
                    S.wait(pe, "dve", f"{x} out {len(TILES) - 1}", i)
                    last = len(GROUPS) - 1
                    S.wait(pe, "act", f"{x} pT {last - last % 2}", i)
                    for n in range(2):
                        for b in range(4):
                            mm = pe.transpose(U[n][:, b * P:(b + 1) * P], ON[:, 4 * n + b, :], ident)
                        S.mark("pe", f"{x} outT {n}", mm)
            S.leave("pe", HEADS)
            S.wait(pe, "pool", "s squares added", HEADS - 1)
            S.mark("pe", "fox squares summed", over_features(halves_of(S2), SQ[0]))
            S.wait(pe, "dve", "s outT 1", HEADS - 1)
            S.mark("pe", "sb squares summed", over_features(U, SQ[1]))
            S.wait(pe, "pool", ("heads lo", EARLY - 2))
            S.wait(pe, "dve", ("heads lo", EARLY - 1))
            S.enter("pe", "out2")
            with pe.Fori(0, KT // 2) as i:
                for m in range(2):
                    pe.wait_ge(w_ready, J_OUT2 + 2 * i + m + 1)
                    freed = ("out2 sb 0", i) if m else ("out2 sb 1", i - 1)
                    S.wait(pe, "dve", *freed)
                    S.mark("pe", f"out2 fox {m}", passes((J_OUT2 + m) % 2, H, range(HEADS), G[0]))
                    passes((J_OUT2 + m) % 2, H, range(HEADS, KT), G[1]).then_inc(gemm_done, 1)
            S.leave("pe", KT // 2)

        @block.scalar
        def _(act):
            S.wait(act, "pe", "out summed")
            S.mark("act", "root1", act.activation(R1, S2, ACT.Sqrt, scale=1.0 / D, bias=epsc))
            S.wait(act, "dve", "mean2")
            S.mark("act", "root2", act.activation(SC, bs[:, 1, :], ACT.Sqrt, scale=1.0 / D, bias=epsc))
            S.wait(act, "dve", "f projected")
            g8, l8 = pr[0][0:S_HEADS, :], pr[1][0:S_HEADS, :]
            S.mark("act", "f logit", act.activation(g8, qt[0:S_HEADS, :], ACT.Identity, bias=fbias[0:S_HEADS, :]))
            S.wait(act, "act", "f logit")
            S.mark("act", "f abs", act.activation(l8, g8, ACT.Abs))
            S.wait(act, "act", "f abs")
            S.mark("act", "f exp", act.activation(l8, l8, ACT.Exp, scale=-1.0))
            S.wait(act, "act", "f exp")
            S.mark("act", "f ln", act.activation(l8, l8, ACT.Ln, bias=1.0))
            S.wait(act, "dve", "forget sums")
            act.dma_start(nf_d, nots[0:S_HEADS, :]).then_inc(nf_stored, 16)
            act.wait_ge(nf_stored, 16)
            S.enter("act", "att")
            with act.Fori(0, HEADS) as i:
                def high_parts(x, part):
                    S.wait(act, "dve", f"{x} {part}", i)
                    for hh in range(2):
                        own, other = slice(HD * hh, HD * hh + HD), slice(HD - HD * hh, P - HD * hh)
                        if part == "q":
                            act.activation(Qh[hh][other, :], qt[own, :], ACT.Copy)
                        dst = Qh[hh] if part == "q" else Ks[hh]
                        S.mark("act", f"{x} {part} high {hh}", act.activation(dst[own, :], qt[own, :], ACT.Copy))

                def chain(x, n):
                    hh, tt = TILES[n]
                    w = (tt + 1) * P
                    if x == "f":
                        S.wait(act, "dve", f"f scores {n}", i)
                        S.mark("act", f"f probs {n}", act.activation(pr[n % 2][:, 0:w], pr[n % 2][:, 0:w], ACT.Exp, scale=-1.0,
                                                                     bias=mn[:, n % 2, :], accum_out=rs[:, n % 4, :]))
                    else:
                        S.wait(act, "pe", f"s z {n}", i)
                        S.mark("act", f"s taken {n}", act.activation(pr[n % 2][:, 0:w], Z[n % 2][:, 0:w], ACT.Sigmoid))
                        if n:
                            S.wait(act, "dve", f"s left {n - 1}", i)
                        S.mark("act", f"s not {n}", act.activation(nots[:, 0:w], Z[n % 2][:, 0:w], ACT.Sigmoid, scale=-1.0))

                def copy_turned(x, n):
                    for c, g in groups_of(n):
                        if c % 2 == 0:
                            w = min(4, TILES[n][1] + 1 - 4 * g)
                            S.wait(act, "pe", f"{x} turned {c}", i)
                            S.mark("act", f"{x} pT {c}", act.activation(pT[0][:, 0:w, :], U[0][:, 0:w * P].rearrange("p (b t) -> p b t", t=P), ACT.Copy))

                for x in "fs":
                    if x == "f":
                        S.wait(act, "dve", "s probs 15", i - 1)
                        for hh in range(2):
                            act.dma_start(fsum[hh], nf_d[bass.ds(2 * i + hh, 1), :].to_broadcast([P, T])).then_inc(nf_landed, 16)
                    if x == "f":
                        high_parts(x, "q")
                    high_parts(x, "k")
                    if x == "s":
                        S.wait(act, "dve", "f scores 15", i)
                    chain(x, 0)
                    S.wait(act, "pe", f"{x} v turned 0", i)
                    S.mark("act", f"{x} v 0", act.activation(av[:, 0:4, :], U[0].rearrange("p (b t) -> p b t", t=P), ACT.Copy))
                    for n in range(len(TILES)):
                        if n + 1 < len(TILES):
                            chain(x, n + 1)
                        copy_turned(x, n)
                    if x == "f":
                        high_parts("s", "q")
                    for n in range(2):
                        S.wait(act, "pe", f"{x} outT {n}", i)
                        if n == 0:
                            S.wait(act, "pool", *((f"s squares added", i - 1) if x == "f" else ("f squares added", i)))
                        S.mark("act", f"{x} squares {n}", act.activation(osq[:, n * NB:(n + 1) * NB], U[n], ACT.Square))
                    S.wait(act, "dve", f"{x} outT 1", i)
                    act.dma_start(row(o_d, i + HEADS * "fs".index(x)), OT).then_inc(o_stored, 16)
                act.wait_ge(o_stored, 32 * i + 32)
            S.leave("act", HEADS)
            for k, src in ((EARLY - 1, H[1][:, EARLY - 1, :].bitcast(F32)), (KT - 1, OT)):
                if k == EARLY - 1:
                    act.wait_ge(o_landed, 16 * EARLY)
                S.mark("act", ("heads hi", k), act.activation(H[0][:, k, :], src, ACT.Copy))
            S.wait(act, "pe", "fox squares summed")
            S.mark("act", "fox root", act.activation(gs[:, 0, :], S2, ACT.Sqrt, scale=2.0 / D, bias=epsc))
            S.wait(act, "pe", "sb squares summed")
            for n in range(2):
                S.mark("act", f"sb root {n}", act.activation(gs[:, 1, n * NB:(n + 1) * NB], U[n], ACT.Sqrt, scale=2.0 / D, bias=epsc))
            S.enter("act", "out2")
            with act.Fori(0, KT // 2) as i:
                for m in range(2):
                    k = 2 * i + m
                    S.wait(act, "dve", f"out2 job {m}", i)
                    settle(act, i)
                    S.mark("act", f"out2 square {m}", act.activation(bs[:, 1, :], tile2(X2, k), ACT.Square))
                    S.wait(act, "dve", f"out2 operand {m}", i)
                    settle(act, i)
                    S.mark("act", f"out2 hi {m}", act.activation(tile2(A[0], k), tile2(A[1], k).bitcast(F32), ACT.Copy))
            S.leave("act", KT // 2)
            act.wait_ge(o_stored, 16 * KT)

        @block.vector
        def _(v):
            def do(name, ins):
                S.mark("dve", name, ins)
                return name

            S.wait(v, "act", "root1")
            do("rstd1", v.reciprocal(R1, R1))
            S.wait(v, "dve", "rstd1")
            S.wait(v, "pe", "out scaled summed")
            do("mean2 half", v.tensor_tensor(bs[:, 1, :], G[1], R1, ALU.mult))
            S.wait(v, "dve", "mean2 half")
            do("mean2", v.tensor_tensor(bs[:, 1, :], bs[:, 1, :], R1, ALU.mult))
            S.wait(v, "act", "root2")
            do("rstd2", v.reciprocal(SC, SC))
            S.wait(v, "dve", "rstd2")
            do("rstd12", v.tensor_tensor(SC, SC, R1, ALU.mult))
            S.wait(v, "dve", "rstd12")
            v.wait_ge(gemm_done, J_FL + 1)
            do("f projected", v.tensor_tensor(qt[0:S_HEADS, :], U2[0:S_HEADS, :], SC[0:S_HEADS, :], ALU.mult))
            g8, l8, F8 = pr[0][0:S_HEADS, :], pr[1][0:S_HEADS, :], nots[0:S_HEADS, :]
            S.wait(v, "act", "f ln")
            do("forget logs", v.scalar_tensor_tensor(g8, g8, 0.0, l8, ALU.min, ALU.subtract))
            S.wait(v, "dve", "forget logs")
            do("forget sums", v.tensor_tensor_scan(F8, g8, g8, 0.0, ALU.add, ALU.bypass))
            do("left all", v.memset(left[:, T:T + 1], 1.0))
            S.enter("dve", "att")
            with v.Fori(0, HEADS) as i:
                def me(name):
                    S.wait(v, "dve", name, i)

                def chain(x, n):
                    hh, tt = TILES[n]
                    w = (tt + 1) * P
                    p = pr[n % 2][:, 0:w]
                    if x == "f":
                        S.wait(v, "pe", f"f z {n}", i)
                        if n == 0:
                            v.wait_ge(nf_landed, 32 * i + 32)
                        settle(v, i)
                        do(f"f scores {n}", v.tensor_tensor_reduce(out=p, in0=fsum[hh][:, 0:w], in1=Z[n % 2][:, 0:w], scale=1.0, scalar=1e30,
                                                                   op0=ALU.add, op1=ALU.min, accum_out=mn[:, n % 2, :]))
                    else:
                        S.wait(v, "act", f"s not {n}", i)
                        if n:
                            me(f"s probs {n - 1}")
                        do(f"s left {n}", v.tensor_tensor_scan(left[:, T - w:T][:, ::-1], nots[:, 0:w][:, ::-1], nots[:, 0:w], 1.0, ALU.mult, ALU.bypass))
                        me(f"s left {n}")
                        do(f"s probs {n}", v.tensor_tensor(p, p, left[:, T - w + 1:T + 1], ALU.mult))

                def copy_turned(x, n):
                    for c, g in groups_of(n):
                        if c % 2 == 1:
                            w = min(4, TILES[n][1] + 1 - 4 * g)
                            S.wait(v, "pe", f"{x} turned {c}", i)
                            do(f"{x} pT {c}", v.tensor_copy(pT[1][:, 0:w, :], U[1][:, 0:w * P].rearrange("p (b t) -> p b t", t=P)))

                def out_of(x, n):
                    hh, tt = TILES[n]
                    src, dst = G[0][:, (n % 2) * NB + HD * hh:(n % 2) * NB + HD * hh + HD], ON[:, tt, HD * hh:HD * hh + HD]
                    if x == "f":
                        S.wait(v, "act", f"f probs {n}", i)
                        do(f"f sums {n}", v.reciprocal(rs[:, n % 4, :], rs[:, n % 4, :]))
                        me(f"f sums {n}")
                    S.wait(v, "pe", f"{x} values {groups_of(n)[-1][0]}", i)
                    do(f"{x} out {n}", v.tensor_scalar(dst, src, rs[:, n % 4, :], None, ALU.mult) if x == "f" else v.tensor_copy(dst, src))

                def project(x, m):
                    jj = J_ATT + ATT_JOBS * i + (m + (3 if x == "s" else 0) + 1)
                    if m == 0:
                        S.wait(v, "dve", f"{before(x, i)[0]} k low 1", before(x, i)[1])
                    elif m == 1:
                        me(f"{x} q low 1")
                    v.wait_ge(gemm_done, jj)
                    by = float(HD) ** -0.5 * (-1 if x == "f" else 1) if m == 0 else 1.0
                    do(f"{x} {('q', 'k', 'vT')[m]}", v.scalar_tensor_tensor(avT if m == 2 else qt, G[(1, 0, 1)[m]], by, SC, ALU.mult, ALU.mult))

                def low_parts(x, m):
                    for hh in range(2):
                        own, other = slice(HD * hh, HD * hh + HD), slice(HD - HD * hh, P - HD * hh)
                        S.wait(v, "act", f"{x} {'qk'[m]} high {hh}", i)
                        high = (Qh, Ks)[m][hh][own, :].bitcast(F32)
                        if m == 0:
                            v.tensor_tensor(Ql[hh][own, :], qt[own, :], high, ALU.subtract)
                        do(f"{x} {'qk'[m]} low {hh}", v.tensor_tensor((Ql, Ks)[m][hh][other, :], qt[own, :], high, ALU.subtract))

                for x in "fs":
                    if x == "f":
                        project(x, 0)
                    low_parts(x, 0)
                    project(x, 1)
                    low_parts(x, 1)
                    project(x, 2)
                    chain(x, 0)
                    if x == "f":
                        chain(x, 1)
                    S.wait(v, "pe", f"{x} v turned 1", i)
                    do(f"{x} v 1", v.tensor_copy(av[:, 4:8, :], U[1].rearrange("p (b t) -> p b t", t=P)))
                    for n in range(len(TILES)):
                        if x == "s" and n + 1 < len(TILES):
                            chain(x, n + 1)
                        if x == "f" and n == len(TILES) - 1:
                            out_of(x, n - 1)
                            project("s", 0)
                        copy_turned(x, n)
                        if n and not (x == "f" and n == len(TILES) - 1):
                            out_of(x, n - 1)
                        if x == "f" and n + 2 < len(TILES):
                            chain(x, n + 2)
                    out_of(x, len(TILES) - 1)
                    for n in range(2):
                        S.wait(v, "act", f"{x} squares {n}", i)
                        if n == 0 and x == "s":
                            v.wait_ge(o_stored, 32 * i + 16)
                        do(f"{x} outT {n}", v.tensor_scalar(OT[:, n * NB:(n + 1) * NB], U[n], par[:, bass.ds(i + (R0["fg"] + HEADS * "fs".index(x)), 1)], None, ALU.mult))
                for m in range(2):
                    k = 2 * i + m
                    do(f"x2 normed {m}", v.scalar_tensor_tensor(tile2(X2, k), tile2(X2, k), par[:, bass.ds(k + R0["f1"], 1)], R1, ALU.mult, ALU.mult))
            S.leave("dve", HEADS)
            for k, src in ((KT - 1, OT), (EARLY - 1, None)):
                S.wait(v, "act", ("heads hi", k))
                do(("heads lo", k), low_part(v, k) if src is None else v.tensor_tensor(H[1][:, k, :], src, H[0][:, k, :].bitcast(F32), ALU.subtract))
            S.wait(v, "act", "fox root")
            do("fox rstd", v.reciprocal(gs[:, 0, :], gs[:, 0, :]))
            S.wait(v, "act", "sb root 1")
            do("sb rstd", v.reciprocal(gs[:, 1, :], gs[:, 1, :]))
            S.wait(v, "dve", "sb rstd")
            S.mark("dve", "out2 zero", v.memset(S2, 0.0))
            S.wait(v, "dve", "out2 zero")
            S.enter("dve", "out2")
            with v.Fori(0, KT // 2) as i:
                def me(name):
                    S.wait(v, "dve", name, i)
                for m in range(2):
                    k = 2 * i + m
                    S.wait(v, "pe", f"out2 fox {m}", i)
                    do(f"out2 fox {m}", v.tensor_tensor(bs[:, 0, :], G[0], gs[:, 0, :], ALU.mult))
                    me(f"out2 fox {m}")
                    do(f"out2 fox added {m}", v.tensor_tensor(tile2(X2, k), tile2(X2, k), bs[:, 0, :], ALU.add))
                    me(f"out2 fox added {m}")
                    v.wait_ge(gemm_done, J_OUT2 + k + 1)
                    do(f"out2 sb {m}", v.tensor_tensor(bs[:, 0, :], G[1], gs[:, 1, :], ALU.mult))
                    me(f"out2 sb {m}")
                    do(f"out2 job {m}", v.tensor_tensor(tile2(X2, k), tile2(X2, k), bs[:, 0, :], ALU.add))
                    me(f"out2 job {m}")
                    do(f"out2 operand {m}", v.tensor_scalar(tile2(A[1], k).bitcast(F32), tile2(X2, k), par[:, bass.ds(k + R0["fn"], 1)], None, ALU.mult))
                    S.wait(v, "act", f"out2 square {m}", i)
                    do(f"out2 sum {m}", v.tensor_tensor(S2, S2, bs[:, 1, :], ALU.add))
                    S.wait(v, "act", f"out2 hi {m}", i)
                    do(f"out2 lo {m}", v.tensor_tensor(tile2(A[1], k), tile2(A[1], k).bitcast(F32), tile2(A[0], k).bitcast(F32), ALU.subtract))
                    me(f"out2 lo {m}")
            S.leave("dve", KT // 2)
            do("out2 squares", v.tensor_copy(bs[:, 0, :], S2))

        w_up, w_down = a["w_up_2"][0], a["w_down_2"][0]

        def ffn_jobs():
            j = J_FFN
            for g, (f0, nf) in enumerate(FFN_GROUPS):
                yield g, f0, nf, j, j + 2 * nf
                j += 2 * nf + KT

        @block.sync
        def _(sp):
            for g, f0, nf, up, down in ffn_jobs():
                with sp.Fori(0, nf) as f:
                    for m in range(2):
                        load_w(up + 2 * f + m, (up + m) % 2, dslab(w_up, f * P + (f0 * P + m * DFF)))
                loads_of_8(down, w_down, nf, f0 * P)
            for t in range(TT):
                for h in range(2):
                    S.wait(sp, ("act", "dve")[h], f"staged {t}")
                sp.dma_start(out[0, t * P:(t + 1) * P, :], (gs, bs)[t % 2][:, 1, :]).then_inc(out_stored[t % 2], 16)
            for s in range(2):
                sp.wait_ge(out_stored[s], 16 * TT // 2)

        @block.gpsimd
        def _(g_):
            for g, f0, nf, up, down in ffn_jobs():
                splits_of(up, pairs=nf)
                splits_of(down, kt=nf)

        @block.tensor
        def _(pe):
            S.wait(pe, "dve", "out2 squares")
            S.mark("pe", "out2 summed", over_features(halves_of(S2), bs[:, 0, :]))
            for g, f0, nf, up, down in ffn_jobs():
                if g:
                    for m in range(2):
                        S.wait(pe, "dve", f"down{g - 1} job {m}", KT // 2 - 1)
                S.enter("pe", f"up{g}")
                with pe.Fori(0, nf) as f:
                    for m in range(2):
                        gemm(up + 2 * f + m, (up + m) % 2, A, ("dve", f"up{g} normed {m}", f - 1))
                S.leave("pe", nf)
                S.wait(pe, "dve", f"up{g} lo", nf - 1)
                products_of_8(f"down{g}", down, H, nf)
            norm_pe("down2")
            for t in range(TT):
                for h in range(2):
                    if t:
                        S.wait(pe, ("act", "dve")[h], f"staged {t - 1}")
                    for b in range(4):
                        k = 4 * h + b
                        if t == 0:
                            S.wait(pe, "dve", ("x4 scaled", k))
                        mm = pe.transpose(U[h][:, b * P:(b + 1) * P], X2[:, k, t * P:(t + 1) * P], ident)
                    S.mark("pe", f"out turned {t} {h}", mm)

        @block.scalar
        def _(act):
            S.wait(act, "pe", "out2 summed")
            S.mark("act", "out2 root", act.activation(bs[:, 1, :], S2, ACT.Sqrt, scale=1.0 / D, bias=epsc))
            for g, f0, nf, up, down in ffn_jobs():
                if g:
                    S.wait(act, "dve", f"down{g - 1} job 1", KT // 2 - 1)
                S.enter("act", f"up{g}")
                with act.Fori(0, nf) as f:
                    for m in range(2):
                        S.wait(act, "dve", f"up{g} normed {m}", f)
                        settle(act, f)
                        S.mark("act", f"up{g} tap {m}", act.activation(gs[:, m, :], bs[:, 0, :], ACT.Identity, bias=conv_col(0, f + (f0 + m * FT)), scale=conv_col(3, f + (f0 + m * FT))))
                        if m == 0:
                            S.wait(act, "dve", f"up{g} conv 0", f)
                            S.mark("act", f"up{g} silu", act.activation(gs[:, 0, :], gs[:, 0, :], ACT.Silu))
                    S.wait(act, "dve", f"up{g} act", f)
                    settle(act, f)
                    S.mark("act", f"up{g} hi", act.activation(tile2(H[0], f), tile2(H[1], f).bitcast(F32), ACT.Copy))
                S.leave("act", nf)
                residual_act(f"down{g}", [], squares=g == len(FFN_GROUPS) - 1)
            S.wait(act, "pe", "down2 summed")
            S.mark("act", "down2 root", act.activation(gs[:, 0, :], S2, ACT.Sqrt, scale=1.0 / D, bias=epsc))
            for t in range(TT):
                S.wait(act, "pe", f"out turned {t} 0")
                if t >= 2:
                    act.wait_ge(out_stored[t % 2], 16 * (t // 2))
                S.mark("act", f"staged {t}", act.activation((gs, bs)[t % 2][:, 1, 0:NB], U[0], ACT.Copy))

        @block.vector
        def _(v):
            def do(name, ins):
                S.mark("dve", name, ins)
                return name
            S.wait(v, "act", "out2 root")
            do("out2 rstd", v.reciprocal(bs[:, 1, :], bs[:, 1, :]))
            S.wait(v, "dve", "out2 rstd")
            for g, f0, nf, up, down in ffn_jobs():
                S.enter("dve", f"up{g}")
                with v.Fori(0, nf) as f:
                    for m in range(2):
                        k = f + (f0 + m * FT)
                        y, u = gs[:, m, :], bs[:, 0, :]
                        v.wait_ge(gemm_done, up + 2 * f + m + 1)
                        if m == 0:
                            S.wait(v, "dve", f"up{g} act", f - 1)
                        else:
                            S.wait(v, "dve", f"up{g} conv 0", f)
                        do(f"up{g} normed {m}", v.tensor_tensor(u, G[(up + m) % 2], bs[:, 1, :], ALU.mult))
                        S.wait(v, "act", f"up{g} tap {m}", f)
                        do(f"up{g} near {m}", v.scalar_tensor_tensor(y[:, 1:T], u[:, 0:T - 1], conv_col(2, k), y[:, 1:T], ALU.mult, ALU.add))
                        S.wait(v, "dve", f"up{g} near {m}", f)
                        do(f"up{g} conv {m}", v.scalar_tensor_tensor(y[:, 2:T], u[:, 0:T - 2], conv_col(1, k), y[:, 2:T], ALU.mult, ALU.add))
                    S.wait(v, "act", f"up{g} silu", f)
                    S.wait(v, "dve", f"up{g} conv 1", f)
                    do(f"up{g} act", v.tensor_tensor(tile2(H[1], f).bitcast(F32), gs[:, 0, :], gs[:, 1, :], ALU.mult))
                    S.wait(v, "act", f"up{g} hi", f)
                    do(f"up{g} lo", v.tensor_tensor(tile2(H[1], f), tile2(H[1], f).bitcast(F32), tile2(H[0], f).bitcast(F32), ALU.subtract))
                S.leave("dve", nf)
                residual_dve(f"down{g}", down, squares=g == len(FFN_GROUPS) - 1)
            S.wait(v, "act", "down2 root")
            do("down2 rstd", v.reciprocal(gs[:, 0, :], gs[:, 0, :]))
            S.wait(v, "dve", "down2 rstd")
            for k in range(KT):
                do(("x4 scaled", k), v.scalar_tensor_tensor(X2[:, k, :], X2[:, k, :], col("fin", k), gs[:, 0, :], ALU.mult, ALU.mult))
            for t in range(TT):
                S.wait(v, "pe", f"out turned {t} 1")
                if t >= 2:
                    v.wait_ge(out_stored[t % 2], 16 * (t // 2))
                do(f"staged {t}", v.tensor_copy((gs, bs)[t % 2][:, 1, NB:D], U[1]))

        @block.scalar
        def _(act):
            for engine in ("act", "dve"):
                act.wait_ge(S.settled[engine], S.n[engine, "settled"])
    return S.at


INPUTS = ("x", "c", "ctx", "c_ctx", "w_mod", "b_mod", "norm_g", "w_in", "w_gate_up_f", "b_gate_f", "w_gate_up_b",
          "b_gate_b", "gla_norm_g", "w_pool", "pool_scale", "w_branch_a", "w_branch_b", "w_out", "final_norm_g", "attn_norm_g_2",
          "w_in_2", "forget_bias_2", "fox_out_g_2", "sb_out_g_2", "w_out_2", "ffn_norm_g_2", "w_up_2", "conv_w_2",
          "conv_b_2", "w_down_2", "final_norm_g_2")


def constants():
    t = np.arange(T)
    i = np.arange(P)
    j = i[:, None]
    levels = np.stack([((j // (2 * s)) == (i // (2 * s))) & ((j % (2 * s) < s) != (i % (2 * s) < s)) for s in LEVELS], 1)
    nf = DK // 4
    freqs = np.power(np.float32(10000.0), -np.arange(nf, dtype=np.float32) / nf).astype(np.float32)
    pos = np.where(i[:, None] < DK // 2, (t // GRID_W)[None], (t % GRID_W)[None]).astype(np.float32)
    angle = (pos * freqs[i % nf][:, None]).astype(np.float32).astype(np.float64)
    sign = np.where(i % (2 * nf) < nf, -1.0, 1.0)[:, None]
    half = np.array([1, 2, 4, 8])[:, None]
    count = np.clip(t + half, 0, T) - np.clip(t - half, 0, T)
    inv = np.broadcast_to((1.0 / count)[:, None, :], (4, P, T))
    mask = np.where(i[None, :] > j, np.float32(1e30), 0.0)
    strict = np.where(i[None, :] >= j, np.float32(-1e30), 0.0)
    return {
        "identity": np.eye(P, dtype=np.float32),
        "causal": np.stack([mask, strict], 1).astype(np.float32),
        "levels": levels.astype(np.float32),
        "cos": np.cos(angle).astype(np.float32),
        "sin": (np.sin(angle) * sign).astype(np.float32),
        "inv_count": np.ascontiguousarray(inv).astype(np.float32),
    }


def kernel(**inputs):
    import concourse.bacc as bacc
    from concourse.bass_utils import run_bass_kernel_spmd as run

    arrays = {n: np.ascontiguousarray(value) for n, value in [(n, inputs[n]) for n in INPUTS] + list(constants().items())}

    def write_down(known):
        nc = bacc.Bacc("TRN2", target_bir_lowering=False, num_devices=1)
        aps = {n: nc.dram_tensor(n, value.shape, mybir.dt.from_np(value.dtype), kind="ExternalInput").ap() for n, value in arrays.items()}
        out = nc.dram_tensor("out", (1, T, D), F32, kind="ExternalOutput").ap()
        return nc, program(nc, aps, out, known)
    _, steps = write_down({})
    nc, _ = write_down(steps)
    return run(nc, [arrays], core_ids=[0]).results[0]["out"]
```

```python
import numpy as np
import concourse.bass as bass
from concourse import mybir

F32 = mybir.dt.float32
F32R = mybir.dt.float32r
BF16 = mybir.dt.bfloat16
U8 = mybir.dt.uint8
ALU = mybir.AluOpType
ACT = mybir.ActivationFunctionType
AX = mybir.AxisListType

P = 128
D = 1024
KT = D // P
T = 1024
TT = T // P
TC = 256
NB = 512
EPS = 1e-6
HEADS, DK, DV = 4, 128, 256
RANK = 16
GATE_NORM = 16.0
GRID_W = 64
CH = 128
POOL_WINDOWS = (2, 4, 8, 16)
LEVELS = (64, 32, 16, 8, 4, 2, 1)
C_Q, C_K, C_V, C_ZA = 0, 512, 1024, 2048
C_LR, C_UB, C_ZB, C_GA, C_GB = 3072, 3104, 4128, 5152, 6176
HD = 64
S_HEADS = 8
S_FQ, S_FK, S_FV, S_FL, S_SQ, S_SK, S_SV = 0, 512, 1024, 1536, 1544, 2056, 2568
DFF = 2816
FT = DFF // P

R0 = dict(c=0, cc=8, ng=16, bm=24, bgf=48, bgb=52, gg=56, ps=58, ag=66, fg=74, sg=78, fn=82, fin=90, f1=98)
R0_ROWS = 106
R1_ROWS = 88
R2_ROWS = 88

CTX_JOBS = 13
PRE_JOBS = [("ctx", 0), ("ctx", 1)]
for _n in range(24):
    PRE_JOBS.append(("pool", _n))
    _ctx = sum(kind == "ctx" for kind, _ in PRE_JOBS)
    if _n not in (4, 10) and _ctx < CTX_JOBS:
        PRE_JOBS.append(("ctx", _ctx))
J_LR = len(PRE_JOBS)
J_GLA = J_LR + 1
GLA_JOBS = 10
J_BRB = J_GLA + HEADS * GLA_JOBS
J_BRA = J_BRB + KT
J_OUT = J_BRA + KT
J_FL = J_OUT + KT
J_ATT = J_FL + 1
ATT_JOBS = 6
J_OUT2 = J_ATT + 4 * ATT_JOBS
J_FFN = J_OUT2 + KT
FFN_GROUPS = ((0, 8), (8, 8), (16, 6))



class Steps:

    def __init__(self, known):
        self.known, self.at, self.n, self.loop, self.sems = known, {}, {}, {}, {}

    def start(self, nc, names):
        self.sems = {n: nc.alloc_semaphore(f"{n}_steps") for n in names}
        self.n = dict.fromkeys(names, 0) | {(n, "settled"): 0 for n in names}
        self.settled = {n: nc.alloc_semaphore(f"{n}_waits_taken") for n in ("act", "dve")}

    def mark(self, engine, name, ins):
        ins.then_inc(self.sems[engine], 1)
        self.n[engine] += 1
        key = (engine, name)
        assert key not in self.at, key
        self.at[key] = (self.n[engine], self.loop.get(engine))
        return ins

    def value(self, engine, name, turn=None):
        table = self.at if (engine, name) in self.at else self.known
        if (engine, name) not in table:
            assert not self.known, (engine, name)
            return 1
        n, loop = table[engine, name]
        if loop is None:
            return n
        before, per = self.known.get(loop, (0, 1))
        return before + (n - before) + turn * per

    def wait(self, eng, engine, name, turn=None):
        eng.wait_ge(self.sems[engine], self.value(engine, name, turn))

    def wait_last(self, eng, engine, names, turn=None):
        self.wait(eng, engine, max(names, key=lambda name: self.value(engine, name, 0)), turn)

    def settle(self, engine, eng):
        eng.sem_inc(self.settled[engine], 1)
        self.n[engine, "settled"] += 1

    def enter(self, engine, name):
        self.loop[engine] = ("loop", engine, name)
        self.before = self.n[engine]
        self.before_settled = self.n[engine, "settled"]

    def leave(self, engine, turns):
        per = self.n[engine] - self.before
        self.at[self.loop[engine]] = (self.before, per)
        self.n[engine] += (turns - 1) * per
        self.n[engine, "settled"] += (turns - 1) * (self.n[engine, "settled"] - self.before_settled)
        self.loop[engine] = None


def program(nc, a, out, known):
    base = (nc.sbuf_base + 31) // 32 * 32
    KB = 1024
    END = 229344 - base

    def sb(name, off, shape, dt=F32):
        return nc.alloc_sbuf_tensor_at(name, shape, dt, offset=base + off)[tuple(slice(None) for _ in shape)]

    H = [sb("H_hi", 0, [P, KT, T], F32R), sb("H_lo", 32 * KB, [P, KT, T], F32R)]
    w_raw = sb("w_raw", 64 * KB, [P, 2, KT, P])
    w_hi = sb("w_hi", 72 * KB, [P, 2, KT, P], F32R)
    w_lo = sb("w_lo", 80 * KB, [P, 2, KT, P], F32R)
    C0 = 88 * KB
    par = sb("par", C0, [P, R0_ROWS + R1_ROWS + R2_ROWS])
    ident = sb("ident", C0 + 1152, [P, P])
    ones = sb("ones", C0 + 1664, [P, P])
    lvl = sb("lvl", C0 + 2176, [P, len(LEVELS), P], U8)
    mod = sb("mod", C0 + 3072, [P, 24, 2])
    gsc = sb("gsc", C0 + 3264, [P, KT, 2])
    identb = sb("identb", C0 + 3328, [P, P], BF16)
    maskb = sb("maskb", C0 + 3584, [P, 2, P], BF16)
    fbias = sb("fbias", C0 + 4096, [P, 1])
    epsc = sb("epsc", C0 + 4128, [P, 1])
    gains = sb("gains", C0 + 4160, [P, KT])
    W0 = C0 + 4192

    def col(name, i=0):
        return par[:, R0[name] + i:R0[name] + i + 1]

    def conv_col(which, i):
        o = R0_ROWS + which * (2 * FT) + i
        return par[:, bass.ds(o, 1)]

    G = [nc.alloc_psum_tensor(f"G{s}", [P, 2 * NB], F32)[:, :] for s in range(2)]
    S2 = nc.alloc_psum_tensor("S2", [P, 2 * NB], F32)[:, :]
    U2 = nc.alloc_psum_tensor("U2", [P, 2 * NB], F32)[:, :]
    U = [U2[:, 0:NB], U2[:, NB:2 * NB]]

    def scratch(name, shape):
        return nc.dram_tensor(name, shape, F32, kind="Internal").ap()

    xT_d, s0_d = scratch("xT_d", (KT, P, T)), scratch("s0_d", (HEADS, 2, P, DV))
    a_d, b_d = scratch("a_d", (KT, P, T)), scratch("b_d", (KT, P, T))
    sga_d, sgb_d = scratch("sga_d", (KT, P, T)), scratch("sgb_d", (KT, P, T))
    o_d = scratch("o_d", (KT, P, T))

    sem = nc.alloc_semaphore
    w_landed = [sem("w_landed0"), sem("w_landed1")]
    w_hi_made, w_ready, gemm_done = sem("w_hi_made"), sem("w_ready"), sem("gemm_done")
    S = Steps(known)
    S.start(nc, ("pe", "act", "dve", "pool"))
    engines = {"pe": nc.tensor, "act": nc.scalar, "dve": nc.vector, "pool": nc.gpsimd}

    def passes(slot, mov, tiles, dst, n_cols=T, late=None):
        hi, lo = mov
        halves = [(n, min(NB, n_cols - n * NB)) for n in range((n_cols + NB - 1) // NB)]
        for k in tiles:
            if late and k == tiles[-1]:
                S.wait(nc.tensor, *late)
            for w, m, first, last in ((w_hi, hi, k == tiles[0], False), (w_hi, lo, False, False),
                                      (w_lo, hi, False, k == tiles[-1])):
                for n, c in halves:
                    mm = nc.tensor.matmul(dst[:, n * NB:n * NB + c], w[:, slot, k, :], m[:, k, n * NB:n * NB + c],
                                          start=first, stop=last)
        return mm

    def gemm(j, slot, mov, freed=None, n_cols=T, kt=KT, pair=None, last=None):
        pe = nc.tensor
        pe.wait_ge(w_ready, j + 1)
        if freed:
            S.wait(pe, *freed)
        passes(slot, mov, range(kt), G[slot] if pair is None else pair, n_cols, last).then_inc(gemm_done, 1)

    def load_w(j, slot, src, kt=KT, first=False):
        if not first:
            nc.sync.wait_ge(w_ready, j - 1)
        nc.sync.dma_start(w_raw[:, slot, 0:kt, :], src).then_inc(w_landed[slot], 16)

    def split_hi(eng, j, slot, landed, kt=KT, first=False):
        eng.wait_ge(w_landed[slot], 16 * landed)
        if not first:
            eng.wait_ge(gemm_done, j - 1)
        dst, src = w_hi[:, slot, 0:kt, :], w_raw[:, slot, 0:kt, :]
        i = eng.activation(dst, src, ACT.Copy) if eng is nc.scalar else \
            eng.tensor_tensor(dst, src, ones.unsqueeze(1).to_broadcast([P, kt, P]), ALU.mult)
        i.then_inc(w_hi_made, 1)

    def split_lo(j, slot, kt=KT):
        nc.gpsimd.wait_ge(w_hi_made, j + 1)
        nc.gpsimd.tensor_tensor(w_lo[:, slot, 0:kt, :], w_raw[:, slot, 0:kt, :],
                                w_hi[:, slot, 0:kt, :].bitcast(F32), ALU.subtract).then_inc(w_ready, 1)

    def split(j, slot, landed, kt=KT):
        split_hi(nc.gpsimd, j, slot, landed, kt)
        split_lo(j, slot, kt)

    def slab(w, c0, kt=KT, r0=0):
        return w[r0:r0 + kt * P, c0:c0 + P].rearrange("(k p) c -> p k c", p=P)

    def settle(eng, turn=None):
        S.settle({nc.scalar: "act", nc.vector: "dve"}[eng], eng)

    def barrier(engine, n):
        eng = engines[engine]
        S.mark(engine, f"phase {n} ended", eng.drain())
        for other in ("pe", "act", "dve"):
            S.wait(eng, other, f"phase {n} ended")

    def after_phase(eng, n):
        for other in ("pe", "act", "dve"):
            S.wait(eng, other, f"phase {n} ended")

    w_in, w_mod = a["w_in"][0], a["w_mod"][0]

    o = W0
    def take(name, shape, dt=F32, size=None):
        nonlocal o
        at = o
        n = int(np.prod(shape[1:])) * {F32: 4, F32R: 4, BF16: 2, U8: 1}[dt]
        o = (o + n + 31) // 32 * 32
        assert o <= END, (name, o, END)
        return sb(name, at, shape, dt)

    xT = take("xT", [P, KT, T])
    wm = take("wm", [P, 2, KT, NB])
    cT = take("cT", [P, KT, TC])
    hc = [take("hc_hi", [P, KT, TC], F32R), take("hc_lo", [P, KT, TC], F32R)]
    x_in = take("x_in", [P, 2, D])
    sq = take("sq", [P, 2, T])
    rb = take("rb", [P, T + TC])
    prow = take("prow", [P, 3, P])
    silc = take("silc", [P, 16])
    lvl_in = take("levels_in", [P, len(LEVELS), P])
    mask_in = take("masks_in", [P, 2, P])
    o = W0
    lrc = take("lrc", [P, TC])
    wup = take("wup", [P, 2, HEADS * DK])
    smask = take("smask", [P, T], BF16)
    kc = take("kc", [P, T])
    vcT = take("vcT", [P, 2, 2, TC])
    vc = take("vc", [P, 2, HEADS * DV])
    c_g = [take("c_gf", [P, T + 8]), take("c_gb", [P, T + 8])]
    c_l = [take("c_lf", [P, T]), take("c_lb", [P, T])]
    c_F = [take("c_F", [P, T]), take("c_X", [P, T])]
    c_k = [take("c_kf", [P, T]), kc]
    c_t = take("c_t", [P, 2, 8])
    d_mov = [take("pooled_hi", [P, 2, T], F32R)]
    pw = sb("pool_work", o, [P, 2, T])
    d_mov.append(take("pooled_lo", [P, 2, T], F32R))
    inv = take("inv_count", [P, T])
    assert o <= W0 + 72 * KB, o
    o = W0 + 72 * KB
    c_kn = [take("c_kfT", [P, 8, P]), take("c_kbT", [P, 8, P])]
    o = W0 + 88 * KB
    c_S = take("c_S", [P, HEADS, 2, DV])
    PAD = 8
    u_in = take("pool_in", [P, T + PAD])
    cs = take("pool_sums", [P, T + 2 * PAD + 1])
    pz = take("silu_zB", [P, 2, T])

    par_landed, const_landed = sem("params_landed"), sem("constants_landed")
    x_landed, wm_landed = [sem("x_landed0"), sem("x_landed1")], [sem("wm_landed0"), sem("wm_landed1")]
    xT_stored, s0_stored, cpar_landed = sem("xT_stored"), sem("s0_stored"), sem("ctx_params_landed")

    def ctx_col(j):
        return C_LR if j == 0 else C_K + (j - 1) * P if j < 5 else C_V + (j - 5) * P

    POOL_PARTS = ("u0", "u1", "z0", "z1", "p0", "p1")
    inv_landed, b_stored = sem("inv_landed"), sem("b_stored")

    def pool_job(n):
        return n // len(POOL_PARTS), POOL_PARTS[n % len(POOL_PARTS)]

    def pre_src(kind, n):
        if kind == "ctx":
            return slab(w_in, ctx_col(n)), KT
        g, what = pool_job(n)
        m = int(what[1])
        if what[0] == "p":
            return a["w_pool"][0, g][:, m * P:(m + 1) * P].rearrange("(k p) c -> p k c", p=P), 2
        return slab(w_in, (C_UB if what[0] == "u" else C_ZB) + (2 * g + m) * P), KT

    def pre_reader(kind, n):
        if kind == "ctx":
            return "act", ("ctx job", n)
        return "dve" if pool_job(n)[1][0] == "p" else "act", ("pool job", n)

    def rows(v):
        return v.rearrange("(r c) -> r c", c=P)

    def broadcast(ap, n):
        return ap.to_broadcast([ap.shape[0], ap.shape[1], n])

    def chunks(v, n=8):
        return v.rearrange("p (c t) -> p c t", c=n)

    def chunk_mask(dst, name):
        g = nc.gpsimd
        S.mark("pool", f"{name} ones", g.memset(dst, 1.0))
        S.wait(g, "pool", f"{name} ones")
        S.mark("pool", name, g.memset(chunks(dst)[:, :, 0:1], 0.0))

    with nc.Block() as block:
        @block.sync
        def _(sp):
            vectors = (("c", a["c"][0]), ("cc", a["c_ctx"]), ("ng", a["norm_g"][0]), ("bm", a["b_mod"][0]),
                       ("bgf", a["b_gate_f"][0]), ("bgb", a["b_gate_b"][0]), ("gg", a["gla_norm_g"][0]),
                       ("ps", a["pool_scale"][0]), ("ag", a["attn_norm_g_2"][0]), ("fg", a["fox_out_g_2"][0]),
                       ("sg", a["sb_out_g_2"][0]), ("fn", a["ffn_norm_g_2"][0]), ("fin", a["final_norm_g_2"]), ("f1", a["final_norm_g"]))
            for name, src in vectors:
                sp.dma_start(prow[R0[name]:R0[name] + src.shape[0] // P, 0, :], rows(src)).then_inc(par_landed, 16)
            cw = a["conv_w_2"][0]
            for row, g, src in ((0, 1, a["conv_b_2"][0]), (44, 1, cw[0]), (0, 2, cw[1]), (44, 2, cw[2])):
                sp.dma_start(prow[row:row + 44, g, :], rows(src)).then_inc(par_landed, 16)
            sp.dma_start(ident, a["identity"]).then_inc(par_landed, 16)
            tiles = [a["ctx"][0, t * P:(t + 1) * P, :] for t in range(2)] + \
                    [a["x"][0, t * P:(t + 1) * P, :] for t in range(TT)]

            def load_tile(t):
                if t >= 2:
                    S.wait(sp, "pe", ("turned", t - 2, 1))
                sp.dma_start(x_in[:, t % 2, :], tiles[t]).then_inc(x_landed[t % 2], 16)

            def load_mod(q):
                if q >= 2:
                    S.wait(sp, "pe", ("modulation", q - 2))
                sp.dma_start(wm[:, q % 2, :, :], w_mod[:, q * NB:(q + 1) * NB].rearrange("(k p) c -> p k c", p=P))\
                    .then_inc(wm_landed[q % 2], 16)
            load_tile(0)
            load_tile(1)
            load_mod(0)
            for t in range(2, 6):
                load_tile(t)
            load_mod(1)
            for t in range(6, 10):
                load_tile(t)
            load_mod(2)
            load_mod(3)
            for j in range(2):
                load_w(j, j, slab(w_in, ctx_col(j)), first=True)
            load_mod(4)
            load_mod(5)
            sp.dma_start(lvl_in, a["levels"]).then_inc(const_landed, 16)
            sp.dma_start(mask_in, a["causal"]).then_inc(const_landed, 16)
            sp.dma_start(fbias[0:S_HEADS, :], a["forget_bias_2"].rearrange("a h -> h a")).then_inc(const_landed, 16)
            after_phase(sp, 1)
            sp.wait_ge(const_landed, 48)
            S.wait(sp, "pool", "gate weights cleared")
            sp.dma_start(wup[0:RANK, 0, :], a["w_gate_up_f"][0]).then_inc(cpar_landed, 16)
            sp.dma_start(wup[RANK:2 * RANK, 1, :], a["w_gate_up_b"][0]).then_inc(cpar_landed, 16)
            for j, (kind, n) in enumerate(PRE_JOBS):
                if j < 2:
                    continue
                src, kt = pre_src(kind, n)
                load_w(j, j % 2, src, kt)
                if kind == "pool" and n % 6 in (0, 4):
                    g = n // 6 + (n % 6 == 4)
                    if n % 6 == 4 and g < 4:
                        S.wait(sp, "dve", ("pooled", g - 1, 1))
                    if g < 4 and (n == 0 or n % 6 == 4):
                        sp.dma_start(inv, a["inv_count"][g]).then_inc(inv_landed, 16)

        @block.gpsimd
        def _(g):
            S.mark("pool", "ones made", g.memset(ones, 1.0))
            S.mark("pool", "eps made", g.memset(epsc, EPS))
            split_lo(0, 0)
            split_lo(1, 1)
            after_phase(g, 1)
            S.mark("pool", "ctx low rank cleared", g.memset(lrc, 0.0))
            S.mark("pool", "gate weights cleared", g.memset(wup, 0.0))
            chunk_mask(smask, "chunk mask")
            for j, (kind, n) in enumerate(PRE_JOBS):
                if j >= 2:
                    split(j, j % 2, j // 2 + 1, pre_src(kind, n)[1])

        @block.tensor
        def _(pe):
            pe.wait_ge(par_landed, 16 * 19)
            for g, (n, at) in enumerate(((R0_ROWS, 0), (R1_ROWS, R0_ROWS), (R2_ROWS, R0_ROWS + R1_ROWS))):
                mm = pe.transpose(G[1][:, at:at + n], prow[0:n, g, :], ident[0:n, 0:n])
            S.mark("pe", "parameters turned", mm)

            def turn(t):
                pe.wait_ge(x_landed[t % 2], 16 * (t // 2 + 1))
                for h in range(2):
                    if t >= 1:
                        S.wait(pe, "act" if h == 0 else "dve", ("turned copied", t - 1))
                    for i in range(4):
                        mm = pe.transpose(U[h][:, i * P:(i + 1) * P], x_in[:, t % 2, (4 * h + i) * P:(4 * h + i + 1) * P], ident)
                    S.mark("pe", ("turned", t, h), mm)

            def modulation(q):
                pe.wait_ge(wm_landed[q % 2], 16 * (q // 2 + 1))
                if q == 0:
                    S.wait(pe, "act", "silu made")
                for m in range(4):
                    c = (NB if q < 4 else 0) + (4 * q + m) * 2
                    for k in range(KT):
                        mm = pe.matmul(G[1][:, c:c + 2], wm[:, q % 2, k, m * P:(m + 1) * P], silc[:, k:16:8],
                                       start=k == 0, stop=k == KT - 1)
                S.mark("pe", ("modulation", q), mm)
            turn(0)
            turn(1)
            modulation(0)
            for t in range(2, 6):
                turn(t)
            modulation(1)
            for t in range(6, 10):
                turn(t)
            S.wait(pe, "pool", "ones made")
            S.wait(pe, "act", ("turned copied", 9))
            for k in range(KT):
                S.wait(pe, "act", ("ctx squares", k // 4))
                mm = pe.matmul(U[0][:, 0:TC], ones, sq[:, k // 4, (k % 4) * TC:(k % 4 + 1) * TC], start=k == 0, stop=k == KT - 1)
                if k % 4 == 3:
                    S.mark("pe", ("ctx squares summed", k // 4), mm)
            for k in range(KT):
                S.wait(pe, "act", ("squares", k))
                for n in range(2):
                    mm = pe.matmul(S2[:, n * NB:(n + 1) * NB], ones, sq[:, k % 2, n * NB:(n + 1) * NB], start=k == 0, stop=k == KT - 1)
                S.mark("pe", ("squares summed", k), mm)
            modulation(2)
            modulation(3)
            for j in range(2):
                if j == 0:
                    S.wait(pe, "dve", ("scaled", "c", KT - 1))
                    gemm(0, 0, hc, n_cols=TC)
            modulation(4)
            modulation(5)
            barrier("pe", 1)
            gemm(1, 1, hc, n_cols=TC)
            def ctx_gates(d):
                if d == 0:
                    S.wait(pe, "act", ("ctx job", 0))
                    pe.wait_ge(cpar_landed, 32)
                for hh in range(2):
                    if d:
                        S.wait(pe, "act", ("ctx gates", 0, hh))
                    for h in range(2):
                        w = wup[:, d, (2 * hh + h) * DK:(2 * hh + h + 1) * DK]
                        mm = pe.matmul(U[hh][:, h * TC:(h + 1) * TC], w, lrc, start=True, stop=True)
                    S.mark("pe", ("ctx gates", d, hh), mm)

            def turn_values(i):
                S.wait(pe, "act", ("ctx job", 6 + 2 * i))
                S.wait(pe, *(("act", ("ctx gates", 1, i)) if i < 2 else ("dve", ("vc", i - 2))))
                for c in range(2):
                    for m in range(2):
                        mm = pe.transpose(U[i % 2][:, (2 * c + m) * P:(2 * c + m + 1) * P], vcT[:, i % 2, m, c * P:(c + 1) * P], ident)
                S.mark("pe", ("vc turned", i), mm)
            def turn_keys(d):
                S.wait(pe, "dve", ("ctx keys", d))
                for h in range(2):
                    S.wait(pe, *(("dve", ("vc", 2 + h)) if d == 0 else ("act", ("ctx keys turned", 0, h))))
                    for i in range(4):
                        mm = pe.transpose(U[h][:, i * P:(i + 1) * P], c_k[d][:, (4 * h + i) * P:(4 * h + i + 1) * P], ident)
                    S.mark("pe", ("ctx keys turned", d, h), mm)

            def updates(d):
                for h in range(HEADS):
                    S.wait(pe, "act", ("ctx keys turned", d, h // 2))
                    if d == 0 and h < 2:
                        S.wait(pe, "act", ("ctx keys turned", 1, h))
                    else:
                        S.wait(pe, "dve", ("ctx state", d - (h < 2), (h - 2) % 4))
                    for c in range(2):
                        mm = pe.matmul(U[h % 2][:, c * DV:(c + 1) * DV], c_kn[d][:, 2 * h + c, :], vc[:, c, h * DV:(h + 1) * DV], start=True, stop=True)
                    S.mark("pe", ("ctx updates", d, h), mm)
            for j, (kind, n) in enumerate(PRE_JOBS):
                if j < 2:
                    continue
                if kind == "pool" and n % 6 == 4:
                    S.wait(pe, "dve", ("pooled lo", n // 6, 1))
                mov = hc if kind == "ctx" else d_mov if n % 6 >= 4 else H
                gemm(j, j % 2, mov, pre_reader(*PRE_JOBS[j - 2]), n_cols=TC if kind == "ctx" else T, kt=pre_src(kind, n)[1])
                if kind == "pool":
                    if n in (0, 1):
                        ctx_gates(n)
                    elif n in (7, 9, 12, 14):
                        turn_values((7, 9, 12, 14).index(n))
                    elif n in (15, 16):
                        turn_keys(n - 15)
                    elif n in (18, 20):
                        updates((n - 18) // 2)
            barrier("pe", 2)

        @block.scalar
        def _(act):
            S.wait(act, "pe", "parameters turned")
            S.mark("act", "parameters", act.activation(par, G[1][:, 0:R0_ROWS + R1_ROWS + R2_ROWS], ACT.Copy))
            S.wait(act, "act", "parameters")
            S.mark("act", "silu made", act.activation(silc, par[:, 0:16], ACT.Silu))
            for t in range(10):
                S.wait(act, "pe", ("turned", t, 0))
                dst = cT[:, 0:4, t * P:(t + 1) * P] if t < 2 else xT[:, 0:4, (t - 2) * P:(t - 1) * P]
                S.mark("act", ("turned copied", t), act.activation(dst, U[0].rearrange("p (i t) -> p i t", i=4), ACT.Copy))
            S.wait(act, "act", ("turned copied", 9))
            S.wait(act, "dve", ("turned copied", 9))
            for i in range(2):
                S.mark("act", ("ctx squares", i), act.activation(sq[:, i, :].rearrange("p (k t) -> p k t", k=4), cT[:, 4 * i:4 * i + 4, :], ACT.Square))
            for k in range(KT):
                S.wait(act, "pe", ("ctx squares summed", k) if k < 2 else ("squares summed", k - 2))
                S.mark("act", ("squares", k), act.activation(sq[:, k % 2, :], xT[:, k, :], ACT.Square))
            S.wait(act, "pe", ("ctx squares summed", 1))
            S.wait(act, "pool", "eps made")
            S.mark("act", "ctx root", act.activation(rb[:, T:T + TC], U[0][:, 0:TC], ACT.Sqrt, scale=1.0 / D, bias=epsc))
            S.wait(act, "pe", ("squares summed", KT - 1))
            S.mark("act", "root", act.activation(rb[:, 0:T], S2, ACT.Sqrt, scale=1.0 / D, bias=epsc))
            for i, (kind, k) in enumerate([("c", k) for k in range(KT)] + [("x", k) for k in range(KT)]):
                S.wait(act, "dve", ("normed", kind, k))
                n, hi, m = (TC, hc[0], 1) if kind == "c" else (T, H[0], 0)
                S.mark("act", ("hi", kind, k), act.activation(hi[:, k, :], sq[:, i % 2, 0:n], ACT.Identity, bias=mod[:, k, m:m + 1]))
                if i == 1:
                    for j in range(2):
                        split_hi(act, j, j, 1, first=True)
            act.dma_start(xT_d.rearrange("k p t -> p k t"), xT).then_inc(xT_stored, 16)
            act.wait_ge(xT_stored, 16)
            barrier("act", 1)

            def evac(j, kind, n):
                act.wait_ge(gemm_done, j + 1)
                if kind == "ctx":
                    src = G[j % 2][:, 0:TC]
                    if n == 0:
                        src, dst = src[0:2 * RANK], lrc[0:2 * RANK]
                        S.wait(act, "pool", "ctx low rank cleared")
                    elif n < 5:
                        dst = kc[:, (n - 1) * TC:n * TC]
                    else:
                        i = n - 5
                        if i >= 4:
                            S.wait(act, "pe", ("vc turned", i // 2 - 2))
                        dst = vcT[:, (i // 2) % 2, i % 2, :]
                    S.mark("act", ("ctx job", n), act.activation(dst, src, ACT.Copy))
                elif pool_job(n)[1][0] == "u":
                    g, m = n // 6, n % 6
                    if n:
                        S.wait(act, "dve", ("pooled", *((g, 0) if m else (g - 1, 1))))
                    S.mark("act", ("pool job", n), act.activation(u_in[:, 0:T], G[j % 2], ACT.Copy))
                else:
                    if n >= 6:
                        act.wait_ge(b_stored, 32 * (n // 6))
                    S.mark("act", ("pool job", n), act.activation(pz[:, n % 6 - 2, :], G[j % 2], ACT.Silu))

            def gates_with_bias(d):
                for hh in range(2):
                    S.wait(act, "pe", ("ctx gates", d, hh))
                    for h in range(2):
                        head = 2 * hh + h
                        i = act.activation(c_g[d][:, d + head * TC:d + (head + 1) * TC], U[hh][:, h * TC:(h + 1) * TC],
                                           ACT.Identity, bias=col("bgb" if d else "bgf", head))
                    S.mark("act", ("ctx gates", d, hh), i)

            def gate_logs():
                S.wait(act, "act", ("ctx gates", 1, 1))
                for d in range(2):
                    i = act.activation(c_l[d], c_g[d][:, d:d + T], ACT.Abs)
                S.mark("act", "ctx gates abs", i)
                S.wait(act, "act", "ctx gates abs")
                for d in range(2):
                    i = act.activation(c_l[d], c_l[d], ACT.Exp, scale=-1.0)
                S.mark("act", "ctx gates exp", i)
                S.wait(act, "act", "ctx gates exp")
                for d in range(2):
                    S.mark("act", ("ctx gate logs", d), act.activation(c_l[d], c_l[d], ACT.Ln, bias=1.0))
            for j, (kind, n) in enumerate(PRE_JOBS):
                if kind == "ctx" or n % 6 < 4:
                    evac(j, kind, n)
                else:
                    S.wait(act, "dve", ("pool job", n))
                    act.dma_start(b_d[2 * (n // 6) + n % 6 - 4], pz[:, n % 6 - 4, :]).then_inc(b_stored, 16)
                if kind == "pool":
                    if n in (0, 1):
                        gates_with_bias(n)
                    if n == 1:
                        gate_logs()
                    elif n == 3:
                        S.wait(act, "dve", "ctx scans")
                        S.mark("act", ("ctx exps", 0), act.activation(c_l[0], c_l[0], ACT.Exp, scale=1.0 / GATE_NORM))
                        S.mark("act", ("ctx exps", 1), act.activation(c_l[1], c_F[1], ACT.Exp, scale=1.0 / GATE_NORM))
                        S.mark("act", "ctx totals", act.activation(c_t, c_t, ACT.Exp, scale=1.0 / GATE_NORM))
                    elif n in (15, 16):
                        d = n - 15
                        for h in range(2):
                            S.wait(act, "pe", ("ctx keys turned", d, h))
                            S.mark("act", ("ctx keys turned", d, h), act.activation(c_kn[d][:, 4 * h:4 * h + 4, :], U[h].rearrange("p (i t) -> p i t", i=4), ACT.Copy))
            act.wait_ge(b_stored, 16 * KT)
            S.wait(act, "dve", ("ctx state", 1, 3))
            act.dma_start(s0_d.rearrange("h d p v -> p h d v"), c_S).then_inc(s0_stored, 16)
            act.wait_ge(s0_stored, 16)
            barrier("act", 2)

        @block.vector
        def _(v):
            for t in range(10):
                S.wait(v, "pe", ("turned", t, 1))
                dst = cT[:, 4:8, t * P:(t + 1) * P] if t < 2 else xT[:, 4:8, (t - 2) * P:(t - 1) * P]
                S.mark("dve", ("turned copied", t), v.tensor_copy(dst, U[1].rearrange("p (i t) -> p i t", i=4)))
            S.wait(v, "act", "parameters")
            S.wait(v, "pe", ("modulation", 3))
            S.mark("dve", "shift, scale", v.tensor_tensor(mod[:, 0:16, :], G[1][:, NB:NB + 32].rearrange("p (m c) -> p m c", c=2),
                                                          broadcast(par[:, R0["bm"]:R0["bm"] + 16].unsqueeze(2), 2), ALU.add))
            S.wait(v, "dve", "shift, scale")
            S.mark("dve", "norm scales", v.scalar_tensor_tensor(gsc, mod[:, 8:16, :], 1.0, broadcast(par[:, R0["ng"]:R0["ng"] + KT].unsqueeze(2), 2), ALU.add, ALU.mult))
            for kind in ("c", "x"):
                r = rb[:, T:T + TC] if kind == "c" else rb[:, 0:T]
                S.wait(v, "act", "ctx root" if kind == "c" else "root")
                S.mark("dve", ("rstd", kind), v.reciprocal(r, r))
            S.wait(v, "dve", ("rstd", "x"))
            i = 0
            for kind in ("c", "x"):
                n, src, hi, lo, m, r = (TC, cT, *hc, 1, rb[:, T:T + TC]) if kind == "c" else (T, xT, *H, 0, rb[:, 0:T])
                for k in range(KT):
                    t = sq[:, i % 2, 0:n]
                    if i == 0:
                        S.wait(v, "pe", ("squares summed", KT - 1))
                    if i >= 2:
                        S.wait(v, "dve", ("scaled", *(("c" if i - 2 < KT else "x"), (i - 2) % KT)))
                    S.mark("dve", ("normed", kind, k), v.scalar_tensor_tensor(t, src[:, k, :], gsc[:, k, m:m + 1], r, ALU.mult, ALU.mult))
                    S.wait(v, "act", ("hi", kind, k))
                    S.mark("dve", ("scaled", kind, k), v.scalar_tensor_tensor(lo[:, k, :], t, mod[:, k, m:m + 1], hi[:, k, :].bitcast(F32), ALU.add, ALU.subtract))
                    i += 1
            S.wait(v, "pe", ("modulation", 5))
            S.mark("dve", "gate", v.tensor_tensor(mod[:, 16:24, :], G[1][:, 32:48].rearrange("p (m c) -> p m c", c=2),
                                                  broadcast(par[:, R0["bm"] + 16:R0["bm"] + 24].unsqueeze(2), 2), ALU.add))
            v.wait_ge(const_landed, 48)
            S.mark("dve", "gains", v.tensor_tensor(gains, par[:, R0["f1"]:R0["f1"] + KT], par[:, R0["ag"]:R0["ag"] + KT], ALU.mult))
            for name, dst, src in (("levels", lvl, lvl_in), ("masks", maskb, mask_in), ("identity", identb, ident)):
                S.mark("dve", name, v.tensor_copy(dst, src))
            barrier("dve", 1)
            def do(name, ins):
                S.mark("dve", name, ins)
                S.wait(v, "dve", name)

            def decay_sums():
                S.wait(v, "pool", "chunk mask")
                for d in range(2):
                    S.wait(v, "act", ("ctx gate logs", d))
                    S.mark("dve", ("ctx logs", d), v.scalar_tensor_tensor(c_g[d][:, d:d + T], c_g[d][:, d:d + T], 0.0, c_l[d], ALU.min, ALU.subtract))
                S.wait(v, "dve", ("ctx logs", 1))
                S.mark("dve", "ctx last logs", v.tensor_copy(c_t[:, 1, :].unsqueeze(2), chunks(c_g[1][:, 1:T + 1])[:, :, CH - 1:CH]))
                S.wait(v, "dve", "ctx last logs")
                S.mark("dve", "ctx starts", v.memset(chunks(c_g[1][:, 0:T])[:, :, 0:1], 0.0))
                S.wait(v, "dve", "ctx starts")
                for d in range(2):
                    i = v.tensor_tensor_scan(c_F[d], smask, c_g[d][:, 0:T], 0.0, ALU.mult, ALU.add)
                S.mark("dve", "ctx sums", i)
                S.wait(v, "dve", "ctx sums")
                S.mark("dve", "ctx ends f", v.tensor_copy(c_t[:, 0, :].unsqueeze(2), chunks(c_F[0])[:, :, CH - 1:CH]))
                S.mark("dve", "ctx ends b", v.tensor_tensor(c_t[:, 1, :].unsqueeze(2), c_t[:, 1, :].unsqueeze(2), chunks(c_F[1])[:, :, CH - 1:CH], ALU.add))
                S.mark("dve", "ctx scans", v.tensor_tensor(chunks(c_l[0]), broadcast(chunks(c_F[0])[:, :, CH - 1:CH], CH), chunks(c_F[0]), ALU.subtract))

            def copy_values(i):
                S.wait(v, "pe", ("vc turned", i))
                S.mark("dve", ("vc", i), v.tensor_copy(vc[:, :, i * DV:(i + 1) * DV], U[i % 2].rearrange("p (c m) -> p c m", c=2)))

            def states(d):
                if d == 0:
                    S.wait(v, "act", "ctx totals")
                for h in range(HEADS):
                    S.wait(v, "pe", ("ctx updates", d, h))
                    far, near = (0, 1) if d == 0 else (1, 0)
                    u = U[h % 2]
                    S.mark("dve", ("ctx far", d, h), v.tensor_copy(c_S[:, h, d, :], u[:, far * DV:(far + 1) * DV]))
                    S.wait(v, "dve", ("ctx far", d, h))
                    S.mark("dve", ("ctx state", d, h), v.scalar_tensor_tensor(
                        c_S[:, h, d, :], c_S[:, h, d, :], c_t[:, d, 2 * h + near:2 * h + near + 1], u[:, near * DV:(near + 1) * DV], ALU.mult, ALU.add))

            v.memset(u_in[:, T:T + PAD], 0.0)
            do("pool pads", v.memset(cs[:, 0:PAD + 1], 0.0))
            for j, (kind, n) in enumerate(PRE_JOBS):
                if kind == "ctx":
                    continue
                g, what = pool_job(n)
                m, half = int(what[1]), POOL_WINDOWS[g] // 2
                if what[0] == "u":
                    S.wait(v, "act", ("pool job", n))
                    do(("pool sums", g, m), v.tensor_tensor_scan(cs[:, PAD + 1:], u_in, u_in, 0.0, ALU.add, ALU.bypass))
                    if g and m == 0:
                        v.wait_ge(gemm_done, PRE_JOBS.index(("pool", n - 1)) + 1)
                    w = pw[:, m, :]
                    do(("pool windows", g, m), v.tensor_tensor(w, cs[:, PAD + half:PAD + half + T], cs[:, PAD - half:PAD - half + T], ALU.subtract))
                    v.wait_ge(inv_landed, 16 * (g + 1))
                    do(("pool means", g, m), v.tensor_tensor(w, w, inv, ALU.mult))
                    do(("pooled", g, m), v.tensor_tensor(w, w, u_in[:, 0:T], ALU.subtract))
                    do(("pooled hi", g, m), v.tensor_copy(d_mov[0][:, m, :], w))
                    do(("pooled lo", g, m), v.tensor_tensor(d_mov[1][:, m, :], w, d_mov[0][:, m, :].bitcast(F32), ALU.subtract))
                elif what[0] == "p":
                    v.wait_ge(gemm_done, j + 1)
                    S.wait(v, "act", ("pool job", n - 2))
                    do(("pool job", n), v.scalar_tensor_tensor(pz[:, m, :], G[j % 2], col("ps", 2 * g + m), pz[:, m, :], ALU.mult, ALU.mult))
                if n == 1:
                    decay_sums()
                elif n == 5:
                    for d in range(2):
                        S.wait(v, "act", ("ctx exps", d))
                        if d == 0:
                            S.wait(v, "act", ("ctx job", 4))
                        do(("ctx keys", d), v.tensor_tensor(c_k[d], kc, c_l[d], ALU.mult))
                elif n in (7, 11, 13, 15):
                    copy_values((7, 11, 13, 15).index(n))
                elif n in (18, 20):
                    states((n - 18) // 2)
            barrier("dve", 2)

        o = W0
        smask3 = take("smask3", [P, T], BF16)
        cos, sin = take("cos_t", [P, T]), take("sin_t", [P, T])
        lr = take("lr", [P, T])
        wuph = take("wup_head", [P, 2, DK])
        K, Q = take("keys", [P, T]), take("queries", [P, T])
        raw, sw = take("raw", [P, T]), take("swapped", [P, T])
        L = [take("sums_f", [P, T + 8]), take("sums_b", [P, T + 8])]
        vT = take("vT", [P, T])
        V = take("V", [P, TT, DV])
        E = [take("exps0", [P, T]), take("exps1", [P, T])]
        X = [take(f"scaled{i}", [P, T]) for i in range(4)]
        probs = take("scores", [P, TT, CH])
        gz = take("silu_zA", [P, 2, T])
        ST = [take("states_f", [P, TT, DV]), take("states_b", [P, TT, DV])]
        KN = [take("keysT_f", [P, TT, P]), take("keysT_b", [P, TT, P])]
        te = take("ends", [P, 2, 8])
        tx = take("end_decays", [P, 2, 8])
        tab_landed, wup_landed, s_landed, swapped = sem("tables_landed"), sem("wup_landed"), sem("states_landed"), sem("swap_landed")
        gate_stored, a_stored = sem("gates_stored"), sem("a_stored")
        PAIRS = len(LEVELS) + 2
        o_T = X[2:4]

        def gla_job(h, i):
            return J_GLA + GLA_JOBS * h + i

        def block_view(t, s):
            v = t.rearrange("p (b u) -> p b u", u=2 * s)
            return v, v[:, :, 0:s], v[:, :, s:2 * s]

        def row(d, k):
            return d[bass.ds(k, 1)].rearrange("k p t -> p (k t)")

        GLA_COLS = (lambda h: C_K + P * h, lambda h: C_Q + P * h, lambda h: C_V + 2 * P * h, lambda h: C_V + 2 * P * h + P,
                    lambda h: C_ZA + 2 * P * h, lambda h: C_ZA + 2 * P * h + P, lambda h: C_GA + 2 * P * h,
                    lambda h: C_GA + 2 * P * h + P, lambda h: C_GB + 2 * P * h, lambda h: C_GB + 2 * P * h + P)

        def dslab(w, c0, kt=KT, r0=0):
            return w[r0:r0 + kt * P, bass.ds(c0, P)].rearrange("(k p) c -> p k c", p=P)

        @block.sync
        def _(sp):
            load_w(J_LR, J_LR % 2, slab(w_in, C_LR))
            after_phase(sp, 2)
            sp.dma_start(cos, a["cos"]).then_inc(tab_landed, 16)
            sp.dma_start(sin, a["sin"]).then_inc(tab_landed, 16)
            S.wait(sp, "pool", "head gate weights cleared")
            with sp.Fori(0, HEADS) as h:
                S.wait(sp, "pe", "gates b1", h - 1)
                sp.dma_start(wuph[0:RANK, 0, :], a["w_gate_up_f"][0][:, bass.ds(h * DK, DK)]).then_inc(wup_landed, 16)
                sp.dma_start(wuph[RANK:2 * RANK, 1, :], a["w_gate_up_b"][0][:, bass.ds(h * DK, DK)]).then_inc(wup_landed, 16)
                for i in range(GLA_JOBS):
                    load_w(gla_job(h, i), i % 2, dslab(w_in, GLA_COLS[i](h)))
                    if i == 5:
                        S.wait(sp, "pe", "o 3", h - 1)
                        for d in range(2):
                            sp.dma_start(ST[d][:, 7 * d, :], s0_d[bass.ds(h, 1), d].rearrange("h p v -> p (h v)")).then_inc(s_landed, 16)

        @block.gpsimd
        def _(g):
            split(J_LR, J_LR % 2, J_LR // 2 + 1)
            after_phase(g, 2)
            S.mark("pool", "low rank cleared", g.memset(lr, 0.0))
            S.mark("pool", "head gate weights cleared", g.memset(wuph, 0.0))
            chunk_mask(smask3, "head chunk mask")
            with g.Fori(0, HEADS) as h:
                for i in range(GLA_JOBS):
                    split(gla_job(h, i), i % 2, J_GLA // 2 + GLA_JOBS // 2 * h + i // 2 + 1)

        @block.tensor
        def _(pe):
            gemm(J_LR, J_LR % 2, H)
            S.wait(pe, "act", "lr")
            pe.wait_ge(tab_landed, 32)
            S.enter("pe", "gla")
            with pe.Fori(0, HEADS) as h:
                def turn_to(dst_free, name, src, blocks):
                    s = turn_to.n % 2
                    turn_to.n += 1
                    S.wait(pe, *dst_free)
                    for i, b in enumerate(blocks):
                        mm = pe.transpose(U[s][:, i * P:(i + 1) * P], src[:, b * P:(b + 1) * P], ident)
                    S.mark("pe", name, mm)
                turn_to.n = 0

                def job(i):
                    freed = {0: ("act", "gate evac 2", h - 1), 1: ("act", "gate evac 3", h - 1), 2: ("act", "raw k", h),
                             3: ("act", "raw q", h), 4: ("act", "vT 0", h), 5: ("act", "vT 1", h), 6: ("act", "zA 0", h),
                             7: ("act", "zA 1", h), 8: ("act", "gate evac 0", h), 9: ("act", "gate evac 1", h)}[i]
                    gemm(gla_job(h, i), i % 2, H, freed)

                def level(w):
                    S.wait(pe, "dve", f"stage {w}", h)
                    S.wait(pe, "dve", f"placed {w - 1}", h)
                    kx, qx = X[2 * (w % 2)], X[2 * (w % 2) + 1]
                    for c in range(TT):
                        mm = pe.matmul(S2[:, c * CH:(c + 1) * CH], kx[:, c * CH:(c + 1) * CH], qx[:, c * CH:(c + 1) * CH], start=True, stop=True)
                    S.mark("pe", f"level {w}", mm)

                job(0)
                pe.wait_ge(wup_landed, 32 * h + 32)
                for d in range(2):
                    if d:
                        job(1)
                    for n in range(2):
                        S.wait(pe, "act", *((f"gates f{n}", h) if d else (f"summed r{n}", h - 1)))
                        S.mark("pe", f"gates {'fb'[d]}{n}", pe.matmul(U[n], wuph[:, d, :], lr[:, n * NB:(n + 1) * NB], start=True, stop=True))
                job(2)
                job(3)
                S.wait(pe, "act", "vT 0", h)
                turn_to(("act", "gates b0", h), "v turned 00", vT, range(0, 4))
                turn_to(("act", "gates b1", h), "v turned 01", vT, range(4, 8))
                job(4)
                S.wait(pe, "act", "vT 1", h)
                turn_to(("act", "V 00", h), "v turned 10", vT, range(0, 4))
                turn_to(("act", "V 01", h), "v turned 11", vT, range(4, 8))
                S.wait(pe, "dve", "stage 0", h)
                for d in range(2):
                    for n in range(2):
                        turn_to(("act", f"V 1{n}" if d == 0 else f"KN 0{n}", h), f"keys turned {d}{n}", X[d], range(4 * n, 4 * n + 4))
                job(5)
                for d in range(2):
                    for i in range(4):
                        S.wait(pe, "act", f"KN {d}1", h)
                        if d == 0 and i < 2:
                            S.wait(pe, "act", f"KN 1{i}", h)
                        else:
                            S.wait(pe, "dve", f"state {d if i >= 2 else 0}{(i - 2) % 4}", h)
                        for n in range(2):
                            c = 2 * i + n if d == 0 else 7 - 2 * i - n
                            mm = pe.matmul(U[i % 2][:, n * DV:(n + 1) * DV], KN[d][:, c, :], V[:, c, :], start=True, stop=True)
                        S.mark("pe", f"updates {d}{i}", mm)
                    if d == 0:
                        job(6)
                S.wait(pe, "dve", "rope q", h)
                S.wait(pe, "dve", "rope k", h)
                for c in range(TT):
                    mm = pe.matmul(S2[:, c * CH:(c + 1) * CH], K[:, c * CH:(c + 1) * CH], Q[:, c * CH:(c + 1) * CH], start=True, stop=True)
                S.mark("pe", "level 0", mm)
                level(1)
                job(7)
                level(2)
                level(3)
                job(8)
                level(4)
                level(5)
                job(9)
                level(6)
                level(7)
                S.wait(pe, "dve", "placed 7", h)
                S.wait(pe, "dve", f"stage {PAIRS - 1}", h)
                for m in range(2):
                    for n in range(2):
                        i = 2 * m + n
                        S.wait(pe, *(("dve", f"state 1{2 + i}", h) if i < 2 else ("act", f"o {i - 2}", h)))
                        for c in range(4 * n, 4 * n + 4):
                            dst = U[n][:, (c % 4) * CH:(c % 4 + 1) * CH]
                            cols, f = slice(c * CH, (c + 1) * CH), slice(m * P, (m + 1) * P)
                            pe.matmul(dst, V[:, c, f], probs[:, c, :], start=True, stop=False)
                            pe.matmul(dst, ST[0][:, c, f], X[0][:, cols], start=False, stop=False)
                            mm = pe.matmul(dst, ST[1][:, c, f], X[1][:, cols], start=False, stop=True)
                        S.mark("pe", f"o {i}", mm)
                S.wait(pe, "dve", "o squares", h)
                for n in range(2):
                    S.wait(pe, "act", f"o {2 + n}", h)
                    mm = pe.matmul(U[n], ones, E[0][:, n * NB:(n + 1) * NB], start=True, stop=True)
                    S.mark("pe", f"o summed {n}", mm)
            S.leave("pe", HEADS)
            barrier("pe", 3)

        @block.scalar
        def _(act):
            act.wait_ge(gemm_done, J_LR + 1)
            S.wait(act, "pool", "low rank cleared")
            S.mark("act", "lr", act.activation(lr[0:2 * RANK, :], G[J_LR % 2][0:2 * RANK, :], ACT.Copy))
            S.enter("act", "gla")
            with act.Fori(0, HEADS) as h:
                def evac(i, name, dst, func=ACT.Copy, **more):
                    act.wait_ge(gemm_done, gla_job(h, i) + 1)
                    S.mark("act", name, act.activation(dst, G[i % 2], func, **more))

                def swap(turn):
                    for q in range(4):
                        src = q ^ 1
                        act.dma_start(sw[32 * q:32 * q + 32, :], raw[32 * src:32 * src + 32, :]).then_inc(swapped, 16)
                evac(0, "raw k", raw)
                S.wait(act, "act", "raw k", h)
                swap(0)
                for d in range(2):
                    b = par[:, bass.ds(h + (R0["bgb"] if d else R0["bgf"]), 1)]
                    for n in range(2):
                        S.wait(act, "pe", f"gates {'fb'[d]}{n}", h)
                        if d == 0 and n == 0:
                            S.wait(act, "dve", "stage 8", h - 1)
                        settle(act, h)
                        S.mark("act", f"gates {'fb'[d]}{n}", act.activation(L[d][:, d + n * NB:d + (n + 1) * NB], U[n], ACT.Identity, bias=b))
                S.wait(act, "act", "gates b1", h)
                S.wait(act, "dve", "o scaled 1", h - 1)
                for d in range(2):
                    i = act.activation(E[d], L[d][:, d:d + T], ACT.Abs)
                S.mark("act", "gates abs", i)
                S.wait(act, "act", "gates abs", h)
                for d in range(2):
                    i = act.activation(E[d], E[d], ACT.Exp, scale=-1.0)
                S.mark("act", "gates exp", i)
                S.wait(act, "act", "gates exp", h)
                for d in range(2):
                    S.mark("act", f"gate logs {d}", act.activation(E[d], E[d], ACT.Ln, bias=1.0))

                S.wait(act, "dve", "rope k", h)
                evac(1, "raw q", raw, scale=float(DK) ** -0.5)
                S.wait(act, "act", "raw q", h)
                swap(1)
                evac(2, "vT 0", vT)
                S.wait(act, "dve", "exponents 0", h)
                i = act.activation(E[0], E[0], ACT.Exp, scale=1.0 / GATE_NORM)
                S.mark("act", "exps 0 0", i)
                S.mark("act", "exps 0 1", act.activation(E[1], L[1][:, 0:T], ACT.Exp, scale=1.0 / GATE_NORM))
                S.mark("act", "end decays", act.activation(tx, te, ACT.Exp, scale=1.0 / GATE_NORM))
                def copy_v(m):
                    for n in range(2):
                        S.wait(act, "pe", f"v turned {m}{n}", h)
                        S.mark("act", f"V {m}{n}", act.activation(V[:, 4 * n:4 * n + 4, m * P:(m + 1) * P], U[n].rearrange("p (c f) -> p c f", f=P), ACT.Copy))
                copy_v(0)
                evac(3, "vT 1", vT)
                copy_v(1)
                for d in range(2):
                    for n in range(2):
                        S.wait(act, "pe", f"keys turned {d}{n}", h)
                        S.mark("act", f"KN {d}{n}", act.activation(KN[d][:, 4 * n:4 * n + 4, :], U[n].rearrange("p (c f) -> p c f", f=P), ACT.Copy))

                def exps(w):
                    for e in range(2):
                        if w < PAIRS - 1 or e == 1:
                            S.wait(act, "dve", f"exponents {w} {e}", h)
                        else:
                            S.wait(act, "dve", f"stage {w - 1}", h)
                        src = L[0][:, 0:T] if w == PAIRS - 1 and e == 0 else E[e]
                        S.mark("act", f"exps {w} {e}", act.activation(E[e], src, ACT.Exp, scale=1.0 / GATE_NORM))
                exps(1)
                evac(4, "zA 0", gz[:, 0, :], ACT.Silu)
                evac(5, "zA 1", gz[:, 1, :], ACT.Silu)

                def gate(i):
                    dst = (raw, sw)[i % 2]
                    if i < 2:
                        S.wait(act, "dve", "rope q", h)
                    else:
                        act.wait_ge(gate_stored, 64 * h + 32)
                    evac(6 + i, f"gate evac {i}", dst, ACT.Sigmoid)
                    S.wait(act, "act", f"gate evac {i}", h)
                    act.dma_start(row((sga_d, sgb_d)[i // 2], 2 * h + i % 2), dst).then_inc(gate_stored, 16)
                exps(2)
                gate(0)
                exps(3)
                exps(4)
                gate(1)
                exps(5)
                exps(6)
                gate(2)
                exps(7)
                exps(8)
                gate(3)
                act.wait_ge(gate_stored, 64 * h + 64)
                for m in range(2):
                    for n in range(2):
                        i = 2 * m + n
                        S.wait(act, "pe", f"o {i}", h)
                        S.mark("act", f"o {i}", act.activation(o_T[m][:, n * NB:(n + 1) * NB], U[n], ACT.Copy))
                for m in range(2):
                    S.wait(act, "act", f"o {2 * m + 1}", h)
                    S.mark("act", f"o squares {m}", act.activation(E[m], o_T[m], ACT.Square))
                for n in range(2):
                    S.wait(act, "pe", f"o summed {n}", h)
                    S.mark("act", f"summed r{n}", act.activation(E[1][:, n * NB:(n + 1) * NB], U[n], ACT.Sqrt, scale=1.0 / DV, bias=epsc))
                S.wait(act, "dve", "o scaled 1", h)
                for m in range(2):
                    act.dma_start(row(a_d, 2 * h + m), o_T[m]).then_inc(a_stored, 16)
                act.wait_ge(a_stored, 32 * h + 32)
            S.leave("act", HEADS)
            barrier("act", 3)

        @block.vector
        def _(v):
            def do(name, ins):
                return S.mark("dve", name, ins)
            v.wait_ge(tab_landed, 32)
            S.wait(v, "pool", "head chunk mask")
            v.wait_ge(const_landed, 48)
            S.enter("dve", "gla")
            with v.Fori(0, HEADS) as h:
                def me(name, turn=None):
                    S.wait(v, "dve", name, h if turn is None else turn)
                def rope(name, n, dst):
                    S.wait(v, "act", f"raw {name}", h)
                    do(f"cos {name}", v.tensor_tensor(dst, raw, cos, ALU.mult))
                    v.wait_ge(swapped, 128 * h + 64 * (n + 1))
                    do(f"sin {name}", v.tensor_tensor(sw, sw, sin, ALU.mult))
                    me(f"sin {name}")
                    do(f"rope {name}", v.tensor_tensor(dst, dst, sw, ALU.add))
                S.wait(v, "pe", "level 0", h - 1)
                rope("k", 0, K)
                for d in range(2):
                    S.wait(v, "act", f"gate logs {d}", h)
                    do(f"logs {d}", v.scalar_tensor_tensor(L[d][:, d:d + T], L[d][:, d:d + T], 0.0, E[d], ALU.min, ALU.subtract))
                me("logs 1")
                do("last logs", v.tensor_copy(te[:, 1, :].unsqueeze(2), chunks(L[1][:, 1:T + 1])[:, :, CH - 1:CH]))
                me("last logs")
                do("starts", v.memset(chunks(L[1][:, 0:T])[:, :, 0:1], 0.0))
                me("starts")
                for d in range(2):
                    i = v.tensor_tensor_scan(L[d][:, 0:T], smask3, L[d][:, 0:T], 0.0, ALU.mult, ALU.add)
                do("sums", i)
                me("sums")
                do("ends f", v.tensor_copy(te[:, 0, :].unsqueeze(2), chunks(L[0][:, 0:T])[:, :, CH - 1:CH]))
                do("ends b", v.tensor_tensor(te[:, 1, :].unsqueeze(2), te[:, 1, :].unsqueeze(2), chunks(L[1][:, 0:T])[:, :, CH - 1:CH], ALU.add))
                F, B = L[0][:, 0:T], L[1][:, 0:T]
                do("exponents 0", v.tensor_tensor(chunks(E[0]), broadcast(chunks(F)[:, :, CH - 1:CH], CH), chunks(F), ALU.subtract))

                rope("q", 1, Q)
                me("rope q")

                def stage(w, first, second):
                    if w >= 2:
                        S.wait(v, "pe", f"level {w - 2}" if w > 2 else "keys turned 11", h)
                    elif w == 0:
                        S.wait(v, "pe", "o 3", h - 1)
                    for e, src in enumerate((first, second)):
                        S.wait(v, "act", f"exps {w} {e}", h)
                        i = v.tensor_tensor(X[2 * (w % 2) + e], src, E[e], ALU.mult)
                        do(f"stage {w}" if e else f"stage {w} k", i)

                def exponents(w):
                    s = LEVELS[w - 1]
                    me(f"stage {w - 1} k")
                    fv, fl, fr = block_view(F, s)
                    bv, bl, br = block_view(B, s)
                    fb, bb = broadcast(fv[:, :, s - 1:s], s), broadcast(bv[:, :, s:s + 1], s)
                    _, kl, kr = block_view(E[0], s)
                    _, ql, qr = block_view(E[1], s)
                    v.tensor_tensor(kl, fb, fl, ALU.subtract)
                    do(f"exponents {w} 0", v.tensor_tensor(kr, br, bb, ALU.subtract))
                    me(f"stage {w - 1}")
                    v.tensor_tensor(ql, bb, bl, ALU.subtract)
                    do(f"exponents {w} 1", v.tensor_tensor(qr, fr, fb, ALU.subtract))

                def place(w):
                    S.wait(v, "pe", f"level {w}", h)
                    s2 = chunks(S2)
                    if w == 0:
                        do("placed 0", v.scalar_tensor_tensor(probs, s2, 2.0, ident.unsqueeze(1).to_broadcast([P, TT, P]), ALU.mult, ALU.mult))
                    else:
                        me(f"placed {w - 1}")
                        settle(v, h)
                        do(f"placed {w}", v.copy_predicated(probs, lvl[:, w - 1, :].unsqueeze(1).to_broadcast([P, TT, P]), s2))
                stage(0, K, K)
                exponents(1)
                v.wait_ge(s_landed, 32 * h + 32)
                S.wait(v, "act", "end decays", h)
                for d in range(2):
                    for i in range(4):
                        S.wait(v, "pe", f"updates {d}{i}", h)
                        for n in range(2):
                            c = 2 * i + n if d == 0 else 7 - 2 * i - n
                            if i == 3 and n == 1:
                                continue
                            to = c + 1 if d == 0 else c - 1
                            if (i, n) != (0, 0):
                                me(f"state {d}{i} {0}" if n else f"state {d}{i - 1}")
                            do(f"state {d}{i}" if n or i == 3 else f"state {d}{i} 0",
                               v.scalar_tensor_tensor(ST[d][:, to, :], ST[d][:, c, :], tx[:, d, c:c + 1], U[i % 2][:, n * DV:(n + 1) * DV], ALU.mult, ALU.add))
                S.wait(v, "act", "gates f0", h)
                stage(1, K, Q)
                S.wait(v, "pe", "o 3", h - 1)
                for w in range(1, len(LEVELS) + 1):
                    if w < len(LEVELS):
                        exponents(w + 1)
                    place(w - 1)
                    if w < len(LEVELS):
                        stage(w + 1, K, Q)
                me(f"stage {PAIRS - 2}")
                do(f"exponents {PAIRS - 1} 1", v.tensor_tensor(chunks(E[1]), broadcast(te[:, 1, :].unsqueeze(2), CH), chunks(B), ALU.subtract))
                place(len(LEVELS))
                stage(PAIRS - 1, Q, Q)
                S.wait(v, "act", "o squares 1", h)
                do("o squares", v.tensor_tensor(E[0], E[0], E[1], ALU.add))
                S.wait(v, "act", "summed r1", h)
                do("o rstd", v.reciprocal(E[1], E[1]))
                me("o rstd")
                for m in range(2):
                    do(f"o normed {m}", v.scalar_tensor_tensor(o_T[m], o_T[m], col("gg", m), E[1], ALU.mult, ALU.mult))
                for m in range(2):
                    me(f"o normed {m}")
                    if m == 0:
                        S.wait(v, "act", "zA 1", h)
                    do(f"o scaled {m}", v.tensor_tensor(o_T[m], o_T[m], gz[:, m, :], ALU.mult))
            S.leave("dve", HEADS)
            barrier("dve", 3)

        o = W0
        A = [take("A_hi", [P, KT, T], F32R), take("A_lo", [P, KT, T], F32R)]
        X2 = take("x2", [P, KT, T])
        gs, bs = take("tiles_in", [P, 2, T]), take("tiles_made", [P, 2, T])

        a_landed, b_landed = sem("a_landed"), sem("b_landed")
        gs_landed = [sem("gs_landed0"), sem("gs_landed1")]
        B_POOL = 4

        def tile2(t, k):
            return t[:, bass.ds(k, 1), :].rearrange("p k t -> p (k t)")

        BRANCHES = (("brb", J_BRB, a["w_branch_b"][0], H), ("bra", J_BRA, a["w_branch_a"][0], A), ("out", J_OUT, a["w_out"][0], H))

        def load_pair(j0, w, i, kt=KT, r0=0):
            for m in range(2):
                load_w(j0 + 2 * i + m, (j0 + m) % 2, dslab(w, (2 * i + m) * P, kt, r0), kt)

        def loads_of_8(j0, w, kt=KT, r0=0, first=0):
            with nc.sync.Fori(first, KT // 2) as i:
                load_pair(j0, w, i, kt, r0)

        def split_pair(j0, i, kt=KT):
            for m in range(2):
                split(j0 + 2 * i + m, (j0 + m) % 2, i + ((j0 + m) // 2 + 1), kt)

        def splits_of(j0, pairs=KT // 2, kt=KT, first=0):
            with nc.gpsimd.Fori(first, pairs) as i:
                split_pair(j0, i, kt)

        def products_of_8(name, j0, mov, kt=KT, last=None):
            S.enter("pe", name)
            with nc.tensor.Fori(0, KT // 2) as i:
                for m in range(2):
                    gemm(j0 + 2 * i + m, (j0 + m) % 2, mov, ("dve", f"{name} job {m}", i - 1), kt=kt, last=last)
            S.leave("pe", KT // 2)

        def low_part(eng, parts, k):
            return eng.tensor_tensor(parts[1][:, k, :], parts[1][:, k, :].bitcast(F32), parts[0][:, k, :].bitcast(F32), ALU.subtract)

        def residual_act(name, first_wait, fetch=None, squares=True):
            act = nc.scalar
            for w in first_wait:
                S.wait(act, *w)
            S.enter("act", name)
            with act.Fori(0, KT // 2) as i:
                for m in range(2):
                    if fetch is not None:
                        S.wait(act, "dve", f"{name} job {m}", i - 1)
                        act.dma_start(gs[:, m, :], row(fetch, 2 * i + m)).then_inc(gs_landed[m], 16)
                    if squares:
                        S.wait(act, "dve", f"{name} sum {m}", i - 1)
                        S.wait(act, "dve", f"{name} job {m}", i)
                        settle(act, i)
                        S.mark("act", f"{name} square {m}", act.activation(bs[:, m, :], tile2(X2, 2 * i + m), ACT.Square))
            S.leave("act", KT // 2)

        def residual_dve(name, j0, fetched=None, gate=False, squares=True):
            v = nc.vector
            if squares:
                S.mark("dve", f"{name} zero", v.memset(S2, 0.0))
                S.wait(v, "dve", f"{name} zero")
            S.enter("dve", name)
            with v.Fori(0, KT // 2) as i:
                for m in range(2):
                    v.wait_ge(gemm_done, j0 + 2 * i + m + 1)
                    if fetched is not None:
                        v.wait_ge(gs_landed[m], 16 * (fetched + i + 1))
                    k = 2 * i + m
                    other = gs[:, m, :] if fetched is not None else tile2(X2, k)
                    by = mod[:, bass.ds(16 + k, 1), 0:1].rearrange("p a b -> p (a b)") if gate else 1.0
                    S.mark("dve", f"{name} job {m}", v.scalar_tensor_tensor(tile2(X2, k), G[(j0 + m) % 2], by, other, ALU.mult, ALU.add))
                    if squares:
                        S.wait(v, "act", f"{name} square {m}", i)
                        S.mark("dve", f"{name} sum {m}", v.tensor_tensor(S2, S2, bs[:, m, :], ALU.add))
                        S.wait(v, "dve", f"{name} sum {m}", i)
            S.leave("dve", KT // 2)
            if squares:
                S.mark("dve", f"{name} squares", v.tensor_copy(bs[:, 1, :], S2))

        def norm_pe(name):
            S.wait(nc.tensor, "dve", f"{name} squares")
            for n in range(2):
                mm = nc.tensor.matmul(S2[:, n * NB:(n + 1) * NB], ones, bs[:, 1, n * NB:(n + 1) * NB], start=True, stop=True)
            S.mark("pe", f"{name} summed", mm)

        def norm_act(name, dst):
            act = nc.scalar
            S.wait(act, "pe", f"{name} summed")
            S.mark("act", f"{name} root", act.activation(gs[:, 0, :], S2, ACT.Sqrt, scale=1.0 / D, bias=epsc))
            for k in range(KT):
                S.wait(act, "dve", (name, "t", k))
                S.mark("act", (name, "hi", k), act.activation(dst[0][:, k, :], bs[:, k % 2, :], ACT.Copy))

        def norm_dve(name, gain, dst):
            v = nc.vector
            S.wait(v, "act", f"{name} root")
            S.mark("dve", f"{name} rstd", v.reciprocal(gs[:, 0, :], gs[:, 0, :]))
            S.wait(v, "dve", f"{name} rstd")
            for k in range(KT):
                if k >= 2:
                    S.wait(v, "dve", (name, "lo", k - 2))
                S.mark("dve", (name, "t", k), v.scalar_tensor_tensor(bs[:, k % 2, :], X2[:, k, :], col(gain, k), gs[:, 0, :], ALU.mult, ALU.mult))
                S.wait(v, "act", (name, "hi", k))
                S.mark("dve", (name, "lo", k), v.tensor_tensor(dst[1][:, k, :], bs[:, k % 2, :], dst[0][:, k, :].bitcast(F32), ALU.subtract))

        @block.sync
        def _(sp):
            load_pair(J_BRB, a["w_branch_b"][0], 0)
            sp.wait_ge(gemm_done, J_BRB)
            for k in range(KT):
                sp.dma_start(H[1][:, k, :].bitcast(F32), b_d[k]).then_inc(b_landed, 16)
            for name, j0, w, _ in BRANCHES:
                loads_of_8(j0, w, first=1 if name == "brb" else 0)

        @block.gpsimd
        def _(g):
            split_pair(J_BRB, 0)
            g.wait_ge(b_landed, 16 * KT)
            for k in range(B_POOL):
                S.mark("pool", ("b hi", k), g.tensor_tensor(H[0][:, k, :].rearrange("p (c t) -> p c t", t=P), H[1][:, k, :].bitcast(F32).rearrange("p (c t) -> p c t", t=P),
                                                           ones.unsqueeze(1).to_broadcast([P, KT, P]), ALU.mult))
                S.wait(g, "pool", ("b hi", k))
                S.mark("pool", ("b lo", k), low_part(g, H, k))
            for name, j0, _, _ in BRANCHES:
                splits_of(j0, first=1 if name == "brb" else 0)

        @block.tensor
        def _(pe):
            S.wait(pe, "pool", ("b lo", B_POOL - 1))
            S.wait(pe, "dve", ("b lo", KT - 1))
            for name, j0, _, mov in BRANCHES:
                if name == "bra":
                    S.wait(pe, "dve", "brb job 0", KT // 2 - 1)
                if name == "out":
                    S.wait(pe, "dve", "mix split 0", KT // 2 - 1)
                products_of_8(name, j0, mov, last={"brb": None, "bra": ("dve", "brb job 1", KT // 2 - 1), "out": ("dve", "mix split 1", KT // 2 - 1)}[name])

        @block.scalar
        def _(act):
            act.wait_ge(b_landed, 16 * KT)
            for k in range(B_POOL, KT):
                S.mark("act", ("b hi", k), act.activation(H[0][:, k, :], H[1][:, k, :].bitcast(F32), ACT.Copy))
            S.enter("act", "brb")
            with act.Fori(0, KT // 2) as i:
                for m in range(2):
                    k = 2 * i + m
                    S.wait(act, "dve", f"brb job {m}", i - 1)
                    act.dma_start(gs[:, m, :], row(sgb_d, k)).then_inc(gs_landed[m], 16)
                    act.dma_start(tile2(A[1], k).bitcast(F32), row(a_d, k)).then_inc(a_landed, 16)
                    act.wait_ge(a_landed, 16 * k + 16)
                    settle(act, i)
                    S.mark("act", f"a hi {m}", act.activation(tile2(A[0], k), tile2(A[1], k).bitcast(F32), ACT.Copy))
            S.leave("act", KT // 2)
            S.wait(act, "dve", "brb job 1", KT // 2 - 1)
            S.enter("act", "bra")
            with act.Fori(0, KT // 2) as i:
                for m in range(2):
                    S.wait(act, "dve", f"mix {m}", i - 1)
                    act.dma_start(gs[:, m, :], row(sga_d, 2 * i + m)).then_inc(gs_landed[m], 16)
                    S.wait(act, "dve", f"mix {m}", i)
                    settle(act, i)
                    S.mark("act", f"mix hi {m}", act.activation(tile2(H[0], 2 * i + m), bs[:, m, :], ACT.Copy))
            S.leave("act", KT // 2)
            S.wait(act, "dve", "mix split 1", KT // 2 - 1)
            S.enter("act", "out")
            with act.Fori(0, KT // 2) as i:
                for m in range(2):
                    k = 2 * i + m
                    S.wait(act, "dve", f"out job {m}", i - 1)
                    act.dma_start(gs[:, m, :], row(xT_d, k)).then_inc(gs_landed[m], 16)
                    S.wait(act, "dve", f"out job {m}", i)
                    settle(act, i)
                    S.mark("act", f"out square {m}", act.activation(bs[:, 0, :], tile2(X2, k), ACT.Square))
                    S.mark("act", f"out scaled square {m}", act.activation(bs[:, 1, :], tile2(X2, k), ACT.Square, scale=par[:, bass.ds(k + R0["f1"], 1)]))
                    S.wait(act, "dve", f"out operand {m}", i)
                    settle(act, i)
                    S.mark("act", f"out hi {m}", act.activation(tile2(A[0], k), tile2(A[1], k).bitcast(F32), ACT.Copy))
            S.leave("act", KT // 2)

        @block.vector
        def _(v):
            def do(name, ins):
                S.mark("dve", name, ins)
                return name
            def me(name, turn=None):
                S.wait(v, "dve", name, turn)
            for k in range(B_POOL, KT):
                S.wait(v, "act", ("b hi", k))
                do(("b lo", k), low_part(v, H, k))
            S.enter("dve", "brb")
            with v.Fori(0, KT // 2) as i:
                for m in range(2):
                    k = 2 * i + m
                    S.wait(v, "act", f"a hi {m}", i)
                    do(f"a lo {m}", v.tensor_tensor(tile2(A[1], k), tile2(A[1], k).bitcast(F32), tile2(A[0], k).bitcast(F32), ALU.subtract))
                    v.wait_ge(gemm_done, J_BRB + k + 1)
                    v.wait_ge(gs_landed[m], 16 * i + 16)
                    do(f"brb job {m}", v.tensor_tensor(tile2(X2, k), G[m], gs[:, m, :], ALU.mult))
            S.leave("dve", KT // 2)
            me("brb job 1", KT // 2 - 1)
            S.enter("dve", "bra")
            with v.Fori(0, KT // 2) as i:
                for m in range(2):
                    k = 2 * i + m
                    v.wait_ge(gemm_done, J_BRA + k + 1)
                    v.wait_ge(gs_landed[m], 16 * i + 16 + 16 * KT // 2)
                    do(f"bra job {m}", v.tensor_tensor(gs[:, m, :], G[m], gs[:, m, :], ALU.mult))
                    me(f"bra job {m}", i)
                    me(f"mix split {m}", i - 1)
                    do(f"mix {m}", v.tensor_tensor(bs[:, m, :], gs[:, m, :], tile2(X2, k), ALU.add))
                    S.wait(v, "act", f"mix hi {m}", i)
                    do(f"mix split {m}", v.tensor_tensor(tile2(H[1], k), bs[:, m, :], tile2(H[0], k).bitcast(F32), ALU.subtract))
            S.leave("dve", KT // 2)
            v.memset(U2, 0.0)
            me(do("out zero", v.memset(S2, 0.0)))
            S.enter("dve", "out")
            with v.Fori(0, KT // 2) as i:
                for m in range(2):
                    k = 2 * i + m
                    v.wait_ge(gemm_done, J_OUT + k + 1)
                    v.wait_ge(gs_landed[m], 16 * i + 16 * (KT + 1))
                    do(f"out job {m}", v.scalar_tensor_tensor(tile2(X2, k), G[(J_OUT + m) % 2], mod[:, bass.ds(16 + k, 1), 0:1].rearrange("p a b -> p (a b)"),
                                                              gs[:, m, :], ALU.mult, ALU.add))
                    me(f"out job {m}", i)
                    do(f"out operand {m}", v.tensor_scalar(tile2(A[1], k).bitcast(F32), tile2(X2, k), gains[:, bass.ds(k, 1)], None, ALU.mult))
                    S.wait(v, "act", f"out square {m}", i)
                    do(f"out sum {m}", v.tensor_tensor(S2, S2, bs[:, 0, :], ALU.add))
                    S.wait(v, "act", f"out scaled square {m}", i)
                    do(f"out scaled sum {m}", v.tensor_tensor(U2, U2, bs[:, 1, :], ALU.add))
                    S.wait(v, "act", f"out hi {m}", i)
                    do(f"out lo {m}", v.tensor_tensor(tile2(A[1], k), tile2(A[1], k).bitcast(F32), tile2(A[0], k).bitcast(F32), ALU.subtract))
                    me(f"out lo {m}", i)
            S.leave("dve", KT // 2)
            v.tensor_copy(bs[:, 0, :], U2)
            do("out squares", v.tensor_copy(bs[:, 1, :], S2))

        o = 0
        Qh = [take(f"q_hi{h}", [P, T], F32R) for h in range(2)]
        Ql = [take(f"q_lo{h}", [P, T], F32R) for h in range(2)]
        Ks = [take(f"k_parts{h}", [P, T], F32R) for h in range(2)]
        av = take("att_v", [P, TT, P])
        ON = take("att_out", [P, TT, P])
        avT = ON.rearrange("p t d -> p (t d)")
        OT = take("att_outT", [P, T])
        osq = take("att_squares", [P, T])
        SQ = [take("fox_squares", [P, T]), take("sb_squares", [P, T])]
        R1 = take("rstd1", [P, T])
        SC = take("rstd12", [P, T])
        qt = take("projected", [P, T])
        pT = [take("probsT0", [P, 4, P]), take("probsT1", [P, 4, P])]
        assert o <= 64 * KB, o
        o = W0 + 96 * KB
        pr = [take("probs0", [P, T]), take("probs1", [P, T])]
        nots = take("not_taken", [P, T])
        left = take("left_over", [P, T + 8])
        rs = take("row_sums", [P, 4, 1])
        mn = take("row_mins", [P, 2, 1])
        nf_d = scratch("forget_sums", (S_HEADS, T))
        w_in2 = a["w_in_2"][0]
        o_stored, o_landed = sem("heads_out_stored"), sem("heads_out_landed")
        nf_stored, nf_landed, out_stored = sem("forget_sums_stored"), sem("forget_sums_landed"), [sem("out_stored0"), sem("out_stored1")]
        Z = [S2, G[1]]
        fsum = [nots, left[:, 0:T]]
        TILES = [(hh, tt) for hh in range(2) for tt in range(TT)]
        GROUPS = [(n, g) for n, (hh, tt) in enumerate(TILES) for g in range(tt // 4 + 1)]
        SCORE_READER = {"f": ("dve", "f scores"), "s": ("act", "s not")}

        def groups_of(n):
            return [(c, g) for c, (m, g) in enumerate(GROUPS) if m == n]

        def before(x, i):
            return ("s", i - 1) if x == "f" else ("f", i)

        ATT_COLS = (S_FQ, S_FK, S_FV, S_SQ, S_SK, S_SV)

        def over_features(dst, src):
            for n in range(2):
                mm = nc.tensor.matmul(dst[n], ones, src[:, n * NB:(n + 1) * NB], start=True, stop=True)
            return mm

        def halves_of(pair):
            return [pair[:, 0:NB], pair[:, NB:2 * NB]]

        EARLY = KT - 1

        @block.sync
        def _(sp):
            load_w(J_FL, J_FL % 2, slab(w_in2, S_FL))
            with sp.Fori(0, HEADS) as i:
                for m, c in enumerate(ATT_COLS):
                    load_w(J_ATT + ATT_JOBS * i + m, (J_ATT + m) % 2, dslab(w_in2, i * P + c))
            sp.wait_ge(gemm_done, J_OUT2)
            sp.wait_ge(o_stored, 16 * EARLY)
            for k in range(EARLY):
                sp.dma_start(A[1][:, k, :].bitcast(F32), o_d[k]).then_inc(o_landed, 16)
            loads_of_8(J_OUT2, a["w_out_2"][0])

        @block.gpsimd
        def _(g):
            split(J_FL, J_FL % 2, J_FL // 2 + 1)

            def add_squares(x, i, name):
                for n in range(2):
                    S.wait(g, "act", f"{x} squares {n}", i)
                s = SQ["fs".index(x)]
                S.mark("pool", name, g.tensor_tensor(s, s, osq, ALU.add))
            g.wait_ge(gemm_done, J_FL)
            S.mark("pool", "square sums cleared", g.memset(SQ[0], 0.0))
            S.mark("pool", "squares cleared", g.memset(osq, 0.0))
            S.mark("pool", "square sums cleared 2", g.memset(SQ[1], 0.0))
            S.wait(g, "pool", "square sums cleared 2")
            S.enter("pool", "att")
            with g.Fori(0, HEADS) as i:
                for m in range(ATT_JOBS):
                    split(J_ATT + ATT_JOBS * i + m, (J_ATT + m) % 2, i * (ATT_JOBS // 2) + ((J_ATT + m) // 2 + 1))
                    if m == 1:
                        add_squares("s", i - 1, "s squares added")
                    if m == 4:
                        add_squares("f", i, "f squares added")
            S.leave("pool", HEADS)
            add_squares("s", HEADS - 1, "last squares added")
            g.wait_ge(o_landed, 16 * EARLY)
            for k in range(EARLY - 1):
                S.mark("pool", ("heads hi", k), g.tensor_tensor(A[0][:, k, :].rearrange("p (c t) -> p c t", t=P), A[1][:, k, :].bitcast(F32).rearrange("p (c t) -> p c t", t=P), ones.unsqueeze(1).to_broadcast([P, KT, P]), ALU.mult))
                S.wait(g, "pool", ("heads hi", k))
                S.mark("pool", ("heads lo", k), low_part(g, A, k))
            splits_of(J_OUT2)

        @block.tensor
        def _(pe):
            S.wait(pe, "dve", "out squares")
            S.mark("pe", "out summed", over_features(halves_of(S2), bs[:, 1, :]))
            S.mark("pe", "out scaled summed", over_features(halves_of(G[1]), bs[:, 0, :]))
            gemm(J_FL, J_FL % 2, A, pair=U2)
            S.wait(pe, "dve", "mean2 half")

            def job(i, x, m):
                y, turn = before(x, i)
                freed = {0: (SCORE_READER[y][0], f"{SCORE_READER[y][1]} 15", turn), 1: ("dve", f"{y} out 15", turn), 2: ("dve", f"{x} q", i)}[m]
                mm = m + (3 if x == "s" else 0)
                gemm(J_ATT + ATT_JOBS * i + mm, (J_ATT + mm) % 2, A, freed, pair=G[(1, 0, 1)[m]])

            def scores(i, x, n):
                hh, tt = TILES[n]
                z, w = Z[n % 2], (tt + 1) * P
                if n == 0:
                    S.wait(pe, "dve", f"{x} k low 1", i)
                    S.wait(pe, "act", f"{x} k high 1", i)
                elif n == 1:
                    S.wait(pe, "dve", f"{x} vT", i)
                else:
                    S.wait(pe, SCORE_READER[x][0], f"{SCORE_READER[x][1]} {n - 2}", i)
                for b in range((w + NB - 1) // NB):
                    cols = slice(b * NB, min(w, (b + 1) * NB))
                    for q in (Qh[hh], Ql[hh]):
                        pe.matmul(z[:, cols], q[:, tt * P:(tt + 1) * P], Ks[hh][:, cols], start=q is Qh[hh], stop=q is Ql[hh] and tt // 4 != b)
                mm = pe.matmul(z[:, tt * P:w], identb, maskb[:, "fs".index(x), :], start=False, stop=True)
                S.mark("pe", f"{x} z {n}", mm)

            def turned(i, x, n):
                maker, made = ("act", f"f probs {n}") if x == "f" else ("dve", f"s probs {n}")
                for c, g in groups_of(n):
                    reader, read = ("act", "dve")[c % 2], f"{x} v {c}" if c < 2 else f"{x} pT {c - 2}"
                    if g == 0 and reader == maker:
                        S.wait_last(pe, maker, (made, read), i)
                    else:
                        if g == 0:
                            S.wait(pe, maker, made, i)
                        S.wait(pe, reader, read, i)
                    tt = TILES[n][1]
                    for b in range(4 * g, min(4 * g + 4, tt + 1)):
                        mm = pe.transpose(U[c % 2][:, (b % 4) * P:(b % 4 + 1) * P], pr[n % 2][:, b * P:(b + 1) * P], ident)
                    S.mark("pe", f"{x} turned {c}", mm)

            def values(i, x, n):
                hh, tt = TILES[n]
                if n >= 2 and groups_of(n)[0][0] % 2 == 0:
                    S.wait(pe, "dve", f"{x} out {n - 2}", i)
                elif n == 0:
                    S.wait(pe, "dve", f"{x} v 1", i)
                for c, g in groups_of(n):
                    S.wait(pe, ("act", "dve")[c % 2], f"{x} pT {c}", i)
                    for b in range(4 * g, min(4 * g + 4, tt + 1)):
                        mm = pe.matmul(G[0][:, (n % 2) * NB:(n % 2) * NB + P], pT[c % 2][:, b % 4, :], av[:, b, :],
                                       start=b == 0, stop=b == tt)
                    S.mark("pe", f"{x} values {c}", mm)

            S.enter("pe", "att")
            with pe.Fori(0, HEADS) as i:
                for x in "fs":
                    if x == "f":
                        job(i, x, 0)
                    job(i, x, 1)
                    job(i, x, 2)
                    scores(i, x, 0)
                    scores(i, x, 1)
                    for n in range(2):
                        S.wait(pe, "dve", f"{before(x, i)[0]} outT {n}", before(x, i)[1])
                        for b in range(4):
                            mm = pe.transpose(U[n][:, b * P:(b + 1) * P], avT[:, (4 * n + b) * P:(4 * n + b + 1) * P], ident)
                        S.mark("pe", f"{x} v turned {n}", mm)
                    for n in range(len(TILES)):
                        if n == len(TILES) - 1 and x == "f":
                            job(i, "s", 0)
                        turned(i, x, n)
                        if n + 2 < len(TILES):
                            scores(i, x, n + 2)
                        values(i, x, n)
                    S.wait(pe, "dve", f"{x} out {len(TILES) - 1}", i)
                    last = len(GROUPS) - 1
                    S.wait(pe, "act", f"{x} pT {last - last % 2}", i)
                    for n in range(2):
                        for b in range(4):
                            mm = pe.transpose(U[n][:, b * P:(b + 1) * P], ON[:, 4 * n + b, :], ident)
                        S.mark("pe", f"{x} outT {n}", mm)
            S.leave("pe", HEADS)
            S.wait(pe, "pool", "last squares added")
            S.mark("pe", "fox squares summed", over_features(halves_of(S2), SQ[0]))
            S.wait(pe, "dve", "s outT 1", HEADS - 1)
            S.mark("pe", "sb squares summed", over_features(U, SQ[1]))
            S.wait(pe, "pool", ("heads lo", EARLY - 2))
            S.wait(pe, "dve", ("heads lo", EARLY - 1))
            S.enter("pe", "out2")
            with pe.Fori(0, KT // 2) as i:
                for m in range(2):
                    pe.wait_ge(w_ready, J_OUT2 + 2 * i + m + 1)
                    freed = ("out2 sb 0", i) if m else ("out2 sb 1", i - 1)
                    S.wait(pe, "dve", *freed)
                    S.mark("pe", f"out2 fox {m}", passes((J_OUT2 + m) % 2, A, range(HEADS), G[0]))
                    passes((J_OUT2 + m) % 2, A, range(HEADS, KT), G[1]).then_inc(gemm_done, 1)
            S.leave("pe", KT // 2)

        @block.scalar
        def _(act):
            S.wait(act, "pe", "out summed")
            S.mark("act", "root1", act.activation(R1, S2, ACT.Sqrt, scale=1.0 / D, bias=epsc))
            S.wait(act, "dve", "mean2")
            S.mark("act", "root2", act.activation(SC, bs[:, 1, :], ACT.Sqrt, scale=1.0 / D, bias=epsc))
            S.wait(act, "dve", "f projected")
            g8, l8 = pr[0][0:S_HEADS, :], pr[1][0:S_HEADS, :]
            S.mark("act", "f logit", act.activation(g8, qt[0:S_HEADS, :], ACT.Identity, bias=fbias[0:S_HEADS, :]))
            S.wait(act, "act", "f logit")
            S.mark("act", "f abs", act.activation(l8, g8, ACT.Abs))
            S.wait(act, "act", "f abs")
            S.mark("act", "f exp", act.activation(l8, l8, ACT.Exp, scale=-1.0))
            S.wait(act, "act", "f exp")
            S.mark("act", "f ln", act.activation(l8, l8, ACT.Ln, bias=1.0))
            S.wait(act, "dve", "forget sums")
            act.dma_start(nf_d, nots[0:S_HEADS, :]).then_inc(nf_stored, 16)
            act.wait_ge(nf_stored, 16)
            S.enter("act", "att")
            with act.Fori(0, HEADS) as i:
                def high_parts(x, part):
                    S.wait(act, "dve", f"{x} {part}", i)
                    for hh in range(2):
                        own, other = slice(HD * hh, HD * hh + HD), slice(HD - HD * hh, P - HD * hh)
                        if part == "q":
                            act.activation(Qh[hh][other, :], qt[own, :], ACT.Copy)
                        dst = Qh[hh] if part == "q" else Ks[hh]
                        S.mark("act", f"{x} {part} high {hh}", act.activation(dst[own, :], qt[own, :], ACT.Copy))

                def chain(x, n):
                    hh, tt = TILES[n]
                    w = (tt + 1) * P
                    if x == "f":
                        S.wait(act, "dve", f"f scores {n}", i)
                        S.mark("act", f"f probs {n}", act.activation(pr[n % 2][:, 0:w], pr[n % 2][:, 0:w], ACT.Exp, scale=-1.0,
                                                                     bias=mn[:, n % 2, :], accum_out=rs[:, n % 4, :]))
                    else:
                        S.wait(act, "pe", f"s z {n}", i)
                        S.mark("act", f"s taken {n}", act.activation(pr[n % 2][:, 0:w], Z[n % 2][:, 0:w], ACT.Sigmoid))
                        if n:
                            S.wait(act, "dve", f"s left {n - 1}", i)
                        S.mark("act", f"s not {n}", act.activation(nots[:, 0:w], Z[n % 2][:, 0:w], ACT.Sigmoid, scale=-1.0))

                def copy_turned(x, n):
                    for c, g in groups_of(n):
                        if c % 2 == 0:
                            w = min(4, TILES[n][1] + 1 - 4 * g)
                            S.wait(act, "pe", f"{x} turned {c}", i)
                            S.mark("act", f"{x} pT {c}", act.activation(pT[0][:, 0:w, :], U[0][:, 0:w * P].rearrange("p (b t) -> p b t", t=P), ACT.Copy))

                for x in "fs":
                    if x == "f":
                        S.wait(act, "dve", "s probs 15", i - 1)
                        for hh in range(2):
                            act.dma_start(fsum[hh], nf_d[bass.ds(2 * i + hh, 1), :].to_broadcast([P, T])).then_inc(nf_landed, 16)
                    if x == "f":
                        high_parts(x, "q")
                    high_parts(x, "k")
                    if x == "s":
                        S.wait(act, "dve", "f scores 15", i)
                    chain(x, 0)
                    S.wait(act, "pe", f"{x} v turned 0", i)
                    S.mark("act", f"{x} v 0", act.activation(av[:, 0:4, :], U[0].rearrange("p (b t) -> p b t", t=P), ACT.Copy))
                    for n in range(len(TILES)):
                        if n + 1 < len(TILES):
                            chain(x, n + 1)
                        copy_turned(x, n)
                    if x == "f":
                        high_parts("s", "q")
                    for n in range(2):
                        S.wait(act, "pe", f"{x} outT {n}", i)
                        if n == 0:
                            S.wait(act, "pool", "s squares added" if x == "f" else "f squares added", i)
                        S.mark("act", f"{x} squares {n}", act.activation(osq[:, n * NB:(n + 1) * NB], U[n], ACT.Square))
                    S.wait(act, "dve", f"{x} outT 1", i)
                    act.dma_start(row(o_d, i + HEADS * "fs".index(x)), OT).then_inc(o_stored, 16)
                act.wait_ge(o_stored, 32 * i + 32)
            S.leave("act", HEADS)
            for k, src in ((EARLY - 1, A[1][:, EARLY - 1, :].bitcast(F32)), (KT - 1, OT)):
                if k == EARLY - 1:
                    act.wait_ge(o_landed, 16 * EARLY)
                S.mark("act", ("heads hi", k), act.activation(A[0][:, k, :], src, ACT.Copy))
            S.wait(act, "pe", "fox squares summed")
            S.mark("act", "fox root", act.activation(gs[:, 0, :], S2, ACT.Sqrt, scale=2.0 / D, bias=epsc))
            S.wait(act, "pe", "sb squares summed")
            for n in range(2):
                S.mark("act", f"sb root {n}", act.activation(gs[:, 1, n * NB:(n + 1) * NB], U[n], ACT.Sqrt, scale=2.0 / D, bias=epsc))
            S.enter("act", "out2")
            with act.Fori(0, KT // 2) as i:
                for m in range(2):
                    k = 2 * i + m
                    S.wait(act, "dve", f"out2 job {m}", i)
                    settle(act, i)
                    S.mark("act", f"out2 square {m}", act.activation(bs[:, 1, :], tile2(X2, k), ACT.Square))
                    S.wait(act, "dve", f"out2 operand {m}", i)
                    settle(act, i)
                    S.mark("act", f"out2 hi {m}", act.activation(tile2(H[0], k), tile2(H[1], k).bitcast(F32), ACT.Copy))
            S.leave("act", KT // 2)
            act.wait_ge(o_stored, 16 * KT)

        @block.vector
        def _(v):
            def do(name, ins):
                S.mark("dve", name, ins)
                return name

            S.wait(v, "act", "root1")
            do("rstd1", v.reciprocal(R1, R1))
            S.wait(v, "dve", "rstd1")
            S.wait(v, "pe", "out scaled summed")
            do("mean2 half", v.tensor_tensor(bs[:, 1, :], G[1], R1, ALU.mult))
            S.wait(v, "dve", "mean2 half")
            do("mean2", v.tensor_tensor(bs[:, 1, :], bs[:, 1, :], R1, ALU.mult))
            S.wait(v, "act", "root2")
            do("rstd2", v.reciprocal(SC, SC))
            S.wait(v, "dve", "rstd2")
            do("rstd12", v.tensor_tensor(SC, SC, R1, ALU.mult))
            S.wait(v, "dve", "rstd12")
            v.wait_ge(gemm_done, J_FL + 1)
            do("f projected", v.tensor_tensor(qt[0:S_HEADS, :], U2[0:S_HEADS, :], SC[0:S_HEADS, :], ALU.mult))
            g8, l8, F8 = pr[0][0:S_HEADS, :], pr[1][0:S_HEADS, :], nots[0:S_HEADS, :]
            S.wait(v, "act", "f ln")
            do("forget logs", v.scalar_tensor_tensor(g8, g8, 0.0, l8, ALU.min, ALU.subtract))
            S.wait(v, "dve", "forget logs")
            do("forget sums", v.tensor_tensor_scan(F8, g8, g8, 0.0, ALU.add, ALU.bypass))
            do("left all", v.memset(left[:, T:T + 1], 1.0))
            S.enter("dve", "att")
            with v.Fori(0, HEADS) as i:
                def me(name):
                    S.wait(v, "dve", name, i)

                def chain(x, n):
                    hh, tt = TILES[n]
                    w = (tt + 1) * P
                    p = pr[n % 2][:, 0:w]
                    if x == "f":
                        S.wait(v, "pe", f"f z {n}", i)
                        if n == 0:
                            v.wait_ge(nf_landed, 32 * i + 32)
                        settle(v, i)
                        do(f"f scores {n}", v.tensor_tensor_reduce(out=p, in0=fsum[hh][:, 0:w], in1=Z[n % 2][:, 0:w], scale=1.0, scalar=1e30,
                                                                   op0=ALU.add, op1=ALU.min, accum_out=mn[:, n % 2, :]))
                    else:
                        S.wait(v, "act", f"s not {n}", i)
                        if n:
                            me(f"s probs {n - 1}")
                        do(f"s left {n}", v.tensor_tensor_scan(left[:, T - w:T][:, ::-1], nots[:, 0:w][:, ::-1], nots[:, 0:w], 1.0, ALU.mult, ALU.bypass))
                        me(f"s left {n}")
                        do(f"s probs {n}", v.tensor_tensor(p, p, left[:, T - w + 1:T + 1], ALU.mult))

                def copy_turned(x, n):
                    for c, g in groups_of(n):
                        if c % 2 == 1:
                            w = min(4, TILES[n][1] + 1 - 4 * g)
                            S.wait(v, "pe", f"{x} turned {c}", i)
                            do(f"{x} pT {c}", v.tensor_copy(pT[1][:, 0:w, :], U[1][:, 0:w * P].rearrange("p (b t) -> p b t", t=P)))

                def out_of(x, n):
                    hh, tt = TILES[n]
                    src, dst = G[0][:, (n % 2) * NB + HD * hh:(n % 2) * NB + HD * hh + HD], ON[:, tt, HD * hh:HD * hh + HD]
                    if x == "f":
                        S.wait(v, "act", f"f probs {n}", i)
                        do(f"f sums {n}", v.reciprocal(rs[:, n % 4, :], rs[:, n % 4, :]))
                        me(f"f sums {n}")
                    S.wait(v, "pe", f"{x} values {groups_of(n)[-1][0]}", i)
                    do(f"{x} out {n}", v.tensor_scalar(dst, src, rs[:, n % 4, :], None, ALU.mult) if x == "f" else v.tensor_copy(dst, src))

                def project(x, m):
                    jj = J_ATT + ATT_JOBS * i + (m + (3 if x == "s" else 0) + 1)
                    if m == 0:
                        S.wait(v, "dve", f"{before(x, i)[0]} k low 1", before(x, i)[1])
                    elif m == 1:
                        me(f"{x} q low 1")
                    v.wait_ge(gemm_done, jj)
                    by = float(HD) ** -0.5 * (-1 if x == "f" else 1) if m == 0 else 1.0
                    do(f"{x} {('q', 'k', 'vT')[m]}", v.scalar_tensor_tensor(avT if m == 2 else qt, G[(1, 0, 1)[m]], by, SC, ALU.mult, ALU.mult))

                def low_parts(x, m):
                    for hh in range(2):
                        own, other = slice(HD * hh, HD * hh + HD), slice(HD - HD * hh, P - HD * hh)
                        S.wait(v, "act", f"{x} {'qk'[m]} high {hh}", i)
                        high = (Qh, Ks)[m][hh][own, :].bitcast(F32)
                        if m == 0:
                            v.tensor_tensor(Ql[hh][own, :], qt[own, :], high, ALU.subtract)
                        do(f"{x} {'qk'[m]} low {hh}", v.tensor_tensor((Ql, Ks)[m][hh][other, :], qt[own, :], high, ALU.subtract))

                for x in "fs":
                    if x == "f":
                        project(x, 0)
                    low_parts(x, 0)
                    project(x, 1)
                    low_parts(x, 1)
                    project(x, 2)
                    chain(x, 0)
                    if x == "f":
                        chain(x, 1)
                    S.wait(v, "pe", f"{x} v turned 1", i)
                    do(f"{x} v 1", v.tensor_copy(av[:, 4:8, :], U[1].rearrange("p (b t) -> p b t", t=P)))
                    for n in range(len(TILES)):
                        if x == "s" and n + 1 < len(TILES):
                            chain(x, n + 1)
                        if x == "f" and n == len(TILES) - 1:
                            out_of(x, n - 1)
                            project("s", 0)
                        copy_turned(x, n)
                        if n and not (x == "f" and n == len(TILES) - 1):
                            out_of(x, n - 1)
                        if x == "f" and n + 2 < len(TILES):
                            chain(x, n + 2)
                    out_of(x, len(TILES) - 1)
                    for n in range(2):
                        S.wait(v, "act", f"{x} squares {n}", i)
                        if n == 0 and x == "s":
                            v.wait_ge(o_stored, 32 * i + 16)
                        do(f"{x} outT {n}", v.tensor_scalar(OT[:, n * NB:(n + 1) * NB], U[n], par[:, bass.ds(i + (R0["fg"] + HEADS * "fs".index(x)), 1)], None, ALU.mult))
                for m in range(2):
                    k = 2 * i + m
                    do(f"x2 normed {m}", v.scalar_tensor_tensor(tile2(X2, k), tile2(X2, k), par[:, bass.ds(k + R0["f1"], 1)], R1, ALU.mult, ALU.mult))
            S.leave("dve", HEADS)
            for k, src in ((KT - 1, OT), (EARLY - 1, None)):
                S.wait(v, "act", ("heads hi", k))
                do(("heads lo", k), low_part(v, A, k) if src is None else v.tensor_tensor(A[1][:, k, :], src, A[0][:, k, :].bitcast(F32), ALU.subtract))
            S.wait(v, "act", "fox root")
            do("fox rstd", v.reciprocal(gs[:, 0, :], gs[:, 0, :]))
            S.wait(v, "act", "sb root 1")
            do("sb rstd", v.reciprocal(gs[:, 1, :], gs[:, 1, :]))
            S.wait(v, "dve", "sb rstd")
            S.mark("dve", "out2 zero", v.memset(S2, 0.0))
            S.wait(v, "dve", "out2 zero")
            S.enter("dve", "out2")
            with v.Fori(0, KT // 2) as i:
                def me(name):
                    S.wait(v, "dve", name, i)
                for m in range(2):
                    k = 2 * i + m
                    S.wait(v, "pe", f"out2 fox {m}", i)
                    do(f"out2 fox {m}", v.tensor_tensor(bs[:, 0, :], G[0], gs[:, 0, :], ALU.mult))
                    me(f"out2 fox {m}")
                    do(f"out2 fox added {m}", v.tensor_tensor(tile2(X2, k), tile2(X2, k), bs[:, 0, :], ALU.add))
                    me(f"out2 fox added {m}")
                    v.wait_ge(gemm_done, J_OUT2 + k + 1)
                    do(f"out2 sb {m}", v.tensor_tensor(bs[:, 0, :], G[1], gs[:, 1, :], ALU.mult))
                    me(f"out2 sb {m}")
                    do(f"out2 job {m}", v.tensor_tensor(tile2(X2, k), tile2(X2, k), bs[:, 0, :], ALU.add))
                    me(f"out2 job {m}")
                    do(f"out2 operand {m}", v.tensor_scalar(tile2(H[1], k).bitcast(F32), tile2(X2, k), par[:, bass.ds(k + R0["fn"], 1)], None, ALU.mult))
                    S.wait(v, "act", f"out2 square {m}", i)
                    do(f"out2 sum {m}", v.tensor_tensor(S2, S2, bs[:, 1, :], ALU.add))
                    S.wait(v, "act", f"out2 hi {m}", i)
                    do(f"out2 lo {m}", v.tensor_tensor(tile2(H[1], k), tile2(H[1], k).bitcast(F32), tile2(H[0], k).bitcast(F32), ALU.subtract))
                    me(f"out2 lo {m}")
            S.leave("dve", KT // 2)
            do("out2 squares", v.tensor_copy(bs[:, 0, :], S2))

        w_up, w_down = a["w_up_2"][0], a["w_down_2"][0]

        def ffn_jobs():
            j = J_FFN
            for g, (f0, nf) in enumerate(FFN_GROUPS):
                yield g, f0, nf, j, j + 2 * nf
                j += 2 * nf + KT

        @block.sync
        def _(sp):
            for g, f0, nf, up, down in ffn_jobs():
                with sp.Fori(0, nf) as f:
                    for m in range(2):
                        load_w(up + 2 * f + m, (up + m) % 2, dslab(w_up, f * P + (f0 * P + m * DFF)))
                loads_of_8(down, w_down, nf, f0 * P)
            for t in range(TT):
                for h in range(2):
                    S.wait(sp, ("act", "dve")[h], f"staged {t}")
                sp.dma_start(out[0, t * P:(t + 1) * P, :], (gs, bs)[t % 2][:, 1, :]).then_inc(out_stored[t % 2], 16)
            for s in range(2):
                sp.wait_ge(out_stored[s], 16 * TT // 2)

        @block.gpsimd
        def _(g_):
            for g, f0, nf, up, down in ffn_jobs():
                splits_of(up, pairs=nf)
                splits_of(down, kt=nf)

        @block.tensor
        def _(pe):
            S.wait(pe, "dve", "out2 squares")
            S.mark("pe", "out2 summed", over_features(halves_of(S2), bs[:, 0, :]))
            for g, f0, nf, up, down in ffn_jobs():
                if g:
                    for m in range(2):
                        S.wait(pe, "dve", f"down{g - 1} job {m}", KT // 2 - 1)
                S.enter("pe", f"up{g}")
                with pe.Fori(0, nf) as f:
                    for m in range(2):
                        gemm(up + 2 * f + m, (up + m) % 2, H, ("dve", f"up{g} normed {m}", f - 1))
                S.leave("pe", nf)
                S.wait(pe, "dve", f"up{g} lo", nf - 2)
                products_of_8(f"down{g}", down, A, nf, last=("dve", f"up{g} lo", nf - 1))
            norm_pe("down2")
            for t in range(TT):
                for h in range(2):
                    if t:
                        S.wait(pe, ("act", "dve")[h], f"staged {t - 1}")
                    for b in range(4):
                        k = 4 * h + b
                        if t == 0:
                            S.wait(pe, "dve", ("x4 scaled", k))
                        mm = pe.transpose(U[h][:, b * P:(b + 1) * P], X2[:, k, t * P:(t + 1) * P], ident)
                    S.mark("pe", f"out turned {t} {h}", mm)

        @block.scalar
        def _(act):
            S.wait(act, "pe", "out2 summed")
            S.mark("act", "out2 root", act.activation(bs[:, 1, :], S2, ACT.Sqrt, scale=1.0 / D, bias=epsc))
            for g, f0, nf, up, down in ffn_jobs():
                if g:
                    S.wait(act, "dve", f"down{g - 1} job 1", KT // 2 - 1)
                S.enter("act", f"up{g}")
                with act.Fori(0, nf) as f:
                    for m in range(2):
                        S.wait(act, "dve", f"up{g} normed {m}", f)
                        settle(act, f)
                        S.mark("act", f"up{g} tap {m}", act.activation(gs[:, m, :], bs[:, 0, :], ACT.Identity, bias=conv_col(0, f + (f0 + m * FT)), scale=conv_col(3, f + (f0 + m * FT))))
                        if m == 0:
                            S.wait(act, "dve", f"up{g} conv 0", f)
                            S.mark("act", f"up{g} silu", act.activation(gs[:, 0, :], gs[:, 0, :], ACT.Silu))
                    S.wait(act, "dve", f"up{g} act", f)
                    settle(act, f)
                    S.mark("act", f"up{g} hi", act.activation(tile2(A[0], f), tile2(A[1], f).bitcast(F32), ACT.Copy))
                S.leave("act", nf)
                residual_act(f"down{g}", [], squares=g == len(FFN_GROUPS) - 1)
            S.wait(act, "pe", "down2 summed")
            S.mark("act", "down2 root", act.activation(gs[:, 0, :], S2, ACT.Sqrt, scale=1.0 / D, bias=epsc))
            for t in range(TT):
                S.wait(act, "pe", f"out turned {t} 0")
                if t >= 2:
                    act.wait_ge(out_stored[t % 2], 16 * (t // 2))
                S.mark("act", f"staged {t}", act.activation((gs, bs)[t % 2][:, 1, 0:NB], U[0], ACT.Copy))

        @block.vector
        def _(v):
            def do(name, ins):
                S.mark("dve", name, ins)
                return name
            S.wait(v, "act", "out2 root")
            do("out2 rstd", v.reciprocal(bs[:, 1, :], bs[:, 1, :]))
            S.wait(v, "dve", "out2 rstd")
            for g, f0, nf, up, down in ffn_jobs():
                S.enter("dve", f"up{g}")
                with v.Fori(0, nf) as f:
                    for m in range(2):
                        k = f + (f0 + m * FT)
                        y, u = gs[:, m, :], bs[:, 0, :]
                        v.wait_ge(gemm_done, up + 2 * f + m + 1)
                        if m == 0:
                            S.wait(v, "dve", f"up{g} act", f - 1)
                        else:
                            S.wait(v, "dve", f"up{g} conv 0", f)
                        do(f"up{g} normed {m}", v.tensor_tensor(u, G[(up + m) % 2], bs[:, 1, :], ALU.mult))
                        S.wait(v, "act", f"up{g} tap {m}", f)
                        do(f"up{g} near {m}", v.scalar_tensor_tensor(y[:, 1:T], u[:, 0:T - 1], conv_col(2, k), y[:, 1:T], ALU.mult, ALU.add))
                        S.wait(v, "dve", f"up{g} near {m}", f)
                        do(f"up{g} conv {m}", v.scalar_tensor_tensor(y[:, 2:T], u[:, 0:T - 2], conv_col(1, k), y[:, 2:T], ALU.mult, ALU.add))
                    S.wait(v, "act", f"up{g} silu", f)
                    S.wait(v, "dve", f"up{g} conv 1", f)
                    do(f"up{g} act", v.tensor_tensor(tile2(A[1], f).bitcast(F32), gs[:, 0, :], gs[:, 1, :], ALU.mult))
                    S.wait(v, "act", f"up{g} hi", f)
                    do(f"up{g} lo", v.tensor_tensor(tile2(A[1], f), tile2(A[1], f).bitcast(F32), tile2(A[0], f).bitcast(F32), ALU.subtract))
                S.leave("dve", nf)
                residual_dve(f"down{g}", down, squares=g == len(FFN_GROUPS) - 1)
            S.wait(v, "act", "down2 root")
            do("down2 rstd", v.reciprocal(gs[:, 0, :], gs[:, 0, :]))
            S.wait(v, "dve", "down2 rstd")
            for k in range(KT):
                do(("x4 scaled", k), v.scalar_tensor_tensor(X2[:, k, :], X2[:, k, :], col("fin", k), gs[:, 0, :], ALU.mult, ALU.mult))
            for t in range(TT):
                S.wait(v, "pe", f"out turned {t} 1")
                if t >= 2:
                    v.wait_ge(out_stored[t % 2], 16 * (t // 2))
                do(f"staged {t}", v.tensor_copy((gs, bs)[t % 2][:, 1, NB:D], U[1]))

        @block.scalar
        def _(act):
            for engine in ("act", "dve"):
                act.wait_ge(S.settled[engine], S.n[engine, "settled"])
    return S.at


INPUTS = ("x", "c", "ctx", "c_ctx", "w_mod", "b_mod", "norm_g", "w_in", "w_gate_up_f", "b_gate_f", "w_gate_up_b",
          "b_gate_b", "gla_norm_g", "w_pool", "pool_scale", "w_branch_a", "w_branch_b", "w_out", "final_norm_g", "attn_norm_g_2",
          "w_in_2", "forget_bias_2", "fox_out_g_2", "sb_out_g_2", "w_out_2", "ffn_norm_g_2", "w_up_2", "conv_w_2",
          "conv_b_2", "w_down_2", "final_norm_g_2")


def constants():
    t = np.arange(T)
    i = np.arange(P)
    j = i[:, None]
    levels = np.stack([((j // (2 * s)) == (i // (2 * s))) & ((j % (2 * s) < s) != (i % (2 * s) < s)) for s in LEVELS], 1)
    nf = DK // 4
    freqs = np.power(np.float32(10000.0), -np.arange(nf, dtype=np.float32) / nf).astype(np.float32)
    pos = np.where(i[:, None] < DK // 2, (t // GRID_W)[None], (t % GRID_W)[None]).astype(np.float32)
    angle = (pos * freqs[i % nf][:, None]).astype(np.float32).astype(np.float64)
    sign = np.where(i % (2 * nf) < nf, -1.0, 1.0)[:, None]
    half = np.array([1, 2, 4, 8])[:, None]
    count = np.clip(t + half, 0, T) - np.clip(t - half, 0, T)
    inv = np.broadcast_to((1.0 / count)[:, None, :], (4, P, T))
    mask = np.where(i[None, :] > j, np.float32(1e30), 0.0)
    strict = np.where(i[None, :] >= j, np.float32(-1e30), 0.0)
    return {
        "identity": np.eye(P, dtype=np.float32),
        "causal": np.stack([mask, strict], 1).astype(np.float32),
        "levels": levels.astype(np.float32),
        "cos": np.cos(angle).astype(np.float32),
        "sin": (np.sin(angle) * sign).astype(np.float32),
        "inv_count": np.ascontiguousarray(inv).astype(np.float32),
    }


def kernel(**inputs):
    import concourse.bacc as bacc
    from concourse.bass_utils import run_bass_kernel_spmd as run

    arrays = {n: np.ascontiguousarray(value) for n, value in [(n, inputs[n]) for n in INPUTS] + list(constants().items())}

    def write_down(known):
        nc = bacc.Bacc("TRN2", target_bir_lowering=False, num_devices=1)
        aps = {n: nc.dram_tensor(n, value.shape, mybir.dt.from_np(value.dtype), kind="ExternalInput").ap() for n, value in arrays.items()}
        out = nc.dram_tensor("out", (1, T, D), F32, kind="ExternalOutput").ap()
        return nc, program(nc, aps, out, known)
    _, steps = write_down({})
    nc, _ = write_down(steps)
    return run(nc, [arrays], core_ids=[0]).results[0]["out"]
```
